# Optimizing a Trainium2 kernel written in Bass

```python
import math
import jax, jax.numpy as jnp
from jax import lax
import numpy as np

D_MODEL = 1024
BATCH = 1
SEQ = 512
DEPTH = 1

N_META = 16
BLOCK = 128
MLA_HEADS = 8
QK_NOPE = 64
QK_ROPE = 32
V_HEAD = 64
Q_LORA = 256
KV_LORA = 128
ROPE_THETA = 10000.0
MLA_WIDTH = MLA_HEADS * V_HEAD
CONV_CH = 512
CONV_K = 31
CONV_WIDTH = CONV_CH
MIX_WIDTH = MLA_WIDTH + CONV_WIDTH
IN_COLS = 2 * CONV_CH + Q_LORA + KV_LORA + QK_ROPE
N_KEYS = 128
N_EXPERTS = N_KEYS * N_KEYS
PEER_HEADS = 8
PEER_DK = 128
PEER_DK_HALF = PEER_DK // 2
PEER_TOPK = 16
PEER_CHUNK = 128
NORM_EPS = 1e-6


def rmsnorm(x, g):
    xf = x.astype(jnp.float32)
    y = xf * lax.rsqrt(jnp.mean(xf * xf, axis=-1, keepdims=True) + NORM_EPS)
    return (y * g.astype(jnp.float32)).astype(x.dtype)

def layernorm(x, g, b):
    xf = x.astype(jnp.float32)
    mu = jnp.mean(xf, axis=-1, keepdims=True)
    var = jnp.mean(jnp.square(xf - mu), axis=-1, keepdims=True)
    y = (xf - mu) * lax.rsqrt(var + NORM_EPS)
    return (y * g.astype(jnp.float32) + b.astype(jnp.float32)).astype(x.dtype)

def rope(x, pos):
    half = x.shape[-1] // 2
    freqs = ROPE_THETA ** (-jnp.arange(half, dtype=jnp.float32) / half)
    ang = pos.astype(jnp.float32)[:, None] * freqs[None, :]
    cos = jnp.cos(ang)[None, :, None, :].astype(x.dtype)
    sin = jnp.sin(ang)[None, :, None, :].astype(x.dtype)
    x1, x2 = x[..., :half], x[..., half:]
    return jnp.concatenate([x1 * cos - x2 * sin, x2 * cos + x1 * sin], axis=-1)

def causal_block_attention(q, k, v):
    B, Tp, H, Dq = q.shape
    nb = Tp // BLOCK
    qb = q.reshape(B, nb, BLOCK, H, Dq).transpose(1, 0, 2, 3, 4)
    kpos = jnp.arange(Tp)
    scale = 1.0 / math.sqrt(Dq)

    def one(args):
        qblk, i = args
        s = jnp.einsum('bqhd,bkhd->bhqk', qblk, k).astype(jnp.float32) * scale
        qpos = i * BLOCK + jnp.arange(BLOCK)
        mask = kpos[None, :] <= qpos[:, None]
        s = jnp.where(mask[None, None], s, -jnp.inf)
        p = jax.nn.softmax(s, axis=-1).astype(v.dtype)
        return jnp.einsum('bhqk,bkhd->bqhd', p, v)

    o = lax.map(one, (qb, jnp.arange(nb)))
    return o.transpose(1, 0, 2, 3, 4).reshape(B, Tp, H, v.shape[-1])

def mla_group(c_q, c_kv, k_rope_in, pos, g_q, w_uq, g_kv, w_ukv):
    B, Tp, _ = c_q.shape
    q = (rmsnorm(c_q, g_q) @ w_uq).reshape(B, Tp, MLA_HEADS, QK_NOPE + QK_ROPE)
    q = jnp.concatenate([q[..., :QK_NOPE], rope(q[..., QK_NOPE:], pos)], axis=-1)
    kv = (rmsnorm(c_kv, g_kv) @ w_ukv).reshape(B, Tp, MLA_HEADS, QK_NOPE + V_HEAD)
    k_nope, v = kv[..., :QK_NOPE], kv[..., QK_NOPE:]
    k_r = rope(k_rope_in[:, :, None, :], pos)
    k = jnp.concatenate([k_nope, jnp.broadcast_to(k_r, (B, Tp, MLA_HEADS, QK_ROPE))], axis=-1)
    o = causal_block_attention(q, k, v)
    return o.reshape(B, Tp, MLA_WIDTH)

def conv_group(a, b, conv_w, conv_b, g_ln, b_ln):
    h = a * jax.nn.sigmoid(b)
    h = lax.conv_general_dilated(h, conv_w[:, None, :].astype(h.dtype), window_strides=(1,),
                                 padding=[(CONV_K - 1, 0)],
                                 dimension_numbers=('NWC', 'WIO', 'NWC'),
                                 feature_group_count=CONV_CH) + conv_b
    h = layernorm(h, g_ln, b_ln)
    return jax.nn.silu(h)

def peer_ffn(xn, wq, keys, u_tab, v_tab):
    B, Tp, D = xn.shape
    xc = xn.reshape(-1, PEER_CHUNK, D)
    K = PEER_TOPK

    def one(xb):
        C = xb.shape[0]
        q = (xb @ wq).reshape(C, PEER_HEADS, 2, PEER_DK_HALF)
        s = jnp.einsum('chpd,hpnd->chpn', q, keys).astype(jnp.float32)
        sv, si = lax.top_k(s, K)
        cand = sv[:, :, 0, :, None] + sv[:, :, 1, None, :]
        cidx = si[:, :, 0, :, None] * N_KEYS + si[:, :, 1, None, :]
        top_s, sel = lax.top_k(cand.reshape(C, PEER_HEADS, K * K), K)
        eidx = jnp.take_along_axis(cidx.reshape(C, PEER_HEADS, K * K), sel, axis=-1)
        g = jax.nn.softmax(top_s, axis=-1)
        u = u_tab[eidx]
        act = jax.nn.gelu(jnp.einsum('chkd,cd->chk', u, xb).astype(jnp.float32), approximate=False)
        w = (g * act).astype(xb.dtype)
        return jnp.einsum('chk,chkd->cd', w, v_tab[eidx])

    return lax.map(one, xc).reshape(B, Tp, D)

def first_inputs(seed: int = 0) -> dict:
    key = jax.random.key(seed)
    ks = jax.random.split(key, 24)
    f32 = jnp.float32
    L, D = DEPTH, D_MODEL

    def nrm(k, shape, scale):
        return jax.random.normal(k, shape, f32) * scale

    def gain(k, shape):
        return 1.0 + 0.02 * jax.random.normal(k, shape, f32)

    return {
        "x": jax.random.normal(ks[0], (BATCH, SEQ, D), f32),
        "meta": nrm(ks[1], (N_META, D), 1.0),
        "g_mix_norm": gain(ks[2], (L, D)),
        "w_in": nrm(ks[3], (L, D, IN_COLS), D ** -0.5),
        "g_q": gain(ks[4], (L, Q_LORA)),
        "w_uq": nrm(ks[5], (L, Q_LORA, MLA_HEADS * (QK_NOPE + QK_ROPE)), Q_LORA ** -0.5),
        "g_kv": gain(ks[6], (L, KV_LORA)),
        "w_ukv": nrm(ks[7], (L, KV_LORA, MLA_HEADS * (QK_NOPE + V_HEAD)), KV_LORA ** -0.5),
        "conv_w": nrm(ks[8], (L, CONV_K, CONV_CH), CONV_K ** -0.5),
        "conv_b": nrm(ks[9], (L, CONV_CH), 0.02),
        "g_conv_ln": gain(ks[10], (L, CONV_CH)),
        "b_conv_ln": nrm(ks[11], (L, CONV_CH), 0.02),
        "g_out_attn": gain(ks[12], (L, MLA_WIDTH)),
        "g_out_conv": gain(ks[13], (L, CONV_WIDTH)),
        "w_out": nrm(ks[14], (L, MIX_WIDTH, D), MIX_WIDTH ** -0.5),
        "g_ffn_norm": gain(ks[15], (L, D)),
        "peer_wq": nrm(ks[16], (L, D, PEER_HEADS * PEER_DK), D ** -0.5),
        "peer_keys": nrm(ks[17], (L, PEER_HEADS, 2, N_KEYS, PEER_DK_HALF), PEER_DK_HALF ** -0.5),
        "peer_u": nrm(ks[18], (L, N_EXPERTS, D), D ** -0.5),
        "peer_v": nrm(ks[19], (L, N_EXPERTS, D), (PEER_HEADS * PEER_TOPK) ** -0.5),
        "g_final": gain(ks[20], (D,)),
    }

def first_block(x, meta, g_mix_norm, w_in, g_q, w_uq, g_kv, w_ukv, conv_w, conv_b, g_conv_ln, b_conv_ln,
              g_out_attn, g_out_conv, w_out, g_ffn_norm, peer_wq, peer_keys, peer_u, peer_v, g_final):
    B, S, D = x.shape
    T = N_META + S
    Tp = ((T + BLOCK - 1) // BLOCK) * BLOCK
    h = jnp.concatenate([jnp.broadcast_to(meta.astype(x.dtype)[None], (B, N_META, D)), x,
                         jnp.zeros((B, Tp - T, D), x.dtype)], axis=1)
    pos = jnp.arange(Tp, dtype=jnp.int32)

    c0 = 2 * CONV_CH
    c1 = c0 + Q_LORA
    c2 = c1 + KV_LORA
    for l in range(DEPTH):
        hn = rmsnorm(h, g_mix_norm[l])
        z = hn @ w_in[l]
        conv_out = conv_group(z[..., :CONV_CH], z[..., CONV_CH:c0], conv_w[l], conv_b[l],
                              g_conv_ln[l], b_conv_ln[l])
        attn_out = mla_group(z[..., c0:c1], z[..., c1:c2], z[..., c2:], pos,
                             g_q[l], w_uq[l], g_kv[l], w_ukv[l])
        mixed = jnp.concatenate([rmsnorm(attn_out, g_out_attn[l]),
                                 rmsnorm(conv_out, g_out_conv[l])], axis=-1)
        h = h + mixed @ w_out[l]
        h = h + peer_ffn(rmsnorm(h, g_ffn_norm[l]), peer_wq[l], peer_keys[l], peer_u[l], peer_v[l])

    h = rmsnorm(h, g_final)
    return h[:, N_META:N_META + S, :]


DEPTH_2 = 2

N_A_LAYERS = DEPTH_2 // 2
N_B_LAYERS = DEPTH_2 - N_A_LAYERS
CONV_WIDTH_2 = 3
FFN_HIDDEN = -(-8 * D_MODEL // (3 * 256)) * 256
N_HEADS = 16
N_KV_GROUPS = 4
HEADS_PER_GROUP = N_HEADS // N_KV_GROUPS
HEAD_DIM = 64
L_CMP = 32
D_CMP = 16
L_SLC = 64
N_SEL = 16
WINDOW = 512
CMP_HIDDEN = 256
Q_BLOCK = 64
N_KV_SETS = 6
RMS_EPS = 1e-5
NEG_INF = -1e30
FORCE_BONUS = 1e4


def rms_norm(x, g):
    xf = x.astype(jnp.float32)
    y = xf * lax.rsqrt(jnp.mean(xf * xf, axis=-1, keepdims=True) + RMS_EPS)
    return (y * g.astype(jnp.float32)).astype(x.dtype)

def short_conv_mixer(h, w_in, conv_w, w_out):
    b_gate, c_gate, v = jnp.split(h @ w_in, 3, axis=-1)
    u = lax.conv_general_dilated(
        c_gate * v, conv_w[:, None, :], window_strides=(1,),
        padding=((CONV_WIDTH_2 - 1, 0),), dimension_numbers=("NWC", "WIO", "NWC"),
        feature_group_count=D_MODEL)
    return (b_gate * u) @ w_out

def swiglu(h, w_gu, w_down):
    g, u = jnp.split(h @ w_gu, 2, axis=-1)
    return (jax.nn.silu(g) * u) @ w_down

def compress(kv_raw, pe, w1, w2):
    bsz, seq = kv_raw.shape[0], kv_raw.shape[1]
    n_cmp = (seq - L_CMP) // D_CMP + 1
    idx = jnp.arange(n_cmp)[:, None] * D_CMP + jnp.arange(L_CMP)[None, :]
    blocks = kv_raw[:, idx] + pe[None, None, :, None, :]
    blocks = blocks.transpose(0, 1, 3, 2, 4).reshape(bsz, n_cmp, N_KV_GROUPS, L_CMP * HEAD_DIM)
    return jax.nn.silu(blocks @ w1) @ w2

def shared_kv(h, kv_norm, w_kv, pe_k, w1_k, w2_k, pe_v, w1_v, w2_v):
    bsz, seq, _ = h.shape
    kv = (rms_norm(h, kv_norm) @ w_kv).reshape(bsz, seq, N_KV_SETS, N_KV_GROUPS, HEAD_DIM)
    k_cmp = compress(kv[:, :, 0], pe_k, w1_k, w2_k)
    v_cmp = compress(kv[:, :, 1], pe_v, w1_v, w2_v)
    return (k_cmp, v_cmp, kv[:, :, 2], kv[:, :, 3], kv[:, :, 4], kv[:, :, 5])

def nsa_mixer(h, w_qg, w_o, k_cmp, v_cmp, k_slc, v_slc, k_win, v_win):
    bsz, seq, _ = h.shape
    G, HPG, dh = N_KV_GROUPS, HEADS_PER_GROUP, HEAD_DIM
    qg = h @ w_qg
    q = (qg[..., :N_HEADS * dh] * (dh ** -0.5)).reshape(bsz, seq, G, HPG, dh)
    gates = jax.nn.sigmoid(qg[..., N_HEADS * dh:].astype(jnp.float32)).reshape(bsz, seq, G, HPG, 3)

    slopes = jnp.exp2(-8.0 * jnp.arange(1, N_HEADS + 1, dtype=jnp.float32) / N_HEADS).reshape(G, HPG)

    n_cmp = k_cmp.shape[1]
    cmp_start = jnp.arange(n_cmp) * D_CMP
    cmp_end = cmp_start + L_CMP - 1
    cmp_center = cmp_end.astype(jnp.float32) - (L_CMP - 1) / 2.0
    n_slc = seq // L_SLC
    n_sel = min(N_SEL, n_slc)
    slc_start = jnp.arange(n_slc) * L_SLC
    overlap = ((cmp_start[:, None] < slc_start[None, :] + L_SLC)
               & (cmp_start[:, None] + L_CMP > slc_start[None, :])).astype(jnp.float32)

    k_blk = k_slc.reshape(bsz, n_slc, L_SLC, G, dh).transpose(0, 3, 1, 2, 4)
    v_blk = v_slc.reshape(bsz, n_slc, L_SLC, G, dh).transpose(0, 3, 1, 2, 4)
    pad = ((0, 0), (WINDOW, 0), (0, 0), (0, 0))
    k_win_pad = jnp.pad(k_win, pad)
    v_win_pad = jnp.pad(v_win, pad)
    b_ix = jnp.arange(bsz)[:, None, None, None]
    g_ix = jnp.arange(G)[None, :, None, None]
    j_blk = jnp.arange(n_slc)

    def one_block(qb):
        q0 = qb * Q_BLOCK
        t = q0 + jnp.arange(Q_BLOCK)
        tf = t.astype(jnp.float32)
        qblk = lax.dynamic_slice_in_dim(q, q0, Q_BLOCK, axis=1)
        gblk = lax.dynamic_slice_in_dim(gates, q0, Q_BLOCK, axis=1)

        s = jnp.einsum("bqghd,bngd->bghqn", qblk, k_cmp).astype(jnp.float32)
        vis = cmp_end[None, :] <= t[:, None]
        s = s - slopes[:, :, None, None] * (tf[:, None] - cmp_center[None, :])
        p_cmp = jax.nn.softmax(jnp.where(vis, s, NEG_INF), axis=-1) * vis
        o_cmp = jnp.einsum("bghqn,bngd->bqghd", p_cmp.astype(v_cmp.dtype), v_cmp)

        imp = jnp.einsum("bghqn,nj->bgqj", p_cmp, overlap)
        cur = t // L_SLC
        valid = j_blk[None, :] <= cur[:, None]
        forced = ((j_blk[None, :] == 0) | (j_blk[None, :] == cur[:, None])
                  | (j_blk[None, :] == cur[:, None] - 1))
        imp = jnp.where(valid, imp + FORCE_BONUS * forced, NEG_INF)
        _, sel = lax.top_k(imp, n_sel)
        k_sel = k_blk[b_ix, g_ix, sel]
        v_sel = v_blk[b_ix, g_ix, sel]
        s = jnp.einsum("bqghd,bgqnld->bghqnl", qblk, k_sel).astype(jnp.float32)
        dist = t[None, None, :, None, None] - (sel[..., None] * L_SLC + jnp.arange(L_SLC))
        dist = dist[:, :, None]
        s = s - slopes[:, :, None, None, None] * dist.astype(jnp.float32)
        s = jnp.where(dist >= 0, s, NEG_INF)
        p = jax.nn.softmax(s.reshape(s.shape[:4] + (n_sel * L_SLC,)), axis=-1).reshape(s.shape)
        o_slc = jnp.einsum("bghqnl,bgqnld->bqghd", p.astype(v_sel.dtype), v_sel)

        kw = lax.dynamic_slice_in_dim(k_win_pad, q0, WINDOW + Q_BLOCK, axis=1)
        vw = lax.dynamic_slice_in_dim(v_win_pad, q0, WINDOW + Q_BLOCK, axis=1)
        spos = q0 - WINDOW + jnp.arange(WINDOW + Q_BLOCK)
        d = t[:, None] - spos[None, :]
        m = (d >= 0) & (d < WINDOW) & (spos >= 0)[None, :]
        s = jnp.einsum("bqghd,bkgd->bghqk", qblk, kw).astype(jnp.float32)
        s = s - slopes[:, :, None, None] * d.astype(jnp.float32)
        p = jax.nn.softmax(jnp.where(m, s, NEG_INF), axis=-1)
        o_win = jnp.einsum("bghqk,bkgd->bqghd", p.astype(vw.dtype), vw)

        o = (gblk[..., 0:1] * o_cmp + gblk[..., 1:2] * o_slc + gblk[..., 2:3] * o_win)
        return o.reshape(bsz, Q_BLOCK, N_HEADS * dh).astype(h.dtype)

    out = lax.map(one_block, jnp.arange(seq // Q_BLOCK))
    out = out.transpose(1, 0, 2, 3).reshape(bsz, seq, N_HEADS * dh)
    return out @ w_o

def second_inputs(seed: int = 0) -> dict:
    key = jax.random.key(seed)
    ks = jax.random.split(key, 24)

    def w(k, shape, fan_in):
        return jax.random.normal(k, shape, jnp.float32) * (fan_in ** -0.5)

    def gain(k, shape):
        return 1.0 + 0.02 * jax.random.normal(k, shape, jnp.float32)

    D, F = D_MODEL, FFN_HIDDEN
    kv_w = N_KV_GROUPS * HEAD_DIM
    qg_w = N_HEADS * HEAD_DIM + 3 * N_HEADS
    return {
        "x": jax.random.normal(ks[0], (BATCH, SEQ, D), jnp.float32),
        "a_norm": gain(ks[1], (N_A_LAYERS, D)),
        "a_w_in": w(ks[2], (N_A_LAYERS, D, 3 * D), D),
        "a_conv": w(ks[3], (N_A_LAYERS, CONV_WIDTH_2, D), CONV_WIDTH_2),
        "a_w_out": w(ks[4], (N_A_LAYERS, D, D), D),
        "kv_norm": gain(ks[5], (D,)),
        "w_kv": w(ks[6], (D, N_KV_SETS * kv_w), D),
        "cmp_pe_k": 0.02 * jax.random.normal(ks[7], (L_CMP, HEAD_DIM), jnp.float32),
        "cmp_w1_k": w(ks[8], (L_CMP * HEAD_DIM, CMP_HIDDEN), L_CMP * HEAD_DIM),
        "cmp_w2_k": w(ks[9], (CMP_HIDDEN, HEAD_DIM), CMP_HIDDEN),
        "cmp_pe_v": 0.02 * jax.random.normal(ks[10], (L_CMP, HEAD_DIM), jnp.float32),
        "cmp_w1_v": w(ks[11], (L_CMP * HEAD_DIM, CMP_HIDDEN), L_CMP * HEAD_DIM),
        "cmp_w2_v": w(ks[12], (CMP_HIDDEN, HEAD_DIM), CMP_HIDDEN),
        "b_norm": gain(ks[13], (N_B_LAYERS, D)),
        "b_w_qg": w(ks[14], (N_B_LAYERS, D, qg_w), D),
        "b_w_o": w(ks[15], (N_B_LAYERS, N_HEADS * HEAD_DIM, D), N_HEADS * HEAD_DIM),
        "f_norm": gain(ks[16], (DEPTH_2, D)),
        "f_w_gu": w(ks[17], (DEPTH_2, D, 2 * F), D),
        "f_w_down": w(ks[18], (DEPTH_2, F, D), F),
        "final_norm": gain(ks[19], (D,)),
    }

def second_block(x, a_norm, a_w_in, a_conv, a_w_out, kv_norm, w_kv, cmp_pe_k, cmp_w1_k, cmp_w2_k,
              cmp_pe_v, cmp_w1_v, cmp_w2_v, b_norm, b_w_qg, b_w_o, f_norm, f_w_gu, f_w_down,
              final_norm):
    h = x
    shared = None
    for layer in range(DEPTH_2):
        if layer < N_A_LAYERS:
            i = layer
            h = h + short_conv_mixer(rms_norm(h, a_norm[i]), a_w_in[i], a_conv[i], a_w_out[i])
        else:
            i = layer - N_A_LAYERS
            if shared is None:
                shared = shared_kv(h, kv_norm, w_kv, cmp_pe_k, cmp_w1_k, cmp_w2_k,
                                   cmp_pe_v, cmp_w1_v, cmp_w2_v)
            k_cmp, v_cmp, k_slc, v_slc, k_win, v_win = shared
            h = h + nsa_mixer(rms_norm(h, b_norm[i]), b_w_qg[i], b_w_o[i],
                              k_cmp, v_cmp, k_slc, v_slc, k_win, v_win)
        h = h + swiglu(rms_norm(h, f_norm[layer]), f_w_gu[layer], f_w_down[layer])
    return rms_norm(h, final_norm)


def setup_inputs(seed=0):
    out = dict(first_inputs(seed))
    for name, value in second_inputs(seed + 1).items():
        if name != "x":
            out[name + "_2"] = value
    return out


def reference(
    x, meta, g_mix_norm, w_in, g_q, w_uq, g_kv, w_ukv, conv_w, conv_b, g_conv_ln, b_conv_ln,
    g_out_attn, g_out_conv, w_out, g_ffn_norm, peer_wq, peer_keys, peer_u, peer_v, g_final,
    a_norm_2, a_w_in_2, a_conv_2, a_w_out_2, kv_norm_2, w_kv_2, cmp_pe_k_2, cmp_w1_k_2,
    cmp_w2_k_2, cmp_pe_v_2, cmp_w1_v_2, cmp_w2_v_2, b_norm_2, b_w_qg_2, b_w_o_2, f_norm_2,
    f_w_gu_2, f_w_down_2, final_norm_2,
):
    x = first_block(
        x, meta, g_mix_norm, w_in, g_q, w_uq, g_kv, w_ukv, conv_w, conv_b, g_conv_ln, b_conv_ln,
        g_out_attn, g_out_conv, w_out, g_ffn_norm, peer_wq, peer_keys, peer_u, peer_v, g_final,
    )
    return second_block(
        x, a_norm_2, a_w_in_2, a_conv_2, a_w_out_2, kv_norm_2, w_kv_2, cmp_pe_k_2, cmp_w1_k_2,
        cmp_w2_k_2, cmp_pe_v_2, cmp_w1_v_2, cmp_w2_v_2, b_norm_2, b_w_qg_2, b_w_o_2, f_norm_2,
        f_w_gu_2, f_w_down_2, final_norm_2,
    )


_drawn_inputs = setup_inputs


def setup_inputs(seed=0):
    import zlib

    import numpy as np

    out = dict(_drawn_inputs(seed))
    spreads = {}
    factors = {'g_q': 3.397,
     'b_conv_ln': 3.054,
     'g_out_attn': 3.25,
     'g_out_conv': 3.24,
     'g_ffn_norm': 7.147,
     'kv_norm_2': 8.0,
     'cmp_pe_k_2': 22.827,
     'cmp_pe_v_2': 60.604,
     'b_norm_2': 8.0,
     'f_norm_2': 3.506}
    for name, (base, spread) in spreads.items():
        noise = np.random.default_rng([zlib.crc32(name.encode()), seed]).standard_normal(out[name].shape)
        drawn = base * np.exp(spread * noise) if base else spread * noise
        out[name] = __import__('jax').numpy.asarray(drawn.astype(out[name].dtype))
    for name, factor in factors.items():
        out[name] = (out[name] * factor).astype(out[name].dtype)
    return out
```

```python
from contextlib import ExitStack

import numpy as np

import concourse.bass as bass
from concourse import mybir

F32 = mybir.dt.float32
F16 = mybir.dt.float16
U32 = mybir.dt.uint32
ALU = mybir.AluOpType
ACT = mybir.ActivationFunctionType
AX = mybir.AxisListType.X

P = 128
D = 1024
DT = D // P
SEQ = 512
NMETA = 16
T1 = SEQ + NMETA
HT = T1 // 2
ST = SEQ // P

HEADS = 8
NOPE = 64
ROPE = 32
VH = 64
DQ = NOPE + ROPE
QL = 256
KVL = 128
CC = 512
CT = CC // P
CK = 31
NK = 128
PH = 8
TOPK = 16
EPS1 = 1e-6

F = 2816
FT = F // P
NH = 16
NG = 4
HPG = NH // NG
HD = 64
LC = 32
DC = 16
NC = (SEQ - LC) // DC + 1
CH = 256
EPS2 = 1e-5
NEG = -1e30
GSCALE = 16384.0

GAINS = [("g_mix_norm", 8), ("g_q", 2), ("g_kv", 1), ("conv_b", 4), ("g_conv_ln", 4), ("b_conv_ln", 4),
         ("g_out_attn", 4), ("g_out_conv", 4), ("g_ffn_norm", 8), ("g_final", 8), ("conv_w", CK * CT),
         ("a_norm_2", 8), ("kv_norm_2", 8), ("b_norm_2", 8), ("f_norm_2", 16), ("final_norm_2", 8),
         ("a_conv_2", 24)]
GCOL = {}
_at = 0
for _name, _n in GAINS:
    GCOL[_name] = _at
    _at += _n
NGAIN = _at


class Count:

    def __init__(self, eng, sem):
        self.eng, self.sem, self.n = eng, sem, 0

    def step(self, ins):
        self.n += 1
        return ins.then_inc(self.sem, 1)

    def wait(self):
        self.eng.wait_ge(self.sem, self.n)

    def link(self, ins):
        self.step(ins)
        self.wait()


class Kit:

    def __init__(self, nc, t, ctx):
        self.nc, self.t, self.ctx = nc, t, ctx
        self.uid = 0
        sb = lambda n, s, d=F32: ctx.enter_context(nc.sbuf_tensor(n, s, d))
        self.hT = sb("hT", [P, DT, T1])
        self.gains = sb("gains", [P, NGAIN])
        self.ones = sb("ones", [P, P])
        self.ident = sb("ident", [P, P])
        self.tri = sb("tri", [P, P])
        self.loaded = ctx.enter_context(nc.semaphore("consts_loaded"))
        self.stored = ctx.enter_context(nc.semaphore("output_stored"))
        self.made = ctx.enter_context(nc.semaphore("ones_made"))

    def gain(self, name, j):
        c = GCOL[name] + j
        return self.gains[:, c:c + 1]

    def real(self, j):
        return self.hT[:, j, NMETA:T1]


class Stage:

    def __init__(self, kit, name):
        self.kit, self.nc, self.name = kit, kit.nc, name
        self.ctx = ExitStack()
        self.sems = []

    def __enter__(self):
        self.ctx.__enter__()
        return self

    def __exit__(self, kind, *a):
        if kind is None:
            self.nc.clear_and_free_semaphores(self.sems)
            self.nc.all_engine_barrier()
        return self.ctx.__exit__(kind, *a)

    def sb(self, name, shape, dt=F32):
        return self.ctx.enter_context(self.nc.sbuf_tensor(f"{self.name}_{name}", shape, dt))

    def banks(self, n=8):
        return self.ctx.enter_context(self.nc.psum_tensor(f"{self.name}_psum", [P, n, 512], F32))

    def sem(self, name):
        self.sems.append(self.nc.alloc_semaphore(f"{self.name}_{name}"))
        return self.sems[-1]


class WeightRing:

    def __init__(self, st, name, slots, cols, tiles):
        self.buf = st.sb(name, [P, slots, cols])
        self.n, self.tiles = slots, tiles
        self.into = [st.sem(f"{name}_in{i}") for i in range(slots)]

    def load_all(self, sp, done):
        for n, w in enumerate(self.tiles):
            if n >= self.n:
                sp.wait_ge(done, n - self.n + 1)
            sp.dma_start(self.buf[:, n % self.n, 0:w.shape[1]], w).then_inc(self.into[n % self.n], 16)

    def take(self, pe, n):
        pe.wait_ge(self.into[n % self.n], 16 * (n // self.n + 1))
        return self.buf[:, n % self.n, :]


class Linear:

    def __init__(self, st, ring, slots, tiles, name="lin"):
        self.ring, self.slots, self.tiles = ring, slots, tiles
        self.index = {t[0]: n for n, t in enumerate(tiles)}
        self.done = st.sem(f"{name}_done")
        self.free = [st.sem(f"{name}_free{i}") for i in range(len(slots))]

    def run(self, pe, only=None):
        for n, (key, m, kt, rhs, need) in enumerate(self.tiles):
            if only is not None and not only(n):
                continue
            if need is not None:
                pe.wait_ge(*need)
            w = self.ring.take(pe, n)
            s = n % len(self.slots)
            if n >= len(self.slots):
                pe.wait_ge(self.free[s], n // len(self.slots))
            for k in range(kt):
                for half, x in enumerate(rhs(k)):
                    mm = pe.matmul(self.slots[s][0:m, half, 0:x.shape[-1]], w[:, k * m:(k + 1) * m], x,
                                   start=(k == 0), stop=(k == kt - 1))
            mm.then_inc(self.done, 1)

    def arrived(self, eng, key):
        n = self.index[key]
        eng.wait_ge(self.done, n + 1)
        s = n % len(self.slots)
        return self.slots[s], self.free[s]


class Norm:

    def __init__(self, st, name, src, dst, n, width, eps, gain, ps, parts, need=None, dim=None):
        self.kit = st.kit
        self.src, self.dst, self.n, self.eps, self.gain = src, dst, n, eps, gain
        self.ps, self.parts, self.need, self.dim = ps, parts, need, dim or n * P
        self.width = width
        self.sq = st.sb(f"{name}_sq", [P, 2, width])
        self.rs = st.sb(f"{name}_rs", [P, width])
        self.squared = st.sem(f"{name}_squared")
        self.summed = st.sem(f"{name}_summed")
        self.var = st.sem(f"{name}_var")
        self.root = st.sem(f"{name}_root")
        self.out = st.sem(f"{name}_out")

    def cols(self, x):
        w = self.width // self.parts
        return [x[:, i * w:(i + 1) * w] for i in range(self.parts)]

    def split(self, x):
        return x.rearrange("p (a b) -> p a b", a=self.parts)

    def on_act(self, act):
        for j in range(self.n):
            if self.need is not None:
                act.wait_ge(self.need[0], self.need[1](j) if callable(self.need[1]) else self.need[1])
            if j >= 2:
                act.wait_ge(self.summed, j - 1)
            act.activation(self.sq[:, j % 2, :], self.src(j), ACT.Square).then_inc(self.squared, 1)
        act.wait_ge(self.var, 1)
        act.activation(self.rs[:, :], self.rs[:, :], ACT.Sqrt).then_inc(self.root, 1)

    def on_pe(self, pe):
        for j in range(self.n):
            pe.wait_ge(self.squared, j + 1)
            for i, x in enumerate(self.cols(self.sq[:, j % 2, :])):
                mm = pe.matmul(self.ps[:, i, 0:x.shape[-1]], self.kit.ones[:, :], x,
                               start=(j == 0), stop=(j == self.n - 1))
            mm.then_inc(self.summed, 1)

    def on_dve(self, dve, own):
        w = self.width // self.parts
        dve.wait_ge(self.summed, self.n)
        dve.tensor_scalar(self.split(self.rs[:, :]), self.ps[:, 0:self.parts, 0:w], 1.0 / self.dim, self.eps,
                          ALU.mult, ALU.add).then_inc(self.var, 1)
        dve.wait_ge(self.root, 1)
        own.link(dve.reciprocal(self.rs[:, :], self.rs[:, :]))
        for j in range(self.n):
            dve.scalar_tensor_tensor(out=self.dst(j), in0=self.src(j), scalar=self.gain(j), in1=self.rs[:, :],
                                     op0=ALU.mult, op1=ALU.mult).then_inc(self.out, 1)


def one_bank_slots(ps, first, n):
    return [ps[:, first + i:first + i + 1, :] for i in range(n)]


def two_bank_slots(ps, first, n):
    return [ps[:, first + 2 * i:first + 2 * i + 2, :] for i in range(n)]


def pieces(w, tiles, cols):
    return [w[n * P:(n + 1) * P, 0:cols] for n in range(tiles)]


def front(kit, out):
    nc, t = kit.nc, kit.t
    with Stage(kit, "front") as st:
        ps = st.banks()
        hn = st.sb("hn", [P, DT, T1])
        conv_in = st.sb("conv_in", [P, CT, CK - 1 + T1])
        sig = st.sb("sig", [P, 2, T1])
        acc = out["mixT"][:, CT:2 * CT, :]
        cq = st.sb("cq", [P, 2, SEQ])
        ckv = st.sb("ckv", [P, T1])
        cos = st.sb("cos", [P, T1])
        sin = st.sb("sin", [P, T1])
        wkv = st.sb("wkv", [P, HEADS * (NOPE + VH)])
        rot = st.sb("rot", [P, 2, T1])
        kr = st.sb("kr", [ROPE, T1])
        mu = st.sb("mu", [P, SEQ])
        side = st.sem("side_loaded")

        w528 = pieces(t["w_ab"], 2 * CT, D) + pieces(t["w_ckv"], 1, D)
        w_small = [t["w_krope"][:, :]]
        ring = WeightRing(st, "w", 5, D, w528 + w_small + pieces(t["w_cq"], 2, D) + pieces(t["w_uq"], 8, 2 * P))

        def halves(buf):
            return lambda k: [buf[:, k, 0:HT], buf[:, k, HT:T1]]

        mix = Norm(st, "mix", lambda j: kit.hT[:, j, :], lambda j: hn[:, j, :], DT, T1, EPS1,
                   lambda j: kit.gain("g_mix_norm", j), ps[:, 6:8, :], 2, need=(kit.loaded, 16))
        qn = Norm(st, "qn", lambda j: cq[:, j, :], lambda j: cq[:, j, :], 2, SEQ, EPS1,
                  lambda j: kit.gain("g_q", j), ps[:, 6:7, :], 1, need=(st.sem("cq_copied"), lambda j: j + 1))
        kn = Norm(st, "kn", lambda j: ckv[:, :], lambda j: ckv[:, :], 1, T1, EPS1,
                  lambda j: kit.gain("g_kv", 0), ps[:, 6:8, :], 2, need=(st.sem("ckv_copied"), 1))
        cq_copied, ckv_copied = qn.need[0], kn.need[0]

        tiles = []
        for c in range(CT):
            tiles.append((("b", c), P, DT, halves(hn), (mix.out, DT)))
            tiles.append((("a", c), P, DT, halves(hn), None))
        tiles.append((("ckv", 0), P, DT, halves(hn), None))
        tiles.append((("krope", 0), 2 * ROPE, DT, halves(hn), None))
        for c in range(2):
            tiles.append((("cq", c), P, DT, lambda k: [hn[:, k, NMETA:T1]], None))
        for c in range(8):
            tiles.append((("q", c), P, 2, lambda k: [cq[:, k, :]], (qn.out, 2)))
        lin = Linear(st, ring, two_bank_slots(ps, 0, 3), tiles)
        n_before_q = lin.index[("q", 0)]

        gated = st.sem("gated")
        sig_done = st.sem("sig_done")
        padded = st.sem("padded")
        conv_done = st.sem("conv_done")
        kv_done = st.sem("kv_done")
        kv_free = st.sem("kv_free")
        ln_sum = st.sem("ln_sum")
        centred = st.sem("centred")
        silu_done = st.sem("silu_done")
        kr_done = st.sem("kr_done")
        kr_spread = st.sem("kr_spread")
        act_steps = st.sem("act_steps")

        ln = Norm(st, "ln", lambda j: acc[:, j, :], lambda j: acc[:, j, :], CT, SEQ, EPS1,
                  lambda j: 1.0, ps[:, 5:6, :], 1, need=(centred, lambda j: j + 1))
        cn = Norm(st, "cn", lambda j: acc[:, j, :], lambda j: out["mixT"][:, CT + j, :], CT, SEQ, EPS1,
                  lambda j: kit.gain("g_out_conv", j), ps[:, 5:6, :], 1, need=(silu_done, lambda j: j + 1))

        with nc.Block() as block:

            @block.sync
            def _(sp):
                sp.dma_start(kit.hT[:, :, :], t["hT0"].rearrange("p (j n) -> p j n", j=DT)).then_inc(kit.loaded, 16)
                sp.dma_start(kit.gains[:, :], t["gains"]).then_inc(side, 16)
                sp.dma_start(kit.ident[:, :], t["c_ident"]).then_inc(side, 16)
                sp.dma_start(kit.tri[:, :], t["c_tri"]).then_inc(side, 16)
                sp.dma_start(cos[:, :], t["c_cos"]).then_inc(side, 16)
                sp.dma_start(sin[:, :], t["c_sin"]).then_inc(side, 16)
                sp.dma_start(wkv[:, :], t["w_ukv"]).then_inc(side, 16)
                ring.load_all(sp, lin.done)

            @block.tensor
            def _(pe):
                pe.wait_ge(kit.made, 1)
                mix.on_pe(pe)
                lin.run(pe, lambda n: n < n_before_q)
                pe.wait_ge(mix.var, 1)
                kn.on_pe(pe)
                pe.wait_ge(kn.var, 1)
                qn.on_pe(pe)
                lin.run(pe, lambda n: n >= n_before_q)
                pe.wait_ge(kn.out, 1)
                pe.wait_ge(side, 96)
                for s in range(3):
                    pe.wait_ge(lin.free[s], len([n for n in range(len(tiles)) if n % 3 == s]))
                for c in range(HEADS // 2):
                    if c >= 2:
                        pe.wait_ge(kv_free, c - 1)
                    for half in range(2):
                        mm = pe.matmul(ps[:, 2 * (c % 2) + half, 0:HT], wkv[:, c * P:(c + 1) * P],
                                       ckv[:, half * HT:(half + 1) * HT], start=True, stop=True)
                    mm.then_inc(kv_done, 1)
                pe.wait_ge(kv_free, HEADS // 2)
                for j in range(ST + 1):
                    if j >= 2:
                        pe.wait_ge(kv_free, HEADS // 2 + j - 1)
                    lo, m = (NMETA + j * P, P) if j < ST else (0, NMETA)
                    pe.matmul(ps[0:m, j % 2, 0:CC], ckv[:, lo:lo + m], wkv[:, HEADS * NOPE:],
                              start=True, stop=True).then_inc(kv_done, 1)
                for c in range(CT):
                    pe.wait_ge(conv_done, c + 1)
                    mm = pe.matmul(ps[:, 4, :], kit.ones[:, :], acc[:, c, :], start=(c == 0), stop=(c == CT - 1))
                mm.then_inc(ln_sum, 1)
                ln.on_pe(pe)
                pe.wait_ge(ln.var, 1)
                cn.on_pe(pe)

            @block.scalar
            def _(act):
                act.wait_ge(side, 96)
                mix.on_act(act)
                for c in range(CT):
                    slot, free = lin.arrived(act, ("b", c))
                    if c >= 2:
                        act.wait_ge(gated, c - 1)
                    act.activation(sig[:, c % 2, :].rearrange("p (a b) -> p a b", a=2), slot[:, :, 0:HT],
                                   ACT.Sigmoid).then_inc(sig_done, 1)
                    act.wait_ge(sig_done, c + 1)
                    act.nop().then_inc(free, 1)
                slot, free = lin.arrived(act, ("ckv", 0))
                act.activation(ckv[:, :].rearrange("p (a b) -> p a b", a=2), slot[:, :, 0:HT],
                               ACT.Copy).then_inc(ckv_copied, 1)
                act.wait_ge(ckv_copied, 1)
                act.nop().then_inc(free, 1)
                for c in range(2):
                    slot, free = lin.arrived(act, ("cq", c))
                    act.activation(cq[:, c, :], slot[:, 0, :], ACT.Copy).then_inc(cq_copied, 1)
                    act.wait_ge(cq_copied, c + 1)
                    act.nop().then_inc(free, 1)
                kn.on_act(act)
                qn.on_act(act)
                for c in range(4):
                    slot, free = lin.arrived(act, ("q", c))
                    for e in range(2):
                        act.activation(out["qT"][0:NOPE, 2 * c + e, :], slot[e * NOPE:(e + 1) * NOPE, 0, :],
                                       ACT.Copy).then_inc(act_steps, 1)
                    act.wait_ge(act_steps, 2 * (c + 1))
                    act.nop().then_inc(free, 1)
                for c in range(HEADS // 2):
                    act.wait_ge(kv_done, c + 1)
                    for e in range(2):
                        act.activation(out["kT"][0:NOPE, 2 * c + e, :].rearrange("p (a b) -> p a b", a=2),
                                       ps[e * NOPE:(e + 1) * NOPE, 2 * (c % 2):2 * (c % 2) + 2, 0:HT],
                                       ACT.Copy).then_inc(act_steps, 1)
                    act.wait_ge(act_steps, 8 + 2 * (c + 1))
                    act.nop().then_inc(kv_free, 1)
                for j in range(ST + 1):
                    act.wait_ge(kv_done, HEADS // 2 + j + 1)
                    m = P if j < ST else NMETA
                    act.activation(out["v"][0:m, j, :], ps[0:m, j % 2, :], ACT.Copy).then_inc(kv_free, 1)
                act.wait_ge(kr_done, 1)
                for h in range(HEADS):
                    act.activation(out["kT"][NOPE:DQ, h, :], kr[:, :], ACT.Copy).then_inc(kr_spread, 1)
                ln.on_act(act)
                for c in range(CT):
                    act.wait_ge(ln.out, c + 1)
                    act.activation(acc[:, c, :], acc[:, c, :], ACT.Silu, bias=kit.gain("b_conv_ln", c),
                                   scale=kit.gain("g_conv_ln", c)).then_inc(silu_done, 1)
                cn.on_act(act)

            @block.gpsimd
            def _(pool):
                pool.memset(kit.ones[:, :], 1.0).then_inc(kit.made, 1)
                pool.memset(conv_in[:, :, 0:CK - 1], 0.0).then_inc(padded, 1)

            own_sem = st.sem("vector_steps")

            @block.vector
            def _(dve):
                own = Count(dve, own_sem)
                dve.wait_ge(side, 96)
                mix.on_dve(dve, own)
                for c in range(CT):
                    slot, free = lin.arrived(dve, ("a", c))
                    dve.wait_ge(sig_done, c + 1)
                    dve.tensor_tensor(conv_in[:, c, CK - 1:].rearrange("p (a b) -> p a b", a=2), slot[:, :, 0:HT],
                                      sig[:, c % 2, :].rearrange("p (a b) -> p a b", a=2), ALU.mult).then_inc(gated, 1)
                    dve.wait_ge(gated, c + 1)
                    dve.nop().then_inc(free, 1)
                slot, free = lin.arrived(dve, ("krope", 0))
                for e, tab in enumerate((cos, sin)):
                    own.step(dve.tensor_tensor(
                        rot[0:ROPE, e, :].rearrange("p (a b) -> p a b", a=2), slot[e * ROPE:(e + 1) * ROPE, :, 0:HT],
                        tab[0:ROPE, :].rearrange("p (a b) -> p a b", a=2), ALU.mult))
                own.wait()
                dve.nop().then_inc(free, 1)
                own.step(dve.tensor_tensor(kr[:, :], rot[0:ROPE, 0, :], rot[0:ROPE, 1, :], ALU.add))
                own.wait()
                dve.nop().then_inc(kr_done, 1)
                kn.on_dve(dve, own)
                qn.on_dve(dve, own)
                for c in range(2):
                    for e, tab in enumerate((cos, sin)):
                        slot, free = lin.arrived(dve, ("q", 4 + 2 * c + e))
                        own.link(dve.tensor_tensor(rot[:, e, 0:SEQ], slot[:, 0, :], tab[:, NMETA:T1], ALU.mult))
                        dve.nop().then_inc(free, 1)
                    for a in range(4):
                        own.step(dve.tensor_tensor(out["qT"][NOPE:DQ, 4 * c + a, :], rot[a * ROPE:(a + 1) * ROPE, 0, 0:SEQ],
                                                   rot[a * ROPE:(a + 1) * ROPE, 1, 0:SEQ], ALU.add))
                    own.wait()
                dve.wait_ge(padded, 1)
                for k in range(CK):
                    for c in range(CT):
                        src = conv_in[:, c, NMETA + k:NMETA + k + SEQ]
                        w = kit.gain("conv_w", k * CT + c)
                        if k:
                            dve.wait_ge(own.sem, own.n - (CT - 1))
                            ins = dve.scalar_tensor_tensor(out=acc[:, c, :], in0=src, scalar=w, in1=acc[:, c, :],
                                                           op0=ALU.mult, op1=ALU.add)
                        else:
                            ins = dve.tensor_scalar(acc[:, c, :], src, w, kit.gain("conv_b", c), ALU.mult, ALU.add)
                        own.step(ins)
                        if k == CK - 1:
                            own.wait()
                            dve.nop().then_inc(conv_done, 1)
                dve.wait_ge(ln_sum, 1)
                own.link(dve.tensor_scalar(mu[:, :], ps[:, 4, :], 1.0 / CC, None, ALU.mult))
                for c in range(CT):
                    dve.tensor_tensor(acc[:, c, :], acc[:, c, :], mu[:, :], ALU.subtract).then_inc(centred, 1)
                dve.wait_ge(centred, CT)
                ln.on_dve(dve, own)
                cn.on_dve(dve, own)


class Attention:

    def __init__(self, st, items, s_slots, pt_slots, o_slots, pcols, flush):
        self.items, self.st = items, st
        self.ident = st.kit.ident
        self.S, self.PT, self.O, self.flush = s_slots, pt_slots, o_slots, flush
        self.pr = st.sb("probs", [P, 3, pcols])
        self.pts = st.sb("probsT", [P, 2, pt_slots[0].shape[-1]])
        n = len(items)
        self.mx = st.sb("mx", [P, 4])
        self.nm = st.sb("nm", [P, 4])
        self.ls = st.sb("ls", [P, 4])
        self.rl = st.sb("rl", [P, 4])
        names = ("scored", "maxed", "exped", "scaled", "turned", "copied", "summed", "flushed", "steps", "extra")
        self.s = {k: st.sem(k) for k in names}
        self.last = {}
        for i, it in enumerate(items):
            self.last[it["bank"]] = i

    def on_pe(self, pe):
        it, s, n_items = self.items, self.s, len(self.items)
        for n in range(n_items + 2):
            if n < n_items:
                x = it[n]
                if n >= len(self.S):
                    pe.wait_ge(s["exped"], n - len(self.S) + 1)
                for keys, col in x["ks"]:
                    mm = pe.matmul(self.S[n % len(self.S)][:, col:col + keys.shape[-1]], x["q"], keys,
                                   start=True, stop=True)
                mm.then_inc(s["scored"], 1)
            if 1 <= n <= n_items:
                x = it[n - 1]
                pe.wait_ge(s["scaled"], n)
                if n - 1 >= len(self.PT):
                    pe.wait_ge(s["copied"], n - len(self.PT))
                pr = self.pr[:, (n - 1) % 3, :]
                for j, (col, w, _) in enumerate(x["pts"]):
                    mm = pe.transpose(self.PT[(n - 1) % len(self.PT)][0:w, j * P:(j + 1) * P], pr[:, col:col + w],
                                      self.ident[:, :])
                mm.then_inc(s["turned"], 1)
            if n >= 2:
                x = it[n - 2]
                pe.wait_ge(s["copied"], n - 1)
                b = x["bank"]
                if b >= len(self.O) and (n == 2 or it[n - 3]["bank"] != b):
                    pe.wait_ge(s["flushed"], b - len(self.O) + 1)
                pt = self.pts[:, n % 2, :]
                for j, (_, w, v) in enumerate(x["pts"]):
                    mm = pe.matmul(x["out"](self.O[b % len(self.O)]), v, pt[0:w, j * P:(j + 1) * P],
                                   start=(x["start"] and j == 0), stop=(x["stop"] and j == len(x["pts"]) - 1))
                mm.then_inc(s["summed"], 1)

    def on_act(self, act):
        it, s, n_items = self.items, self.s, len(self.items)
        for n in range(n_items + 1):
            if n < n_items:
                x = it[n]
                act.wait_ge(s["maxed"], n + 1)
                if n >= 3:
                    act.wait_ge(s["turned"], n - 2)
                act.activation(self.pr[:, n % 3, 0:x["hi"] - x["lo"]], self.S[n % len(self.S)][:, x["lo"]:x["hi"]],
                               ACT.Exp, bias=self.nm[:, n % 4:n % 4 + 1], scale=x["scale"],
                               accum_out=self.ls[:, n % 4:n % 4 + 1]).then_inc(s["exped"], 1)
            if n >= 1:
                x = it[n - 1]
                act.wait_ge(s["turned"], n)
                if n >= 3:
                    act.wait_ge(s["summed"], n - 2)
                runs = []
                for j, (_, w, _) in enumerate(x["pts"]):
                    if runs and runs[-1][2] == w:
                        runs[-1][1] = j + 1
                    else:
                        runs.append([j, j + 1, w])
                for i, (a, b, w) in enumerate(runs):
                    c = act.activation(self.pts[0:w, (n - 1) % 2, a * P:b * P],
                                       self.PT[(n - 1) % len(self.PT)][0:w, a * P:b * P], ACT.Copy)
                    if i < len(runs) - 1:
                        c.then_inc(s["extra"], 1)
                        self.extra = self.extra + 1
                        act.wait_ge(s["extra"], self.extra)
                c.then_inc(s["copied"], 1)

    extra = 0

    def on_dve(self, dve):
        it, s, n_items = self.items, self.s, len(self.items)
        own = Count(dve, s["steps"])
        for n in range(n_items + 4):
            if n < n_items:
                x = it[n]
                S = self.S[n % len(self.S)]
                c = slice(n % 4, n % 4 + 1)
                dve.wait_ge(s["scored"], n + 1)
                for col, m in x["masks"]:
                    own.link(dve.tensor_tensor(S[:, col:col + m.shape[-1]], S[:, col:col + m.shape[-1]], m, ALU.add))
                own.link(dve.tensor_reduce(self.mx[:, c], S[:, x["lo"]:x["hi"]], AX, ALU.max))
                dve.tensor_scalar(self.nm[:, c], self.mx[:, c], -x["scale"], None, ALU.mult).then_inc(s["maxed"], 1)
            if 1 <= n <= n_items:
                x = it[n - 1]
                c = slice((n - 1) % 4, (n - 1) % 4 + 1)
                dve.wait_ge(s["exped"], n)
                own.link(dve.reciprocal(self.rl[:, c], self.ls[:, c]))
                pr = self.pr[:, (n - 1) % 3, 0:x["hi"] - x["lo"]]
                if x["gate"] is None:
                    ins = dve.tensor_scalar(pr, pr, self.rl[:, c], None, ALU.mult)
                else:
                    ins = dve.tensor_scalar(pr, pr, self.rl[:, c], x["gate"], ALU.mult, ALU.mult)
                if x["vis"] is not None:
                    own.link(ins)
                    ins = dve.tensor_tensor(pr, pr, x["vis"], ALU.mult)
                ins.then_inc(s["scaled"], 1)
            for b, i in self.last.items():
                if i + 3 == n:
                    dve.wait_ge(s["summed"], i + 1)
                    self.flush(dve, b, self.O[b % len(self.O)]).then_inc(s["flushed"], 1)


def mla(kit, io):
    nc = kit.nc
    with Stage(kit, "mla") as st:
        ps = st.banks()
        flat = ps[:, :, :].rearrange("p b n -> p (b n)")
        attn = st.sb("attnT", [P, CT, SEQ])
        items = []
        off = 512 - NMETA
        for hp in range(HEADS // 2):
            for h in (2 * hp, 2 * hp + 1):
                for j in range(ST):
                    keys = (j + 1) * P
                    items.append(dict(
                        q=io["qT"][:, h, j * P:(j + 1) * P],
                        ks=[(io["kT"][:, h, 0:NMETA], off), (io["kT"][:, h, NMETA:NMETA + keys], 512)],
                        lo=off, hi=512 + keys, masks=[(512 + j * P, kit.tri[:, :])],
                        pts=[(NMETA + i * P, P, io["v"][:, i, h * VH:(h + 1) * VH]) for i in range(j + 1)]
                        + [(0, NMETA, io["v"][0:NMETA, ST, h * VH:(h + 1) * VH])],
                        out=lambda o, e=h % 2, j=j: o[e * VH:(e + 1) * VH, j * P:(j + 1) * P],
                        bank=hp, start=True, stop=True, scale=DQ ** -0.5, gate=None, vis=None))
        at = Attention(st, items, [flat[:, 0:1024], flat[:, 1024:2048]], [flat[:, 2048:2048 + 640]],
                       [ps[:, 6, :], ps[:, 7, :]], T1,
                       lambda dve, b, o: dve.tensor_copy(attn[:, b, :], o))
        an = Norm(st, "an", lambda j: attn[:, j, :], lambda j: io["mixT"][:, j, :], CT, SEQ, EPS1,
                  lambda j: kit.gain("g_out_attn", j), ps[:, 0:1, :], 1, need=(at.s["flushed"], lambda j: j + 1))
        own_sem = st.sem("vector_steps")
        with nc.Block() as block:

            @block.tensor
            def _(pe):
                at.on_pe(pe)
                an.on_pe(pe)

            @block.scalar
            def _(act):
                at.on_act(act)
                an.on_act(act)

            @block.vector
            def _(dve):
                at.on_dve(dve)
                an.on_dve(dve, Count(dve, own_sem))


def route(kit, io):
    nc, t = kit.nc, kit.t
    NS = 2 * PH
    with Stage(kit, "route") as st:
        ps = st.banks()
        ring = WeightRing(st, "w", 4, D, pieces(t["w_out"], DT, D) + pieces(t["peer_wq"], DT, D))
        keys = st.sb("keys", [P, PH, NK])
        qT = st.sb("qT", [P, PH, SEQ])
        sc = st.sb("scores", [P, NS, NK])
        rest = st.sb("rest", [P, NS, NK])
        sv = st.sb("sv", [P, PH, 2, TOPK])
        si = st.sb("si", [P, NS, TOPK], U32)
        sif = st.sb("sif", [P, PH, 2, TOPK])
        cand = st.sb("cand", [P, PH, TOPK * TOPK])
        left = st.sb("left", [P, PH, TOPK * TOPK])
        tops = st.sb("tops", [P, PH, TOPK])
        sel = st.sb("sel", [P, PH, TOPK], U32)
        ab = st.sb("ab", [P, 2, PH * TOPK], U32)
        abf = st.sb("abf", [P, 2, PH * TOPK])
        eq = st.sb("eq", [P, PH, TOPK, TOPK])
        three = st.sb("three", [P, 3, PH * TOPK])
        tot = st.sb("tot", [P, PH])
        i16 = st.sb("i16", [P, TOPK])
        side = st.sem("side_loaded")
        hsum = st.sem("residual_added")
        q_copied = st.sem("q_copied")
        scored = st.sem("scored")
        s_copied = st.sem("s_copied")
        s_used = st.sem("s_used")
        shifted = st.sem("shifted")
        exped = st.sem("exped")
        ready = st.sem("gates_ready")
        turned = st.sem("turned")
        own_sem = st.sem("vector_steps")
        fin_sem = st.sem("turned_copied")

        fn = Norm(st, "fn", lambda j: kit.real(j), lambda j: io["xn"][:, j, :], DT, SEQ, EPS1,
                  lambda j: kit.gain("g_ffn_norm", j), ps[:, 4:5, :], 1, need=(hsum, lambda j: j + 1))
        tiles = [(("o", n), P, DT, lambda k: [io["mixT"][:, k, :]], None) for n in range(DT)]
        tiles += [(("q", n), P, DT, lambda k: [io["xn"][:, k, :]], (fn.out, DT)) for n in range(DT)]
        lin = Linear(st, ring, one_bank_slots(ps, 0, 4), tiles)
        with nc.Block() as block:

            @block.sync
            def _(sp):
                sp.dma_start(keys[:, :, :], t["peer_keys"].rearrange("p (h n) -> p h n", h=PH)).then_inc(side, 16)
                sp.dma_start(i16[:, :], t["c_iota"][:, 0:TOPK]).then_inc(side, 16)
                ring.load_all(sp, lin.done)

            @block.tensor
            def _(pe):
                lin.run(pe, lambda n: n < DT)
                fn.on_pe(pe)
                lin.run(pe, lambda n: n >= DT)
                pe.wait_ge(side, 32)
                pe.wait_ge(q_copied, DT)
                for j in range(ST):
                    if j:
                        pe.wait_ge(s_copied, 4 * j)
                    for h in range(PH):
                        for half in range(2):
                            lo = half * (P // 2)
                            bank = 2 * half + h // 4
                            mm = pe.matmul(ps[:, bank, (h % 4) * NK:(h % 4 + 1) * NK],
                                           qT[lo:lo + P // 2, h, j * P:(j + 1) * P], keys[lo:lo + P // 2, h, :],
                                           start=True, stop=True)
                    mm.then_inc(scored, 1)
                    pe.wait_ge(ready, j + 1)
                    for i in range(3):
                        mm = pe.transpose(ps[:, 5 + i, j * P:(j + 1) * P], three[:, i, :], kit.ident[:, :])
                    mm.then_inc(turned, 1)

            @block.scalar
            def _(act):
                fn.on_act(act)
                for n in range(DT):
                    slot, free = lin.arrived(act, ("q", n))
                    act.activation(qT[:, n, :], slot[:, 0, :], ACT.Copy).then_inc(q_copied, 1)
                    act.wait_ge(q_copied, n + 1)
                    act.nop().then_inc(free, 1)
                for j in range(ST):
                    act.wait_ge(scored, j + 1)
                    if j:
                        act.wait_ge(s_used, j)
                    for bank in range(4):
                        half, h0 = bank // 2, 4 * (bank % 2)
                        act.activation(sc[:, :, :].rearrange("p (h a) n -> p h a n", a=2)[:, h0:h0 + 4, half, :],
                                       ps[:, bank, :].rearrange("p (h n) -> p h n", h=4), ACT.Copy)\
                            .then_inc(s_copied, 1)
                    act.wait_ge(shifted, j + 1)
                    act.activation(tops[:, :, :], tops[:, :, :], ACT.Exp).then_inc(exped, 1)

            @block.vector
            def _(dve):
                own = Count(dve, own_sem)
                for n in range(DT):
                    slot, free = lin.arrived(dve, ("o", n))
                    dve.tensor_tensor(kit.real(n), kit.real(n), slot[:, 0, :], ALU.add).then_inc(hsum, 1)
                    dve.wait_ge(hsum, n + 1)
                    dve.nop().then_inc(free, 1)
                fn.on_dve(dve, own)
                dve.wait_ge(side, 32)
                svf = sv[:, :, :, :].rearrange("p h a k -> p (h a) k")
                for j in range(ST):
                    dve.wait_ge(s_copied, 4 * (j + 1))
                    for i in range(NS):
                        own.step(dve.max(svf[:, i, 0:8], sc[:, i, :]))
                    own.wait()
                    for i in range(NS):
                        own.step(dve.max_index(si[:, i, 0:8], svf[:, i, 0:8], sc[:, i, :]))
                        own.step(dve.match_replace(rest[:, i, :], svf[:, i, 0:8], sc[:, i, :], -3e38))
                    own.wait()
                    dve.nop().then_inc(s_used, 1)
                    for i in range(NS):
                        own.step(dve.max(svf[:, i, 8:16], rest[:, i, :]))
                    own.wait()
                    for i in range(NS):
                        own.step(dve.max_index(si[:, i, 8:16], svf[:, i, 8:16], rest[:, i, :]))
                    own.wait()
                    own.step(dve.tensor_copy(sif[:, :, :, :].rearrange("p h a k -> p (h a) k"), si[:, :, :]))
                    for h in range(PH):
                        own.step(dve.tensor_tensor(
                            cand[:, h, :].rearrange("p (a b) -> p a b", a=TOPK),
                            sv[:, h, 0, :].unsqueeze(2).to_broadcast([P, TOPK, TOPK]),
                            sv[:, h, 1, :].unsqueeze(1).to_broadcast([P, TOPK, TOPK]), ALU.add))
                    own.wait()
                    for h in range(PH):
                        own.step(dve.max(tops[:, h, 0:8], cand[:, h, :]))
                    own.wait()
                    for h in range(PH):
                        own.step(dve.max_index(sel[:, h, 0:8], tops[:, h, 0:8], cand[:, h, :]))
                        own.step(dve.match_replace(left[:, h, :], tops[:, h, 0:8], cand[:, h, :], -3e38))
                    own.wait()
                    for h in range(PH):
                        own.step(dve.max(tops[:, h, 8:16], left[:, h, :]))
                    own.wait()
                    for h in range(PH):
                        own.step(dve.max_index(sel[:, h, 8:16], tops[:, h, 8:16], left[:, h, :]))
                    own.step(dve.tensor_copy(tot[:, :], tops[:, :, 0]))
                    own.wait()
                    dve.tensor_tensor(tops[:, :, :], tops[:, :, :], tot[:, :].unsqueeze(2).to_broadcast([P, PH, TOPK]),
                                      ALU.subtract).then_inc(shifted, 1)
                    self_ = sel[:, :, :].rearrange("p h k -> p (h k)")
                    own.step(dve.tensor_scalar(ab[:, 0, :], self_, 4, None, ALU.logical_shift_right))
                    own.step(dve.tensor_scalar(ab[:, 1, :], self_, 15, None, ALU.bitwise_and))
                    own.wait()
                    own.link(dve.tensor_copy(abf[:, :, :], ab[:, :, :]))
                    if j:
                        dve.wait_ge(turned, j)
                    for i in range(2):
                        own.link(dve.tensor_tensor(
                            eq[:, :, :, :].rearrange("p h k a -> p (h k) a"),
                            abf[:, i, :].unsqueeze(2).to_broadcast([P, PH * TOPK, TOPK]),
                            i16[:, :].unsqueeze(1).to_broadcast([P, PH * TOPK, TOPK]), ALU.is_equal))
                        for h in range(PH):
                            own.step(dve.tensor_tensor(
                                eq[:, h, :, :], eq[:, h, :, :],
                                sif[:, h, i, :].unsqueeze(1).to_broadcast([P, TOPK, TOPK]), ALU.mult))
                        own.wait()
                        own.link(dve.tensor_reduce(three[:, i, :], eq[:, :, :, :].rearrange("p h k a -> p (h k) a"),
                                                   AX, ALU.add))
                    dve.wait_ge(exped, j + 1)
                    own.link(dve.tensor_reduce(tot[:, :], tops[:, :, :], AX, ALU.add))
                    own.link(dve.reciprocal(tot[:, :], tot[:, :]))
                    dve.scalar_tensor_tensor(
                        out=three[:, 2, :].rearrange("p (h k) -> p h k", h=PH), in0=tops[:, :, :], scalar=GSCALE,
                        in1=tot[:, :].unsqueeze(2).to_broadcast([P, PH, TOPK]), op0=ALU.mult, op1=ALU.mult)\
                        .then_inc(ready, 1)
                    dve.wait_ge(ready, j + 1)
                dve.wait_ge(turned, ST)
                for i in range(2):
                    own.step(dve.tensor_copy(io["idxT"][:, i, :], ps[:, 5 + i, :]))
                own.link(dve.tensor_copy(io["g16"][:, :], ps[:, 7, :]))
                own.link(dve.tensor_copy(io["gT"][:, 0, :], io["g16"][:, :]))
                own.link(dve.tensor_tensor(io["gT"][:, 1, :], ps[:, 7, :], io["gT"][:, 0, :], ALU.subtract))


CHUNKS = NK
PARTS = 4
PCH = CHUNKS // PARTS
TB = SEQ // PCH
GRP = 4


def experts(kit, io):
    nc, t = kit.nc, kit.t
    with Stage(kit, "experts") as st:
        ps = st.banks()
        G = st.sb("gates", [P, PCH * SEQ])
        U = st.sb("u", [P, GRP, DT, P])
        V = st.sb("v", [P, 2, GRP, D])
        W = st.sb("w", [P, 2, GRP, SEQ])
        O2 = st.sb("second_hot", [P, 2, TB, P], F16)
        O1 = st.sb("first_hot", [P, 2, 2, TB, PCH], F16)
        E1 = st.sb("first_eq", [P, TB, PCH], F16)
        iota = st.sb("iota", [P, P])
        side = st.sem("side_loaded")
        u_in = [st.sem(f"u_in{i}") for i in range(GRP)]
        v_in = [st.sem(f"v_in{i}") for i in range(2)]
        acted = st.sem("first_done")
        gelued = st.sem("gelued")
        weighed = st.sem("weighed")
        hot = st.sem("hot_made")
        gated = st.sem("gates_summed")
        gcopied = st.sem("gates_copied")
        odone = st.sem("second_done")
        oadded = st.sem("second_added")
        own_sem = st.sem("vector_steps")
        groups = CHUNKS // GRP

        def region(par, n):
            if par == 0:
                return G[:, n * SEQ:(n + 1) * SEQ].rearrange("p (s t) -> p s t", s=PCH)
            return G[:, :].rearrange("p (s n t) -> p s n t", s=PCH, n=PCH)[:, :, n, :]

        with nc.Block() as block:

            @block.sync
            def _(sp):
                sp.dma_start(iota[:, :], t["c_iota"]).then_inc(side, 16)
                for g in range(groups):
                    for c in range(GRP):
                        n = g * GRP + c
                        if n >= GRP:
                            sp.wait_ge(acted, n - GRP + 1)
                        sp.dma_start(U[:, c, :, :], t["peer_uT"][n * P:(n + 1) * P, :]
                                     .rearrange("p (k e) -> p k e", k=DT)).then_inc(u_in[c], 16)
                    if g >= 2:
                        sp.wait_ge(odone, DT * (g - 1))
                    sp.dma_start(V[:, g % 2, :, :], t["peer_v"][g * GRP * P:(g + 1) * GRP * P, :]
                                 .rearrange("(c p) d -> p c d", p=P)).then_inc(v_in[g % 2], 16)

            def gate_block(pe, b):
                pe.wait_ge(hot, b + 1)
                if b >= 2:
                    pe.wait_ge(gcopied, b - 1)
                for i in range(TB):
                    for piece in range(2):
                        mm = pe.matmul(ps[:, 6 + b % 2, i * PCH:(i + 1) * PCH], O2[:, b % 2, i, :],
                                       O1[:, b % 2, piece, i, :], start=(piece == 0), stop=(piece == 1))
                mm.then_inc(gated, 1)

            @block.tensor
            def _(pe):
                for b in range(PCH):
                    gate_block(pe, b)
                for g in range(groups + 1):
                    if g < groups:
                        for c in range(GRP):
                            n = g * GRP + c
                            pe.wait_ge(u_in[c], 16 * (g + 1))
                            if n >= 3:
                                pe.wait_ge(gelued, n - 2)
                            for k in range(DT):
                                mm = pe.matmul(ps[:, n % 3, :], U[:, c, k, :], io["xn"][:, k, :],
                                               start=(k == 0), stop=(k == DT - 1))
                            mm.then_inc(acted, 1)
                            if n < CHUNKS - PCH:
                                gate_block(pe, PCH + n)
                    if g >= 1:
                        q = g - 1
                        pe.wait_ge(v_in[q % 2], 16 * (q // 2 + 1))
                        pe.wait_ge(weighed, GRP * g)
                        for d in range(DT):
                            m = q * DT + d
                            if m >= 3:
                                pe.wait_ge(oadded, m - 2)
                            for c in range(GRP):
                                mm = pe.matmul(ps[:, 3 + m % 3, :], V[:, q % 2, c, d * P:(d + 1) * P],
                                               W[:, q % 2, c, :], start=(c == 0), stop=(c == GRP - 1))
                            mm.then_inc(odone, 1)

            @block.scalar
            def _(act):
                for n in range(CHUNKS):
                    g = n // GRP
                    act.wait_ge(acted, n + 1)
                    if g >= 2:
                        act.wait_ge(odone, DT * (g - 1))
                    act.activation(W[:, g % 2, n % GRP, :], ps[:, n % 3, :], ACT.Gelu).then_inc(gelued, 1)

            @block.vector
            def _(dve):
                own = Count(dve, own_sem)
                dve.wait_ge(side, 16)

                def hots(b):
                    part, tb = b // PCH, b % PCH
                    tok = slice(tb * TB, (tb + 1) * TB)
                    if b >= 2:
                        dve.wait_ge(gated, b - 1)
                    own.step(dve.tensor_tensor(O2[:, b % 2, :, :], iota[:, :].unsqueeze(1).to_broadcast([P, TB, P]),
                                               io["idxT"][:, 1, tok].unsqueeze(2).to_broadcast([P, TB, P]),
                                               ALU.is_equal))
                    own.step(dve.tensor_tensor(
                        E1[:, :, :], iota[:, part * PCH:(part + 1) * PCH].unsqueeze(1).to_broadcast([P, TB, PCH]),
                        io["idxT"][:, 0, tok].unsqueeze(2).to_broadcast([P, TB, PCH]), ALU.is_equal))
                    own.wait()
                    for piece in range(2):
                        own.step(dve.tensor_tensor(
                            O1[:, b % 2, piece, :, :], E1[:, :, :],
                            io["gT"][:, piece, tok].unsqueeze(2).to_broadcast([P, TB, PCH]), ALU.mult))
                    own.wait()
                    dve.nop().then_inc(hot, 1)

                def keep(b, par):
                    dve.wait_ge(gated, b + 1)
                    dve.tensor_copy(region(par, b % PCH),
                                    ps[:, 6 + b % 2, :].rearrange("p (t i) -> p i t", i=PCH)).then_inc(gcopied, 1)

                for b in range(PCH + 1):
                    if b < PCH:
                        hots(b)
                    if b:
                        keep(b - 1, 1)
                dve.wait_ge(gcopied, PCH)

                def add_group(q):
                    for d in range(DT):
                        m = q * DT + d
                        dve.wait_ge(odone, m + 1)
                        if q:
                            dve.wait_ge(oadded, m - DT + 1)
                        dve.tensor_tensor(kit.real(d), kit.real(d), ps[:, 3 + m % 3, :], ALU.add).then_inc(oadded, 1)

                hots(PCH)
                for g in range(groups + 1):
                    if g < groups:
                        for c in range(GRP):
                            n = g * GRP + c
                            par = (n // PCH) % 2
                            dve.wait_ge(gelued, n + 1)
                            dve.wait_ge(gcopied, PCH * (n // PCH + 1))
                            w = W[:, g % 2, c, :].rearrange("p (s t) -> p s t", s=PCH)
                            dve.scalar_tensor_tensor(out=w, in0=region(par, n % PCH), scalar=1.0 / GSCALE, in1=w,
                                                     op0=ALU.mult, op1=ALU.mult).then_inc(weighed, 1)
                            if n < CHUNKS - PCH:
                                dve.wait_ge(weighed, n + 1)
                                keep(PCH + n, par)
                                if n + 1 < CHUNKS - PCH:
                                    hots(PCH + n + 1)
                    if g >= 1:
                        add_group(g - 1)
                dve.wait_ge(oadded, groups * DT)


def short(kit):
    nc, t = kit.nc, kit.t
    with Stage(kit, "short") as st:
        ps = st.banks()
        hn = st.sb("hn", [P, DT, SEQ])
        cbuf = st.sb("c", [P, 2, SEQ])
        cv = st.sb("cv", [P, 2, 2 + SEQ])
        u = st.sb("u", [P, DT, SEQ])
        ring = WeightRing(st, "w", 4, D, pieces(t["a_w_in"], 3 * DT, D) + pieces(t["a_w_out"], DT, D))
        gf = Norm(st, "gf", kit.real, kit.real, DT, SEQ, EPS1, lambda j: kit.gain("g_final", j), ps[:, 7:8, :], 1)
        an = Norm(st, "an", kit.real, lambda j: hn[:, j, :], DT, SEQ, EPS2, lambda j: kit.gain("a_norm_2", j),
                  ps[:, 7:8, :], 1, need=(gf.out, lambda j: j + 1))
        padded, copied, mixed, added = st.sem("padded"), st.sem("c_copied"), st.sem("mixed"), st.sem("added")
        own_sem = st.sem("vector_steps")
        tiles = []
        for i in range(DT):
            for part in "cvb":
                tiles.append(((part, i), P, DT, lambda k: [hn[:, k, :]], (an.out, DT) if not tiles else None))
        for n in range(DT):
            tiles.append((("o", n), P, DT, lambda k: [u[:, k, :]], (mixed, DT)))
        lin = Linear(st, ring, one_bank_slots(ps, 0, 7), tiles)
        with nc.Block() as block:

            @block.sync
            def _(sp):
                ring.load_all(sp, lin.done)

            @block.gpsimd
            def _(pool):
                pool.memset(cv[:, :, 0:2], 0.0).then_inc(padded, 1)

            @block.tensor
            def _(pe):
                gf.on_pe(pe)
                pe.wait_ge(gf.var, 1)
                an.on_pe(pe)
                lin.run(pe)

            @block.scalar
            def _(act):
                gf.on_act(act)
                an.on_act(act)
                for i in range(DT):
                    slot, free = lin.arrived(act, ("c", i))
                    if i >= 2:
                        act.wait_ge(mixed, i - 1)
                    act.activation(cbuf[:, i % 2, :], slot[:, 0, :], ACT.Copy).then_inc(copied, 1)
                    act.wait_ge(copied, i + 1)
                    act.nop().then_inc(free, 1)

            @block.vector
            def _(dve):
                own = Count(dve, own_sem)
                gf.on_dve(dve, own)
                an.on_dve(dve, own)
                dve.wait_ge(padded, 1)
                for i in range(DT):
                    slot, free = lin.arrived(dve, ("v", i))
                    dve.wait_ge(copied, i + 1)
                    own.link(dve.tensor_tensor(cv[:, i % 2, 2:], slot[:, 0, :], cbuf[:, i % 2, :], ALU.mult))
                    dve.nop().then_inc(free, 1)
                    w = [kit.gain("a_conv_2", k * DT + i) for k in range(3)]
                    own.link(dve.tensor_scalar(u[:, i, :], cv[:, i % 2, 0:SEQ], w[0], None, ALU.mult))
                    for k in (1, 2):
                        own.link(dve.scalar_tensor_tensor(out=u[:, i, :], in0=cv[:, i % 2, k:k + SEQ], scalar=w[k],
                                                          in1=u[:, i, :], op0=ALU.mult, op1=ALU.add))
                    slot, free = lin.arrived(dve, ("b", i))
                    own.link(dve.tensor_tensor(u[:, i, :], u[:, i, :], slot[:, 0, :], ALU.mult))
                    dve.nop().then_inc(free, 1)
                    dve.nop().then_inc(mixed, 1)
                for n in range(DT):
                    slot, free = lin.arrived(dve, ("o", n))
                    dve.tensor_tensor(kit.real(n), kit.real(n), slot[:, 0, :], ALU.add).then_inc(added, 1)
                    dve.wait_ge(added, n + 1)
                    dve.nop().then_inc(free, 1)


def ffn(kit, layer, final=None):
    nc, t = kit.nc, kit.t
    with Stage(kit, f"ffn{layer}") as st:
        ps = st.banks()
        hn = st.sb("hn", [P, DT, SEQ])
        silu = st.sb("silu", [P, 2, SEQ])
        mid = st.sb("mid", [P, FT, SEQ])
        gu = t["f_w_gu"][layer * 2 * FT * P:(layer + 1) * 2 * FT * P, :]
        down = t["f_w_down"][layer * DT * P:(layer + 1) * DT * P, :]
        ring = WeightRing(st, "w", 4, F, pieces(gu, 2 * FT, D) + pieces(down, DT, F))
        fn = Norm(st, "fn", kit.real, lambda j: hn[:, j, :], DT, SEQ, EPS2,
                  lambda j: kit.gain("f_norm_2", layer * DT + j), ps[:, 7:8, :], 1)
        silued, mixed, added = st.sem("silued"), st.sem("mixed"), st.sem("added")
        own_sem, stored = st.sem("vector_steps"), kit.stored
        last = None
        if final is not None:
            last = Norm(st, "last", kit.real, lambda j: hn[:, j, :], DT, SEQ, EPS2,
                        lambda j: kit.gain("final_norm_2", j), ps[:, 7:8, :], 1, need=(added, lambda j: j + 1))
        tiles = []
        for i in range(FT):
            for part in "gu":
                tiles.append(((part, i), P, DT, lambda k: [hn[:, k, :]], (fn.out, DT) if not tiles else None))
        for n in range(DT):
            tiles.append((("d", n), P, FT, lambda k: [mid[:, k, :]], (mixed, FT)))
        lin = Linear(st, ring, one_bank_slots(ps, 0, 7), tiles)
        with nc.Block() as block:

            @block.sync
            def _(sp):
                ring.load_all(sp, lin.done)
                if last is not None:
                    for j in range(DT):
                        sp.wait_ge(last.out, j + 1)
                        sp.dma_start(final[j * P:(j + 1) * P, :], hn[:, j, :]).then_inc(stored, 16)
                    sp.wait_ge(stored, 16 * DT)

            @block.tensor
            def _(pe):
                fn.on_pe(pe)
                lin.run(pe)
                if last is not None:
                    last.on_pe(pe)

            @block.scalar
            def _(act):
                fn.on_act(act)
                for i in range(FT):
                    slot, free = lin.arrived(act, ("g", i))
                    if i >= 2:
                        act.wait_ge(mixed, i - 1)
                    act.activation(silu[:, i % 2, :], slot[:, 0, :], ACT.Silu).then_inc(silued, 1)
                    act.wait_ge(silued, i + 1)
                    act.nop().then_inc(free, 1)
                if last is not None:
                    last.on_act(act)

            @block.vector
            def _(dve):
                own = Count(dve, own_sem)
                fn.on_dve(dve, own)
                for i in range(FT):
                    slot, free = lin.arrived(dve, ("u", i))
                    dve.wait_ge(silued, i + 1)
                    dve.tensor_tensor(mid[:, i, :], slot[:, 0, :], silu[:, i % 2, :], ALU.mult).then_inc(mixed, 1)
                    dve.wait_ge(mixed, i + 1)
                    dve.nop().then_inc(free, 1)
                for n in range(DT):
                    slot, free = lin.arrived(dve, ("d", n))
                    dve.tensor_tensor(kit.real(n), kit.real(n), slot[:, 0, :], ALU.add).then_inc(added, 1)
                    dve.wait_ge(added, n + 1)
                    dve.nop().then_inc(free, 1)
                if last is not None:
                    last.on_dve(dve, own)


def nsa_in(kit, io):
    nc, t = kit.nc, kit.t
    with Stage(kit, "nsain") as st:
        ps = st.banks()
        hk = st.sb("hk", [P, DT, SEQ])
        hq = st.sb("hq", [P, DT, SEQ])
        kn = Norm(st, "kn", kit.real, lambda j: hk[:, j, :], DT, SEQ, EPS2, lambda j: kit.gain("kv_norm_2", j),
                  ps[:, 7:8, :], 1)
        wv = st.sb("wv", [P, DT, 2 * NG * HD])
        wg = st.sb("wg", [P, DT, 3 * NH])
        raw = st.sb("raw", [P, 2, NG, SEQ])
        X = st.sb("X", [P, 2, 2, NG, SEQ // DC, DC // 2])
        w1 = st.sb("w1", [P, LC // 2, CH])
        w2 = st.sb("w2", [P, 2, 2, HD])
        pe2 = st.sb("pe2", [P, 2, LC])
        hid = st.sb("hid", [P, 2, NG * NC])
        side = st.sem("side_loaded")
        w1_in = [st.sem("w1k_loaded"), st.sem("w1v_loaded")]
        ring = WeightRing(st, "w", 4, D, pieces(t["w_kraw"], 8, D) + pieces(t["w_q2"], DT, D))
        b_out = st.sem("b_normed")
        tiles = [(("k", n), P, DT, lambda k: [hk[:, k, :]], (kn.out, DT)) for n in range(8)]
        tiles += [(("q", n), P, DT, lambda k: [hq[:, k, :]], (b_out, DT)) for n in range(DT)]
        lin = Linear(st, ring, one_bank_slots(ps, 0, 5), tiles)
        own_sem = st.sem("vector_steps")
        act_sem = st.sem("scalar_steps")
        vdone, vcopied = st.sem("v_done"), st.sem("v_copied")
        gdone, gcopied = st.sem("g_done"), st.sem("g_copied")
        x_made, hid_done, hid_silu, c_done, c_copied = (st.sem(n) for n in
                                                        ("x_made", "hid_done", "hid_silu", "c_done", "c_copied"))
        rawed = st.sem("rawed")
        with nc.Block() as block:

            @block.sync
            def _(sp):
                sp.dma_start(wv[:, :, :], t["w_v2"].rearrange("p (k n) -> p k n", k=DT)).then_inc(side, 16)
                sp.dma_start(wg[:, :, :], t["w_gate2"].rearrange("p (k n) -> p k n", k=DT)).then_inc(side, 16)
                sp.dma_start(w2[:, :, :, :], t["cmp_w2"].rearrange("p (a c n) -> p a c n", a=2, c=2)).then_inc(side, 16)
                sp.dma_start(pe2[:, :, :], t["cmp_pe"].rearrange("p (a l) -> p a l", a=2)).then_inc(side, 16)
                for h in range(NH):
                    sp.dma_start(io["qT"][HD:HD + 2, h, :], t["c_qrows"][2 * h:2 * h + 2, :]).then_inc(side, 16)
                for g in range(NG):
                    for b in range(2):
                        sp.dma_start(io["kT"][HD:HD + 2, b, g, :], t["c_krows"]).then_inc(side, 16)
                sp.dma_start(io["kc"][HD:HD + 2, :, :], t["c_crows"].rearrange("r (g n) -> r g n", g=NG)).then_inc(side, 16)
                sp.dma_start(io["vis"][:, :, :, :], t["c_vis"].rearrange("p (a j n) -> p a j n", a=2, j=ST)).then_inc(side, 16)
                sp.dma_start(w1[:, :, :], t["cmp_w1"][0:P, :].rearrange("p (m c) -> p m c", c=CH)).then_inc(w1_in[0], 16)
                ring.load_all(sp, lin.done)
                sp.wait_ge(hid_done, 1)
                sp.dma_start(w1[:, :, :], t["cmp_w1"][P:2 * P, :].rearrange("p (m c) -> p m c", c=CH)).then_inc(w1_in[1], 16)

            n_side = 16 * (4 + NH + 2 * NG + 2)

            @block.tensor
            def _(pe):
                kn.on_pe(pe)
                lin.run(pe)
                pe.wait_ge(side, n_side)
                for s in range(2):
                    pe.wait_ge(lin.free[s], len([n for n in range(len(tiles)) if n % 5 == s]))
                for j in range(ST):
                    if j >= 1:
                        pe.wait_ge(vcopied, j)
                    for k in range(DT):
                        mm = pe.matmul(ps[:, 0, :], hk[:, k, j * P:(j + 1) * P], wv[:, k, :],
                                       start=(k == 0), stop=(k == DT - 1))
                    mm.then_inc(vdone, 1)
                    if j >= 1:
                        pe.wait_ge(gcopied, j)
                    for k in range(DT):
                        mm = pe.matmul(ps[:, 1, 0:3 * NH], hq[:, k, j * P:(j + 1) * P], wg[:, k, :],
                                       start=(k == 0), stop=(k == DT - 1))
                    mm.then_inc(gdone, 1)
                for kind in range(2):
                    pe.wait_ge(w1_in[kind], 16)
                    pe.wait_ge(x_made, kind + 1)
                    for c in range(2):
                        for m in range(LC // 2):
                            win, r = m // (DC // 2), m % (DC // 2)
                            mm = pe.matmul(ps[:, 5 + c, 0:NG * NC], w1[:, m, c * P:(c + 1) * P],
                                           X[:, kind, win, :, win:win + NC, r], start=(m == 0), stop=(m == LC // 2 - 1))
                    mm.then_inc(hid_done, 1)
                    pe.wait_ge(hid_silu, 2 * (kind + 1))
                    if kind == 0:
                        for c in range(2):
                            mm = pe.matmul(ps[0:HD, 7, 0:NG * NC], w2[:, 0, c, :], hid[:, c, :],
                                           start=(c == 0), stop=(c == 1))
                        mm.then_inc(c_done, 1)
                        pe.wait_ge(c_copied, 1)
                    else:
                        for g in range(NG):
                            for c in range(2):
                                mm = pe.matmul(ps[0:NC, 7, g * HD:(g + 1) * HD], hid[:, c, g * NC:(g + 1) * NC],
                                               w2[:, 1, c, :], start=(c == 0), stop=(c == 1))
                        mm.then_inc(c_done, 1)

            @block.scalar
            def _(act):
                own = Count(act, act_sem)
                kn.on_act(act)
                for n in (4, 5, 6, 7):
                    slot, free = lin.arrived(act, ("k", n))
                    for e in range(2):
                        own.step(act.activation(io["kT"][0:HD, (n - 4) // 2, 2 * (n % 2) + e, :],
                                                slot[e * HD:(e + 1) * HD, 0, :], ACT.Copy))
                    own.wait()
                    act.nop().then_inc(free, 1)
                for n in range(DT):
                    slot, free = lin.arrived(act, ("q", n))
                    for e in range(2):
                        own.step(act.activation(io["qT"][0:HD, 2 * n + e, :], slot[e * HD:(e + 1) * HD, 0, :],
                                                ACT.Copy, scale=HD ** -0.5))
                    own.wait()
                    act.nop().then_inc(free, 1)
                for j in range(ST):
                    act.wait_ge(vdone, j + 1)
                    act.activation(io["v"][:, j, :], ps[:, 0, :], ACT.Copy).then_inc(vcopied, 1)
                    act.wait_ge(gdone, j + 1)
                    act.activation(io["gate"][:, j, :], ps[:, 1, 0:3 * NH], ACT.Sigmoid).then_inc(gcopied, 1)
                for kind in range(2):
                    act.wait_ge(hid_done, kind + 1)
                    if kind:
                        act.wait_ge(c_done, 1)
                    for c in range(2):
                        act.activation(hid[:, c, :], ps[:, 5 + c, 0:NG * NC], ACT.Silu).then_inc(hid_silu, 1)
                act.wait_ge(c_done, 2)
                own.link(act.activation(io["vc"][:, :], ps[0:NC, 7, 0:NG * HD], ACT.Copy))

            @block.vector
            def _(dve):
                own = Count(dve, own_sem)
                kn.on_dve(dve, own)
                for j in range(DT):
                    dve.scalar_tensor_tensor(out=hq[:, j, :], in0=kit.real(j), scalar=kit.gain("b_norm_2", j),
                                             in1=kn.rs[:, :], op0=ALU.mult, op1=ALU.mult).then_inc(b_out, 1)
                dve.wait_ge(side, n_side)
                for kind in range(2):
                    for n in range(2):
                        slot, free = lin.arrived(dve, ("k", 2 * kind + n))
                        for e in range(2):
                            g = 2 * n + e
                            own.step(dve.tensor_copy(raw[0:HD, kind, g, :], slot[e * HD:(e + 1) * HD, 0, :]))
                            own.step(dve.tensor_copy(raw[HD:P, kind, g, 0:SEQ - 1], slot[e * HD:(e + 1) * HD, 0, 1:SEQ]))
                        own.wait()
                        dve.nop().then_inc(free, 1)
                    for win in range(2):
                        for g in range(NG):
                            own.step(dve.tensor_tensor(
                                X[:, kind, win, g, :, :], raw[:, kind, g, :].rearrange("p (n r) -> p n r", r=DC)[:, :, 0:DC:2],
                                pe2[:, kind, win * DC:(win + 1) * DC:2].unsqueeze(1)
                                .to_broadcast([P, SEQ // DC, DC // 2]), ALU.add))
                    own.wait()
                    dve.nop().then_inc(x_made, 1)
                dve.wait_ge(c_done, 1)
                dve.tensor_copy(io["kc"][0:HD, :, :].rearrange("p g n -> p (g n)"), ps[0:HD, 7, 0:NG * NC])\
                   .then_inc(c_copied, 1)


def nsa(kit, io):
    nc = kit.nc
    with Stage(kit, "nsa") as st:
        ps = st.banks()
        items = []
        for hp in range(NH // 2):
            for j in range(ST):
                for h in (2 * hp, 2 * hp + 1):
                    g = h // HPG
                    q = io["qT"][:, h, j * P:(j + 1) * P]
                    out = lambda o, e=h % 2, j=j: o[e * HD:(e + 1) * HD, j * P:(j + 1) * P]
                    gate = lambda b: io["gate"][:, j, 3 * h + b:3 * h + b + 1]
                    items.append(dict(q=q, ks=[(io["kc"][:, g, :], 0)], lo=0, hi=NC,
                                      masks=[(0, io["vis"][:, 0, j, :])],
                                      pts=[(0, NC, io["vc"][:, g * HD:(g + 1) * HD])], out=out, bank=hp,
                                      start=True, stop=False, scale=1.0, gate=gate(0), vis=io["vis"][:, 1, j, :]))
                    for b in range(2):
                        n = (j + 1) * P
                        items.append(dict(
                            q=q, ks=[(io["kT"][:, b, g, 0:n], 0)], lo=0, hi=n, masks=[(j * P, kit.tri[:, :])],
                            pts=[(i * P, P, io["v"][:, i, (b * NG + g) * HD:(b * NG + g + 1) * HD])
                                 for i in range(j + 1)],
                            out=out, bank=hp, start=False, stop=(b == 1), scale=1.0, gate=gate(1 + b), vis=None))
        at = Attention(st, items, [ps[:, i, :] for i in range(3)], [ps[:, 3 + i, :] for i in range(2)],
                       [ps[:, 6, :], ps[:, 7, :]], SEQ,
                       lambda dve, b, o: dve.tensor_copy(io["attnT"][:, b, :], o))
        with nc.Block() as block:

            @block.tensor
            def _(pe):
                at.on_pe(pe)

            @block.scalar
            def _(act):
                at.on_act(act)

            @block.vector
            def _(dve):
                at.on_dve(dve)


def nsa_out(kit, io):
    nc, t = kit.nc, kit.t
    with Stage(kit, "nsaout") as st:
        ps = st.banks()
        ring = WeightRing(st, "w", 4, D, pieces(t["b_w_o"], DT, D))
        lin = Linear(st, ring, one_bank_slots(ps, 0, 6),
                     [(("o", n), P, DT, lambda k: [io["attnT"][:, k, :]], None) for n in range(DT)])
        added = st.sem("added")
        with nc.Block() as block:

            @block.sync
            def _(sp):
                ring.load_all(sp, lin.done)

            @block.tensor
            def _(pe):
                lin.run(pe)

            @block.vector
            def _(dve):
                for n in range(DT):
                    slot, free = lin.arrived(dve, ("o", n))
                    dve.tensor_tensor(kit.real(n), kit.real(n), slot[:, 0, :], ALU.add).then_inc(added, 1)
                    dve.wait_ge(added, n + 1)
                    dve.nop().then_inc(free, 1)


def build_program(nc, t, out, dump=None, upto=99):
    with ExitStack() as ctx:
        kit = Kit(nc, t, ctx)

        def done(n):
            if dump is not None and upto == n:
                dump(kit)
                return True
            return False

        with ExitStack() as late:
            sb = lambda n, s, d=F32: late.enter_context(nc.sbuf_tensor(n, s, d))
            io = {"xn": sb("xn", [P, DT, SEQ]), "idxT": sb("idxT", [P, 2, SEQ]), "gT": sb("gT", [P, 2, SEQ]),
                  "g16": sb("g16", [P, SEQ], F16)}
            with ExitStack() as first:
                sb1 = lambda n, s, d=F32: first.enter_context(nc.sbuf_tensor(n, s, d))
                io["mixT"] = sb1("mixT", [P, 2 * CT, SEQ])
                with ExitStack() as qkv:
                    sb2 = lambda n, s, d=F32: qkv.enter_context(nc.sbuf_tensor(n, s, d))
                    io.update(qT=sb2("qT", [DQ, HEADS, SEQ]), kT=sb2("kT", [DQ, HEADS, T1]), v=sb2("v", [P, ST + 1, CC]))
                    front(kit, io)
                    kit.io = io
                    if done(1):
                        return
                    mla(kit, io)
                    if done(2):
                        return
                route(kit, io)
            if done(3):
                return
            experts(kit, io)
        if done(4):
            return
        short(kit)
        if done(5):
            return
        ffn(kit, 0)
        if done(6):
            return
        with ExitStack() as qkv:
            sb = lambda n, s, d=F32: qkv.enter_context(nc.sbuf_tensor(n, s, d))
            io = {"qT": sb("q2T", [HD + 2, NH, SEQ]), "kT": sb("k2T", [HD + 2, 2, NG, SEQ]),
                  "v": sb("v2", [P, ST, 2 * NG * HD]), "gate": sb("gate2", [P, ST, 3 * NH]),
                  "kc": sb("kc", [HD + 2, NG, NC]), "vc": sb("vc", [NC, NG * HD]), "vis": sb("vis", [P, 2, ST, NC])}
            nsa_in(kit, io)
            kit.io = io
            if done(7):
                return
            io["attnT"] = sb("attn2T", [P, DT, SEQ])
            nsa(kit, io)
            if done(8):
                return
            nsa_out(kit, io)
        if done(9):
            return
        ffn(kit, 1, final=out)


def constants():
    f = np.float32
    pos = np.arange(T1, dtype=f)
    freq = (f(10000.0) ** (-np.arange(ROPE // 2, dtype=f) / f(ROPE // 2))).astype(f)
    ang = (freq[:, None] * pos[None, :]).astype(f)
    cos, sin = np.cos(ang).astype(f), np.sin(ang).astype(f)
    slopes = np.exp2(-8.0 * np.arange(1, NH + 1) / NH).astype(f)
    tok = np.arange(SEQ, dtype=f)
    qrows = np.stack([np.stack([np.full(SEQ, s, f), -s * tok]) for s in slopes]).reshape(2 * NH, SEQ)
    centre = np.arange(NC, dtype=f) * DC + (LC - 1) / 2.0
    end = np.arange(NC) * DC + LC - 1
    see = (end[None, :] <= np.arange(SEQ)[:, None])
    vis = np.stack([np.where(see, 0.0, NEG), see.astype(f)]).astype(f).reshape(2, ST, P, NC).transpose(2, 0, 1, 3)
    return {
        "c_cos": np.tile(np.concatenate([cos, cos]), (4, 1)),
        "c_sin": np.tile(np.concatenate([-sin, sin]), (4, 1)),
        "c_ident": np.eye(P, dtype=f),
        "c_tri": np.where(np.arange(P)[None, :] <= np.arange(P)[:, None], 0.0, NEG).astype(f),
        "c_iota": np.tile(np.arange(P, dtype=f), (P, 1)),
        "c_qrows": qrows.astype(f),
        "c_krows": np.stack([tok, np.ones(SEQ, f)]),
        "c_crows": np.tile(np.stack([centre, np.ones(NC)]).astype(f), (1, NG)),
        "c_vis": vis.reshape(P, 2 * ST * NC),
    }


def tiles_of(w, m=P):
    k, n = w.shape
    return w.reshape(k // P, P, n // m, m).transpose(2, 1, 0, 3).reshape(n // m * P, k // P * m)


def lay_out(i):
    ht = np.concatenate([i["meta"], i["x"][0]], axis=0).T
    a = {"hT0": ht.reshape(DT, P, T1).transpose(1, 0, 2).reshape(P, DT * T1)}
    a["gains"] = np.concatenate([i[n].reshape(-1, P) for n, _ in GAINS], axis=0).T
    w = i["w_in"][0]
    ab = np.concatenate([np.concatenate([w[:, CC + c * P:CC + (c + 1) * P], w[:, c * P:(c + 1) * P]], axis=1)
                         for c in range(CT)], axis=1)
    c0 = 2 * CC
    a["w_ab"] = tiles_of(ab)
    a["w_cq"] = tiles_of(w[:, c0:c0 + QL])
    a["w_ckv"] = tiles_of(w[:, c0 + QL:c0 + QL + KVL])
    kr = w[:, c0 + QL + KVL:]
    a["w_krope"] = tiles_of(np.concatenate([kr, kr[:, ROPE // 2:], kr[:, :ROPE // 2]], axis=1), 2 * ROPE)
    uq = i["w_uq"][0].reshape(QL, HEADS, DQ)
    nope, rope = uq[:, :, :NOPE], uq[:, :, NOPE:]
    swap = np.concatenate([rope[:, :, ROPE // 2:], rope[:, :, :ROPE // 2]], axis=2)
    rope, swap = rope.reshape(QL, 2, P), swap.reshape(QL, 2, P)
    both = np.stack([rope, swap], axis=2).reshape(QL, 4 * P)
    a["w_uq"] = tiles_of(np.concatenate([nope.reshape(QL, HEADS * NOPE), both], axis=1))
    ukv = i["w_ukv"][0].reshape(KVL, HEADS, NOPE + VH)
    a["w_ukv"] = np.concatenate([ukv[:, :, :NOPE].reshape(KVL, -1), ukv[:, :, NOPE:].reshape(KVL, -1)], axis=1)
    a["w_out"] = tiles_of(i["w_out"][0])
    a["peer_wq"] = tiles_of(i["peer_wq"][0])
    a["peer_keys"] = i["peer_keys"][0].transpose(1, 3, 0, 2).reshape(P, PH * NK)
    a["peer_uT"] = i["peer_u"][0].reshape(CHUNKS, P, DT, P).transpose(0, 3, 2, 1).reshape(CHUNKS * P, D)
    a["peer_v"] = i["peer_v"][0]
    wi = i["a_w_in_2"][0]
    order = [wi[:, p * D + n * P:p * D + (n + 1) * P] for n in range(DT) for p in (1, 2, 0)]
    a["a_w_in"] = tiles_of(np.concatenate(order, axis=1))
    a["a_w_out"] = tiles_of(i["a_w_out_2"][0])
    gu = i["f_w_gu_2"]
    order = [gu[:, :, p * F + n * P:p * F + (n + 1) * P] for n in range(FT) for p in range(2)]
    gu = np.concatenate(order, axis=2)
    a["f_w_gu"] = np.concatenate([tiles_of(gu[0]), tiles_of(gu[1])], axis=0)
    a["f_w_down"] = np.concatenate([tiles_of(i["f_w_down_2"][0]), tiles_of(i["f_w_down_2"][1])], axis=0)
    kv = i["w_kv_2"].reshape(D, 6, NG * HD)
    a["w_kraw"] = tiles_of(np.concatenate([kv[:, s] for s in (0, 1, 2, 4)], axis=1))
    a["w_v2"] = np.concatenate([kv[:, 3], kv[:, 5]], axis=1).reshape(DT, P, -1).transpose(1, 0, 2).reshape(P, -1)
    qg = i["b_w_qg_2"][0]
    a["w_q2"] = tiles_of(qg[:, :NH * HD])
    a["w_gate2"] = qg[:, NH * HD:].reshape(DT, P, -1).transpose(1, 0, 2).reshape(P, -1)
    a["b_w_o"] = tiles_of(i["b_w_o_2"][0])
    w1 = np.stack([i["cmp_w1_k_2"], i["cmp_w1_v_2"]]).reshape(2, LC // 2, P, CH)
    a["cmp_w1"] = w1.transpose(0, 2, 1, 3).reshape(2 * P, LC // 2 * CH)
    w2 = np.stack([i["cmp_w2_k_2"], i["cmp_w2_v_2"]]).reshape(2, 2, P, HD)
    a["cmp_w2"] = w2.transpose(2, 0, 1, 3).reshape(P, 4 * HD)
    pe = np.stack([i["cmp_pe_k_2"], i["cmp_pe_v_2"]]).transpose(2, 0, 1)
    a["cmp_pe"] = np.concatenate([pe, np.roll(pe, -1, axis=2)], axis=0).reshape(P, 2 * LC)
    return a


def kernel(**inputs):
    import concourse.bacc as bacc
    from concourse.bass_utils import run_bass_kernel_spmd

    nc = bacc.Bacc("TRN2", target_bir_lowering=False, num_devices=1)
    laid = lay_out({k: np.asarray(v) for k, v in inputs.items()})
    laid.update(constants())
    arrays, aps = {}, {}
    for name, a in laid.items():
        a = np.ascontiguousarray(a)
        arrays[f"in_{name}"] = a
        aps[name] = nc.dram_tensor(f"in_{name}", a.shape, mybir.dt.from_np(a.dtype), kind="ExternalInput").ap()
    out = nc.dram_tensor("out_T", (D, SEQ), F32, kind="ExternalOutput").ap()
    build_program(nc, aps, out)
    r = run_bass_kernel_spmd(nc, [arrays], core_ids=[0])
    return np.ascontiguousarray(r.results[0]["out_T"].T)[None]
```

```python
from contextlib import ExitStack

import numpy as np

import concourse.bass as bass
from concourse import mybir

F32 = mybir.dt.float32
F32R = mybir.dt.float32r
F16 = mybir.dt.float16
U32 = mybir.dt.uint32
ALU = mybir.AluOpType
ACT = mybir.ActivationFunctionType
AX = mybir.AxisListType.X

P = 128
D = 1024
DT = D // P
SEQ = 512
NMETA = 16
T1 = SEQ + NMETA
HT = T1 // 2
ST = SEQ // P

HEADS = 8
NOPE = 64
ROPE = 32
VH = 64
DQ = NOPE + ROPE
QL = 256
KVL = 128
CC = 512
CT = CC // P
CK = 31
NK = 128
PH = 8
TOPK = 16
EPS1 = 1e-6

F = 2816
FT = F // P
NH = 16
NG = 4
HPG = NH // NG
HD = 64
LC = 32
DC = 16
NC = (SEQ - LC) // DC + 1
CH = 256
EPS2 = 1e-5
NEG = -1e30
GSCALE = 16384.0

GAINS = [("g_mix_norm", 8), ("g_q", 2), ("g_kv", 1), ("conv_b", 4), ("g_conv_ln", 4), ("b_conv_ln", 4),
         ("g_out_attn", 4), ("g_out_conv", 4), ("g_ffn_norm", 8), ("g_final", 8), ("conv_w", CK * CT),
         ("a_norm_2", 8), ("kv_norm_2", 8), ("b_norm_2", 8), ("f_norm_2", 16), ("final_norm_2", 8),
         ("a_conv_2", 24)]
GCOL = {}
_at = 0
for _name, _n in GAINS:
    GCOL[_name] = _at
    _at += _n
NGAIN = _at


class Count:

    def __init__(self, eng, sem):
        self.eng, self.sem, self.n = eng, sem, 0

    def step(self, ins):
        self.n += 1
        return ins.then_inc(self.sem, 1)

    def wait(self):
        self.eng.wait_ge(self.sem, self.n)

    def link(self, ins):
        self.step(ins)
        self.wait()


class Kit:

    def __init__(self, nc, t, ctx):
        self.nc, self.t, self.ctx = nc, t, ctx
        self.uid = 0
        sb = lambda n, s, d=F32: ctx.enter_context(nc.sbuf_tensor(n, s, d))
        self.hT = sb("hT", [P, DT, T1])
        self.gains = sb("gains", [P, NGAIN])
        self.ones = sb("ones", [P, P])
        self.ident = sb("ident", [P, P])
        self.tri = sb("tri", [P, P])
        self.loaded = ctx.enter_context(nc.semaphore("consts_loaded"))
        self.stored = ctx.enter_context(nc.semaphore("output_stored"))
        self.made = ctx.enter_context(nc.semaphore("ones_made"))

    def gain(self, name, j):
        c = GCOL[name] + j
        return self.gains[:, c:c + 1]

    def real(self, j):
        return self.hT[:, j, NMETA:T1]


class Stage:

    def __init__(self, kit, name):
        self.kit, self.nc, self.name = kit, kit.nc, name
        self.ctx = ExitStack()
        self.sems = []

    def __enter__(self):
        self.ctx.__enter__()
        return self

    def __exit__(self, kind, *a):
        if kind is None:
            self.nc.clear_and_free_semaphores(self.sems)
            self.nc.all_engine_barrier()
        return self.ctx.__exit__(kind, *a)

    def sb(self, name, shape, dt=F32):
        return self.ctx.enter_context(self.nc.sbuf_tensor(f"{self.name}_{name}", shape, dt))

    def banks(self, n=8):
        return self.ctx.enter_context(self.nc.psum_tensor(f"{self.name}_psum", [P, n, 512], F32))

    def sem(self, name):
        self.sems.append(self.nc.alloc_semaphore(f"{self.name}_{name}"))
        return self.sems[-1]


class WeightRing:

    def __init__(self, st, name, slots, cols, tiles):
        self.buf = st.sb(name, [P, slots, cols])
        self.n, self.tiles = slots, tiles
        self.into = [st.sem(f"{name}_in{i}") for i in range(slots)]

    def load_all(self, sp, done):
        for n, w in enumerate(self.tiles):
            if n >= self.n:
                sp.wait_ge(done, n - self.n + 1)
            sp.dma_start(self.buf[:, n % self.n, 0:w.shape[1]], w).then_inc(self.into[n % self.n], 16)

    def take(self, pe, n):
        pe.wait_ge(self.into[n % self.n], 16 * (n // self.n + 1))
        return self.buf[:, n % self.n, :]


class Linear:

    def __init__(self, st, ring, slots, tiles, name="lin"):
        self.ring, self.slots, self.tiles = ring, slots, tiles
        self.index = {t[0]: n for n, t in enumerate(tiles)}
        self.done = st.sem(f"{name}_done")
        self.free = [st.sem(f"{name}_free{i}") for i in range(len(slots))]

    def run(self, pe, only=None):
        for n, (key, m, kt, rhs, need) in enumerate(self.tiles):
            if only is not None and not only(n):
                continue
            if need is not None:
                pe.wait_ge(*need)
            w = self.ring.take(pe, n)
            s = n % len(self.slots)
            if n >= len(self.slots):
                pe.wait_ge(self.free[s], n // len(self.slots))
            for k in range(kt):
                for half, x in enumerate(rhs(k)):
                    mm = pe.matmul(self.slots[s][0:m, half, 0:x.shape[-1]], w[:, k * m:(k + 1) * m], x,
                                   start=(k == 0), stop=(k == kt - 1))
            mm.then_inc(self.done, 1)

    def arrived(self, eng, key):
        n = self.index[key]
        eng.wait_ge(self.done, n + 1)
        s = n % len(self.slots)
        return self.slots[s], self.free[s]


class SplitRing:

    def __init__(self, st, name, slots, cols, tiles, done):
        self.buf = st.sb(name, [P, slots, cols])
        self.hi = st.sb(f"{name}_hi", [P, 2, cols], F32R)
        self.lo = st.sb(f"{name}_lo", [P, 2, cols], F32R)
        self.n, self.tiles, self.done, self.n_rounded = slots, tiles, done, 0
        self.into = [st.sem(f"{name}_in{i}") for i in range(slots)]
        self.rounded = st.sem(f"{name}_rounded")
        self.split = st.sem(f"{name}_split")

    def load_all(self, sp):
        for n, w in enumerate(self.tiles):
            if n >= self.n:
                sp.wait_ge(self.split, n - self.n + 1)
            sp.dma_start(self.buf[:, n % self.n, 0:w.shape[1]], w).then_inc(self.into[n % self.n], 16)

    def round_to(self, act, m):
        for n in range(self.n_rounded, min(m, len(self.tiles))):
            c = self.tiles[n].shape[1]
            act.wait_ge(self.into[n % self.n], 16 * (n // self.n + 1))
            if n >= 2:
                act.wait_ge(self.done, n - 1)
            act.activation(self.hi[:, n % 2, 0:c], self.buf[:, n % self.n, 0:c], ACT.Copy).then_inc(self.rounded, 1)
        self.n_rounded = max(self.n_rounded, min(m, len(self.tiles)))

    def split_all(self, pool):
        for n, w in enumerate(self.tiles):
            c = w.shape[1]
            pool.wait_ge(self.rounded, n + 1)
            pool.tensor_tensor(self.lo[:, n % 2, 0:c], self.buf[:, n % self.n, 0:c],
                               self.hi[:, n % 2, 0:c].bitcast(F32), ALU.subtract).then_inc(self.split, 1)

    def take(self, pe, n):
        pe.wait_ge(self.split, n + 1)
        return self.hi[:, n % 2, :], self.lo[:, n % 2, :]


def product(pe, out, w, x, start, stop):
    pe.matmul(out, w[0], x[0], start=start, stop=False)
    pe.matmul(out, w[0], x[1], start=False, stop=False)
    return pe.matmul(out, w[1], x[0], start=False, stop=stop)


def tile(key, rhs=None, ks=DT, need=None, start=True, stop=True, by=None):
    start = start and by is None
    return dict(by=by, key=key, rhs=rhs, ks=range(ks) if isinstance(ks, int) else ks, need=need, start=start, stop=stop)


class SplitLinear:

    def __init__(self, st, slots, tiles, name="lin"):
        self.slots, self.tiles = slots, tiles
        self.index, self.place = {}, []
        s = -1
        for n, x in enumerate(tiles):
            s += x["start"]
            self.place.append(s)
            if x["stop"]:
                self.index[x["key"]] = n
        self.done = st.sem(f"{name}_done")
        self.free = [st.sem(f"{name}_free{i}") for i in range(len(slots))]
        self.uses = s + 1

    def run(self, pe, only=None):
        for n, x in enumerate(self.tiles):
            if only is not None and not only(n):
                continue
            whi, wlo = self.ring.take(pe, n)
            if x["by"] is not None:
                x["by"](pe, whi, wlo).then_inc(self.done, 1)
                continue
            use = self.place[n]
            s = use % len(self.slots)
            if x["start"] and use >= len(self.slots):
                pe.wait_ge(self.free[s], use // len(self.slots))
            for i, k in enumerate(x["ks"]):
                if x["need"] is not None:
                    pe.wait_ge(x["need"][0], x["need"][1](k))
                c = slice(i * P, (i + 1) * P)
                for half, pair in enumerate(x["rhs"](k)):
                    mm = product(pe, self.slots[s][:, half, 0:pair[0].shape[-1]], (whi[:, c], wlo[:, c]), pair,
                                 x["start"] and i == 0, x["stop"] and i == len(x["ks"]) - 1)
            mm.then_inc(self.done, 1)

    def all_free(self, pe):
        for s in range(len(self.slots)):
            pe.wait_ge(self.free[s], len([u for u in range(self.uses) if u % len(self.slots) == s]))

    def arrived(self, eng, key):
        n = self.index[key]
        eng.wait_ge(self.done, n + 1)
        s = self.place[n] % len(self.slots)
        return self.slots[s], self.free[s]


def rounding(lin, act, key):
    n = lin.index[key]
    lin.ring.round_to(act, n + 2)
    there = lin.arrived(act, key)
    lin.ring.round_to(act, n + 3)
    return there


def split_linear(st, slots, tiles, ring_slots, cols, weights):
    lin = SplitLinear(st, slots, tiles)
    lin.ring = SplitRing(st, "w", ring_slots, cols, weights, lin.done)
    return lin


class Split:

    def __init__(self, hi, lo):
        self.hi, self.lo = hi, lo

    def pair(self, *at):
        return self.hi[at], self.lo[at]

    def write_hi(self, dve, at, src):
        return dve.tensor_copy(self.hi[at], src)

    def write_lo(self, dve, at, src):
        return dve.tensor_tensor(self.lo[at], src, self.hi[at].bitcast(F32), ALU.subtract)

    def write_all(self, dve, own, src, n, there):
        for k in range(n + 1):
            if k:
                own.wait()
            if k < n:
                own.step(self.write_hi(dve, (slice(None), k), src[:, k, :]))
            if k:
                self.write_lo(dve, (slice(None), k - 1), src[:, k - 1, :]).then_inc(there, 1)


class Norm:

    def __init__(self, st, name, src, dst, n, width, eps, gain, ps, parts, need=None, bufs=None, split=None):
        self.kit = st.kit
        self.src, self.dst, self.n, self.eps, self.gain = src, dst, n, eps, gain
        self.ps, self.parts, self.need, self.dim, self.split = ps, parts, need, n * P, split
        self.width = width
        sq, rs, tmp = bufs or (st.sb(f"{name}_sq", [P, 2, width]), st.sb(f"{name}_rs", [P, width]), None)
        if split is not None and tmp is None:
            tmp = st.sb(f"{name}_tmp", [P, 3, width])
        self.bufs = (sq, rs, tmp)
        self.sq, self.rs = sq[:, :, 0:width], rs[:, 0:width]
        self.tmp = None if tmp is None else tmp[:, :, 0:width]
        self.squared = st.sem(f"{name}_squared")
        self.summed = st.sem(f"{name}_summed")
        self.var = st.sem(f"{name}_var")
        self.root = st.sem(f"{name}_root")
        self.out = st.sem(f"{name}_out")

    def cols(self, x):
        w = self.width // self.parts
        return [x[:, i * w:(i + 1) * w] for i in range(self.parts)]

    def halves(self, x):
        return x.rearrange("p (a b) -> p a b", a=self.parts)

    def on_act(self, act, meanwhile=None):
        for j in range(self.n):
            if self.need is not None:
                act.wait_ge(self.need[0], self.need[1](j))
            if j >= 2:
                act.wait_ge(self.summed, j - 1)
            act.activation(self.sq[:, j % 2, :], self.src(j), ACT.Square).then_inc(self.squared, 1)
        if meanwhile is not None:
            meanwhile()
        act.wait_ge(self.var, 1)
        act.activation(self.rs, self.rs, ACT.Sqrt).then_inc(self.root, 1)

    def on_pe(self, pe):
        for j in range(self.n):
            pe.wait_ge(self.squared, j + 1)
            for i, x in enumerate(self.cols(self.sq[:, j % 2, :])):
                mm = pe.matmul(self.ps[:, i, 0:x.shape[-1]], self.kit.ones[:, :], x,
                               start=(j == 0), stop=(j == self.n - 1))
            mm.then_inc(self.summed, 1)

    def on_dve(self, dve, own):
        w = self.width // self.parts
        dve.wait_ge(self.summed, self.n)
        dve.tensor_scalar(self.halves(self.rs), self.ps[:, 0:self.parts, 0:w], 1.0 / self.dim, self.eps,
                          ALU.mult, ALU.add).then_inc(self.var, 1)
        dve.wait_ge(self.root, 1)
        own.link(dve.reciprocal(self.rs, self.rs))
        self.scale(dve, own, self.src, self.gain, self.split, self.out)

    def scale(self, dve, own, src, gain, split, out):
        if split is None:
            for j in range(self.n):
                dve.scalar_tensor_tensor(out=self.dst(j), in0=src(j), scalar=gain(j), in1=self.rs,
                                         op0=ALU.mult, op1=ALU.mult).then_inc(out, 1)
            dve.wait_ge(out, self.n)
            return
        to, at = split
        for j in range(self.n + 2):
            if j < self.n:
                own.step(dve.scalar_tensor_tensor(out=self.tmp[:, j % 3, :], in0=src(j), scalar=gain(j),
                                                  in1=self.rs, op0=ALU.mult, op1=ALU.mult))
            if 0 <= j - 1 < self.n:
                own.step(to.write_hi(dve, at(j - 1), self.tmp[:, (j - 1) % 3, :]))
            if j >= 2:
                own.step(to.write_lo(dve, at(j - 2), self.tmp[:, (j - 2) % 3, :]))
            own.wait()
            if j >= 2:
                dve.nop().then_inc(out, 1)


def one_bank_slots(ps, first, n):
    return [ps[:, first + i:first + i + 1, :] for i in range(n)]


def two_bank_slots(ps, first, n):
    return [ps[:, first + 2 * i:first + 2 * i + 2, :] for i in range(n)]


def pieces(w, tiles, cols):
    return [w[n * P:(n + 1) * P, 0:cols] for n in range(tiles)]


def front(kit, out):
    nc, t = kit.nc, kit.t
    with Stage(kit, "front") as st:
        ps = st.banks()
        hn = out["hn"]
        conv_in = st.sb("conv_in", [P, CT, CK - 1 + T1])
        sig = st.sb("sig", [P, 2, T1])
        acc = out["mixT"][:, CT:2 * CT, :]
        cq = st.sb("cq", [P, 2, SEQ])
        cqn = Split(st.sb("cq_hi", [P, 2, SEQ], F32R), st.sb("cq_lo", [P, 2, SEQ], F32R))
        ckv = st.sb("ckv", [P, T1])
        cos = st.sb("cos", [P, T1])
        sin = st.sb("sin", [P, T1])
        wkv = st.sb("wkv", [P, HEADS * (NOPE + VH)])
        rot = st.sb("rot", [P, 2, T1])
        kr = st.sb("kr", [ROPE, T1])
        mu = st.sb("mu", [P, SEQ])
        side = st.sem("side_loaded")

        def halves(k):
            return [hn.pair(slice(None), k, slice(0, HT)), hn.pair(slice(None), k, slice(HT, T1))]

        mix = Norm(st, "mix", lambda j: kit.hT[:, j, :], None, DT, T1, EPS1,
                   lambda j: kit.gain("g_mix_norm", j), ps[:, 6:8, :], 2, need=(kit.loaded, lambda j: 16),
                   split=(hn, lambda j: (slice(None), j)))
        qn = Norm(st, "qn", lambda j: cq[:, j, :], None, 2, SEQ, EPS1,
                  lambda j: kit.gain("g_q", j), ps[:, 6:7, :], 1, need=(st.sem("cq_copied"), lambda j: j + 1),
                  bufs=mix.bufs, split=(cqn, lambda j: (slice(None), j)))
        kn = Norm(st, "kn", lambda j: ckv[:, :], lambda j: ckv[:, :], 1, T1, EPS1,
                  lambda j: kit.gain("g_kv", 0), ps[:, 6:8, :], 2, need=(st.sem("ckv_copied"), lambda j: 1),
                  bufs=mix.bufs)
        cq_copied, ckv_copied = qn.need[0], kn.need[0]

        tiles = []
        for c in range(CT):
            tiles.append(tile(("b", c), halves, need=(mix.out, lambda k: k + 1)))
            tiles.append(tile(("a", c), halves))
        tiles.append(tile(("ckv", 0), halves))
        tiles.append(tile(("krope", 0), halves))
        for c in range(2):
            tiles.append(tile(("cq", c), lambda k: [hn.pair(slice(None), k, slice(NMETA, T1))]))
        for c in range(8):
            tiles.append(tile(("q", c), lambda k: [cqn.pair(slice(None), k)], ks=2, need=(qn.out, lambda k: k + 1)))
        lin = split_linear(st, two_bank_slots(ps, 0, 3), tiles, 3, D,
                           pieces(t["w_ab"], 2 * CT, D) + pieces(t["w_ckv"], 1, D) + [t["w_krope"][:, :]]
                           + pieces(t["w_cq"], 2, D) + pieces(t["w_uq"], 8, 2 * P))
        n_before_q = lin.index[("q", 0)]

        gated = st.sem("gated")
        sig_done = st.sem("sig_done")
        padded = st.sem("padded")
        conv_done = st.sem("conv_done")
        kv_done = st.sem("kv_done")
        kv_free = st.sem("kv_free")
        ln_sum = st.sem("ln_sum")
        centred = st.sem("centred")
        silu_done = st.sem("silu_done")
        kr_done = st.sem("kr_done")
        kr_spread = st.sem("kr_spread")
        act_steps = st.sem("act_steps")

        ln = Norm(st, "ln", lambda j: acc[:, j, :], lambda j: acc[:, j, :], CT, SEQ, EPS1,
                  lambda j: 1.0, ps[:, 5:6, :], 1, need=(centred, lambda j: j + 1),
                  bufs=mix.bufs)
        cn = Norm(st, "cn", lambda j: acc[:, j, :], lambda j: acc[:, j, :], CT, SEQ, EPS1,
                  lambda j: kit.gain("g_out_conv", j), ps[:, 5:6, :], 1, need=(silu_done, lambda j: j + 1),
                  bufs=ln.bufs)

        with nc.Block() as block:

            @block.sync
            def _(sp):
                sp.dma_start(kit.hT[:, :, :], t["hT0"].rearrange("p (j n) -> p j n", j=DT)).then_inc(kit.loaded, 16)
                sp.dma_start(kit.gains[:, :], t["gains"]).then_inc(side, 16)
                sp.dma_start(kit.ident[:, :], t["c_ident"]).then_inc(side, 16)
                sp.dma_start(kit.tri[:, :], t["c_tri"]).then_inc(side, 16)
                sp.dma_start(cos[:, :], t["c_cos"]).then_inc(side, 16)
                sp.dma_start(sin[:, :], t["c_sin"]).then_inc(side, 16)
                sp.dma_start(wkv[:, :], t["w_ukv"]).then_inc(side, 16)
                lin.ring.load_all(sp)

            @block.tensor
            def _(pe):
                pe.wait_ge(kit.made, 1)
                mix.on_pe(pe)
                lin.run(pe, lambda n: n < n_before_q)
                pe.wait_ge(mix.var, 1)
                kn.on_pe(pe)
                pe.wait_ge(kn.var, 1)
                qn.on_pe(pe)
                lin.run(pe, lambda n: n >= n_before_q)
                pe.wait_ge(kn.out, 1)
                pe.wait_ge(side, 96)
                for s in range(3):
                    pe.wait_ge(lin.free[s], len([n for n in range(len(tiles)) if n % 3 == s]))
                for c in range(HEADS // 2):
                    if c >= 2:
                        pe.wait_ge(kv_free, c - 1)
                    for half in range(2):
                        mm = pe.matmul(ps[:, 2 * (c % 2) + half, 0:HT], wkv[:, c * P:(c + 1) * P],
                                       ckv[:, half * HT:(half + 1) * HT], start=True, stop=True)
                    mm.then_inc(kv_done, 1)
                pe.wait_ge(kv_free, HEADS // 2)
                for j in range(ST + 1):
                    if j >= 2:
                        pe.wait_ge(kv_free, HEADS // 2 + j - 1)
                    lo, m = (NMETA + j * P, P) if j < ST else (0, NMETA)
                    pe.matmul(ps[0:m, j % 2, 0:CC], ckv[:, lo:lo + m], wkv[:, HEADS * NOPE:],
                              start=True, stop=True).then_inc(kv_done, 1)
                pe.wait_ge(conv_done, 1)
                for c in range(CT):
                    mm = pe.matmul(ps[:, 4, :], kit.ones[:, :], acc[:, c, :], start=(c == 0), stop=(c == CT - 1))
                mm.then_inc(ln_sum, 1)
                ln.on_pe(pe)
                pe.wait_ge(ln.var, 1)
                cn.on_pe(pe)

            @block.scalar
            def _(act):
                act.wait_ge(side, 96)
                mix.on_act(act, lambda: lin.ring.round_to(act, 2))
                for c in range(CT):
                    slot, free = rounding(lin, act, ("b", c))
                    if c >= 2:
                        act.wait_ge(gated, c - 1)
                    act.activation(sig[:, c % 2, :].rearrange("p (a b) -> p a b", a=2), slot[:, :, 0:HT],
                                   ACT.Sigmoid).then_inc(sig_done, 1)
                    act.wait_ge(sig_done, c + 1)
                    act.nop().then_inc(free, 1)
                slot, free = rounding(lin, act, ("ckv", 0))
                act.activation(ckv[:, :].rearrange("p (a b) -> p a b", a=2), slot[:, :, 0:HT],
                               ACT.Copy).then_inc(ckv_copied, 1)
                act.wait_ge(ckv_copied, 1)
                act.nop().then_inc(free, 1)
                for c in range(2):
                    slot, free = rounding(lin, act, ("cq", c))
                    act.activation(cq[:, c, :], slot[:, 0, :], ACT.Copy).then_inc(cq_copied, 1)
                    act.wait_ge(cq_copied, c + 1)
                    act.nop().then_inc(free, 1)
                kn.on_act(act)
                qn.on_act(act)
                for c in range(4):
                    slot, free = rounding(lin, act, ("q", c))
                    for e in range(2):
                        act.activation(out["qT"][0:NOPE, 2 * c + e, :], slot[e * NOPE:(e + 1) * NOPE, 0, :],
                                       ACT.Copy).then_inc(act_steps, 1)
                    act.wait_ge(act_steps, 2 * (c + 1))
                    act.nop().then_inc(free, 1)
                lin.ring.round_to(act, len(tiles))
                for c in range(HEADS // 2):
                    act.wait_ge(kv_done, c + 1)
                    for e in range(2):
                        act.activation(out["kT"][0:NOPE, 2 * c + e, :].rearrange("p (a b) -> p a b", a=2),
                                       ps[e * NOPE:(e + 1) * NOPE, 2 * (c % 2):2 * (c % 2) + 2, 0:HT],
                                       ACT.Copy).then_inc(act_steps, 1)
                    act.wait_ge(act_steps, 8 + 2 * (c + 1))
                    act.nop().then_inc(kv_free, 1)
                for j in range(ST + 1):
                    act.wait_ge(kv_done, HEADS // 2 + j + 1)
                    m = P if j < ST else NMETA
                    act.activation(out["v"][0:m, j, :], ps[0:m, j % 2, :], ACT.Copy).then_inc(kv_free, 1)
                act.wait_ge(kr_done, 1)
                for h in range(HEADS):
                    act.activation(out["kT"][NOPE:DQ, h, :], kr[:, :], ACT.Copy).then_inc(kr_spread, 1)
                ln.on_act(act)
                for c in range(CT):
                    act.wait_ge(ln.out, c + 1)
                    act.activation(acc[:, c, :], acc[:, c, :], ACT.Silu, bias=kit.gain("b_conv_ln", c),
                                   scale=kit.gain("g_conv_ln", c)).then_inc(silu_done, 1)
                cn.on_act(act)

            @block.gpsimd
            def _(pool):
                pool.memset(kit.ones[:, :], 1.0).then_inc(kit.made, 1)
                pool.memset(conv_in[:, :, 0:CK - 1], 0.0).then_inc(padded, 1)
                lin.ring.split_all(pool)

            own_sem = st.sem("vector_steps")

            @block.vector
            def _(dve):
                own = Count(dve, own_sem)
                dve.wait_ge(side, 96)
                mix.on_dve(dve, own)
                taps = [0] * CT
                last_tap = [0] * CT

                def conv(m, there):
                    for _ in range(m):
                        left = [c for c in range(there) if taps[c] < CK]
                        if not left:
                            return
                        c = left[sum(taps) % len(left)]
                        k = taps[c]
                        src = conv_in[:, c, NMETA + k:NMETA + k + SEQ]
                        w = kit.gain("conv_w", k * CT + c)
                        if k:
                            dve.wait_ge(own.sem, last_tap[c])
                            ins = dve.scalar_tensor_tensor(out=acc[:, c, :], in0=src, scalar=w, in1=acc[:, c, :],
                                                           op0=ALU.mult, op1=ALU.add)
                        else:
                            ins = dve.tensor_scalar(acc[:, c, :], src, w, kit.gain("conv_b", c), ALU.mult, ALU.add)
                        own.step(ins)
                        taps[c], last_tap[c] = k + 1, own.n

                dve.wait_ge(padded, 1)
                for c in range(CT):
                    slot, free = lin.arrived(dve, ("a", c))
                    dve.wait_ge(sig_done, c + 1)
                    dve.tensor_tensor(conv_in[:, c, CK - 1:].rearrange("p (a b) -> p a b", a=2), slot[:, :, 0:HT],
                                      sig[:, c % 2, :].rearrange("p (a b) -> p a b", a=2), ALU.mult).then_inc(gated, 1)
                    dve.wait_ge(gated, c + 1)
                    dve.nop().then_inc(free, 1)
                    conv(11, c + 1)
                slot, free = lin.arrived(dve, ("krope", 0))
                for e, tab in enumerate((cos, sin)):
                    own.step(dve.tensor_tensor(
                        rot[0:ROPE, e, :].rearrange("p (a b) -> p a b", a=2), slot[e * ROPE:(e + 1) * ROPE, :, 0:HT],
                        tab[0:ROPE, :].rearrange("p (a b) -> p a b", a=2), ALU.mult))
                own.wait()
                dve.nop().then_inc(free, 1)
                own.step(dve.tensor_tensor(kr[:, :], rot[0:ROPE, 0, :], rot[0:ROPE, 1, :], ALU.add))
                own.wait()
                dve.nop().then_inc(kr_done, 1)
                conv(22, CT)
                kn.on_dve(dve, own)
                qn.on_dve(dve, own)
                for c in range(2):
                    for e, tab in enumerate((cos, sin)):
                        slot, free = lin.arrived(dve, ("q", 4 + 2 * c + e))
                        own.link(dve.tensor_tensor(rot[:, e, 0:SEQ], slot[:, 0, :], tab[:, NMETA:T1], ALU.mult))
                        dve.nop().then_inc(free, 1)
                    for a in range(4):
                        own.step(dve.tensor_tensor(out["qT"][NOPE:DQ, 4 * c + a, :], rot[a * ROPE:(a + 1) * ROPE, 0, 0:SEQ],
                                                   rot[a * ROPE:(a + 1) * ROPE, 1, 0:SEQ], ALU.add))
                    own.wait()
                conv(CK * CT, CT)
                own.wait()
                dve.nop().then_inc(conv_done, 1)
                dve.wait_ge(ln_sum, 1)
                own.link(dve.tensor_scalar(mu[:, :], ps[:, 4, :], 1.0 / CC, None, ALU.mult))
                for c in range(CT):
                    dve.tensor_tensor(acc[:, c, :], acc[:, c, :], mu[:, :], ALU.subtract).then_inc(centred, 1)
                dve.wait_ge(centred, CT)
                ln.on_dve(dve, own)
                cn.on_dve(dve, own)


class Attention:

    def __init__(self, st, items, s_slots, pt_slots, o_slots, pcols, flush):
        self.items, self.st = items, st
        self.ident = st.kit.ident
        self.S, self.PT, self.O, self.flush = s_slots, pt_slots, o_slots, flush
        self.pr = st.sb("probs", [P, 4, pcols])
        self.pts = st.sb("probsT", [P, 3, pt_slots[0].shape[-1]])
        n = len(items)
        self.mx = st.sb("mx", [P, 4])
        self.nm = st.sb("nm", [P, 4])
        self.ls = st.sb("ls", [P, 4])
        self.rl = st.sb("rl", [P, 4])
        names = ("scored", "maxed", "exped", "scaled", "turned", "copied", "summed", "flushed", "steps", "extra")
        self.s = {k: st.sem(k) for k in names}
        self.last = {}
        for i, it in enumerate(items):
            self.last[it["bank"]] = i

    def on_pe(self, pe):
        it, s, n_items = self.items, self.s, len(self.items)
        for n in range(n_items + 3):
            if n < n_items:
                x = it[n]
                if n >= len(self.S):
                    pe.wait_ge(s["exped"], n - len(self.S) + 1)
                for keys, col in x["ks"]:
                    mm = pe.matmul(self.S[n % len(self.S)][:, col:col + keys.shape[-1]], x["q"], keys,
                                   start=True, stop=True)
                mm.then_inc(s["scored"], 1)
            if 2 <= n <= n_items + 1:
                m = n - 2
                x = it[m]
                pe.wait_ge(s["scaled"], m + 1)
                if m >= len(self.PT):
                    pe.wait_ge(s["copied"], m - len(self.PT) + 1)
                pr = self.pr[:, m % 4, :]
                for j, (col, w, _) in enumerate(x["pts"]):
                    mm = pe.transpose(self.PT[m % len(self.PT)][0:w, j * P:(j + 1) * P], pr[:, col:col + w],
                                      self.ident[:, :])
                mm.then_inc(s["turned"], 1)
            if n >= 3:
                m = n - 3
                x = it[m]
                pe.wait_ge(s["copied"], m + 1)
                b = x["bank"]
                if b >= len(self.O) and (m == 0 or it[m - 1]["bank"] != b):
                    pe.wait_ge(s["flushed"], b - len(self.O) + 1)
                pt = self.pts[:, m % 3, :]
                for j, (_, w, v) in enumerate(x["pts"]):
                    mm = pe.matmul(x["out"](self.O[b % len(self.O)]), v, pt[0:w, j * P:(j + 1) * P],
                                   start=(x["start"] and j == 0), stop=(x["stop"] and j == len(x["pts"]) - 1))
                mm.then_inc(s["summed"], 1)

    def on_act(self, act):
        it, s, n_items = self.items, self.s, len(self.items)
        for n in range(n_items + 2):
            if n < n_items:
                x = it[n]
                act.wait_ge(s["maxed"], n + 1)
                if n >= 4:
                    act.wait_ge(s["turned"], n - 3)
                act.activation(self.pr[:, n % 4, 0:x["hi"] - x["lo"]], self.S[n % len(self.S)][:, x["lo"]:x["hi"]],
                               ACT.Exp, bias=self.nm[:, n % 4:n % 4 + 1], scale=x["scale"],
                               accum_out=self.ls[:, n % 4:n % 4 + 1]).then_inc(s["exped"], 1)
            if n >= 2:
                m = n - 2
                x = it[m]
                act.wait_ge(s["turned"], m + 1)
                if m >= 3:
                    act.wait_ge(s["summed"], m - 2)
                runs = []
                for j, (_, w, _) in enumerate(x["pts"]):
                    if runs and runs[-1][2] == w:
                        runs[-1][1] = j + 1
                    else:
                        runs.append([j, j + 1, w])
                for i, (a, b, w) in enumerate(runs):
                    c = act.activation(self.pts[0:w, m % 3, a * P:b * P],
                                       self.PT[m % len(self.PT)][0:w, a * P:b * P], ACT.Copy)
                    if i < len(runs) - 1:
                        c.then_inc(s["extra"], 1)
                        self.extra = self.extra + 1
                        act.wait_ge(s["extra"], self.extra)
                c.then_inc(s["copied"], 1)

    extra = 0

    def on_dve(self, dve):
        it, s, n_items = self.items, self.s, len(self.items)
        own = Count(dve, s["steps"])
        for n in range(n_items + 5):
            if n < n_items:
                x = it[n]
                S = self.S[n % len(self.S)]
                c = slice(n % 4, n % 4 + 1)
                dve.wait_ge(s["scored"], n + 1)
                for col, m in x["masks"]:
                    own.link(dve.tensor_tensor(S[:, col:col + m.shape[-1]], S[:, col:col + m.shape[-1]], m, ALU.add))
                own.link(dve.tensor_reduce(self.mx[:, c], S[:, x["lo"]:x["hi"]], AX, ALU.max))
                dve.tensor_scalar(self.nm[:, c], self.mx[:, c], -x["scale"], None, ALU.mult).then_inc(s["maxed"], 1)
            if 1 <= n <= n_items:
                x = it[n - 1]
                c = slice((n - 1) % 4, (n - 1) % 4 + 1)
                dve.wait_ge(s["exped"], n)
                own.link(dve.reciprocal(self.rl[:, c], self.ls[:, c]))
                pr = self.pr[:, (n - 1) % 4, 0:x["hi"] - x["lo"]]
                if x["gate"] is None:
                    ins = dve.tensor_scalar(pr, pr, self.rl[:, c], None, ALU.mult)
                else:
                    ins = dve.tensor_scalar(pr, pr, self.rl[:, c], x["gate"], ALU.mult, ALU.mult)
                if x["vis"] is not None:
                    own.link(ins)
                    ins = dve.tensor_tensor(pr, pr, x["vis"], ALU.mult)
                ins.then_inc(s["scaled"], 1)
            for b, i in self.last.items():
                if i + 4 == n:
                    dve.wait_ge(s["summed"], i + 1)
                    self.flush(dve, b, self.O[b % len(self.O)]).then_inc(s["flushed"], 1)


def mla(kit, io):
    nc = kit.nc
    with Stage(kit, "mla") as st:
        ps = st.banks()
        flat = ps[:, :, :].rearrange("p b n -> p (b n)")
        attn = st.sb("attnT", [P, CT, SEQ])
        items = []
        off = 512 - NMETA
        for hp in range(HEADS // 2):
            for h in (2 * hp, 2 * hp + 1):
                for j in range(ST):
                    keys = (j + 1) * P
                    items.append(dict(
                        q=io["qT"][:, h, j * P:(j + 1) * P],
                        ks=[(io["kT"][:, h, 0:NMETA], off), (io["kT"][:, h, NMETA:NMETA + keys], 512)],
                        lo=off, hi=512 + keys, masks=[(512 + j * P, kit.tri[:, :])],
                        pts=[(NMETA + i * P, P, io["v"][:, i, h * VH:(h + 1) * VH]) for i in range(j + 1)]
                        + [(0, NMETA, io["v"][0:NMETA, ST, h * VH:(h + 1) * VH])],
                        out=lambda o, e=h % 2, j=j: o[e * VH:(e + 1) * VH, j * P:(j + 1) * P],
                        bank=hp, start=True, stop=True, scale=DQ ** -0.5, gate=None, vis=None))
        at = Attention(st, items, [flat[:, 0:1024], flat[:, 1024:2048]], [flat[:, 2048:2048 + 640]],
                       [ps[:, 6, :], ps[:, 7, :]], T1,
                       lambda dve, b, o: dve.tensor_copy(attn[:, b, :], o))
        an = Norm(st, "an", lambda j: attn[:, j, :], lambda j: io["mixT"][:, j, :], CT, SEQ, EPS1,
                  lambda j: kit.gain("g_out_attn", j), ps[:, 0:1, :], 1, need=(at.s["flushed"], lambda j: j + 1))
        own_sem = st.sem("vector_steps")
        with nc.Block() as block:

            @block.tensor
            def _(pe):
                at.on_pe(pe)
                an.on_pe(pe)

            @block.scalar
            def _(act):
                at.on_act(act)
                an.on_act(act)

            @block.vector
            def _(dve):
                at.on_dve(dve)
                an.on_dve(dve, Count(dve, own_sem))


def route(kit, io):
    nc, t = kit.nc, kit.t
    NS = 2 * PH
    with Stage(kit, "route") as st:
        ps = st.banks()
        keys = st.sb("keys", [P, PH, NK])
        qT = st.sb("qT", [P, PH, SEQ])
        sc = st.sb("scores", [P, NS, NK])
        rest = st.sb("rest", [P, NS, NK])
        sv = st.sb("sv", [P, PH, 2, TOPK])
        si = st.sb("si", [P, NS, TOPK], U32)
        sif = st.sb("sif", [P, PH, 2, TOPK])
        cand = st.sb("cand", [P, PH, TOPK * TOPK])
        left = rest[:, :, :].rearrange("p (h a) n -> p h (a n)", a=2)
        tops = st.sb("tops", [P, PH, TOPK])
        sel = st.sb("sel", [P, PH, TOPK], U32)
        ab = st.sb("ab", [P, 2, PH * TOPK], U32)
        abf = st.sb("abf", [P, 2, PH * TOPK])
        eq = st.sb("eq", [P, PH, TOPK, TOPK])
        three = st.sb("three", [P, 3, PH * TOPK])
        tot = st.sb("tot", [P, PH])
        i16 = st.sb("i16", [P, TOPK])
        mix = Split(st.sb("mix_hi", [P, 2 * CT, SEQ], F32R), st.sb("mix_lo", [P, 2 * CT, SEQ], F32R))
        mix_split = st.sem("mix_split")
        side = st.sem("side_loaded")
        hsum = st.sem("residual_added")
        q_copied = st.sem("q_copied")
        scored = st.sem("scored")
        s_copied = st.sem("s_copied")
        s_used = st.sem("s_used")
        shifted = st.sem("shifted")
        exped = st.sem("exped")
        ready = st.sem("gates_ready")
        turned = st.sem("turned")
        own_sem = st.sem("vector_steps")
        fin_sem = st.sem("turned_copied")

        fn = Norm(st, "fn", lambda j: kit.real(j), None, DT, SEQ, EPS1,
                  lambda j: kit.gain("g_ffn_norm", j), ps[:, 4:5, :], 1, need=(hsum, lambda j: j + 1),
                  split=(io["xn"], lambda j: (slice(None), j)))
        tiles = [tile(("o", n), lambda k: [mix.pair(slice(None), k)], need=(mix_split, lambda k: k + 1)) for n in range(DT)]
        tiles += [tile(("q", n), lambda k: [io["xn"].pair(slice(None), k)], need=(fn.out, lambda k: k + 1))
                  for n in range(DT)]
        lin = split_linear(st, one_bank_slots(ps, 0, 4), tiles, 3, D,
                           pieces(t["w_out"], DT, D) + pieces(t["peer_wq"], DT, D))
        with nc.Block() as block:

            @block.sync
            def _(sp):
                sp.dma_start(keys[:, :, :], t["peer_keys"].rearrange("p (h n) -> p h n", h=PH)).then_inc(side, 16)
                sp.dma_start(i16[:, :], t["c_iota"]).then_inc(side, 16)
                lin.ring.load_all(sp)

            @block.gpsimd
            def _(pool):
                lin.ring.split_all(pool)

            @block.tensor
            def _(pe):
                lin.run(pe, lambda n: n < DT)
                fn.on_pe(pe)
                lin.run(pe, lambda n: n >= DT)
                pe.wait_ge(side, 32)
                pe.wait_ge(q_copied, DT)
                for j in range(ST):
                    if j:
                        pe.wait_ge(s_copied, 4 * j)
                    for h in range(PH):
                        for half in range(2):
                            lo = half * (P // 2)
                            bank = 2 * half + h // 4
                            mm = pe.matmul(ps[:, bank, (h % 4) * NK:(h % 4 + 1) * NK],
                                           qT[lo:lo + P // 2, h, j * P:(j + 1) * P], keys[lo:lo + P // 2, h, :],
                                           start=True, stop=True)
                    mm.then_inc(scored, 1)
                    pe.wait_ge(ready, j + 1)
                    for i in range(3):
                        mm = pe.transpose(ps[:, 5 + i, j * P:(j + 1) * P], three[:, i, :], kit.ident[:, :])
                    mm.then_inc(turned, 1)

            @block.scalar
            def _(act):
                lin.ring.round_to(act, DT)
                fn.on_act(act, lambda: lin.ring.round_to(act, DT + 2))
                for n in range(DT):
                    slot, free = rounding(lin, act, ("q", n))
                    act.activation(qT[:, n, :], slot[:, 0, :], ACT.Copy).then_inc(q_copied, 1)
                    act.wait_ge(q_copied, n + 1)
                    act.nop().then_inc(free, 1)
                for j in range(ST):
                    act.wait_ge(scored, j + 1)
                    if j:
                        act.wait_ge(s_used, j)
                    for bank in range(4):
                        half, h0 = bank // 2, 4 * (bank % 2)
                        act.activation(sc[:, :, :].rearrange("p (h a) n -> p h a n", a=2)[:, h0:h0 + 4, half, :],
                                       ps[:, bank, :].rearrange("p (h n) -> p h n", h=4), ACT.Copy)\
                            .then_inc(s_copied, 1)
                    act.wait_ge(shifted, j + 1)
                    act.activation(tops[:, :, :], tops[:, :, :], ACT.Exp).then_inc(exped, 1)

            @block.vector
            def _(dve):
                own = Count(dve, own_sem)
                mix.write_all(dve, own, io["mixT"], DT, mix_split)
                for n in range(DT):
                    slot, free = lin.arrived(dve, ("o", n))
                    dve.tensor_tensor(kit.real(n), kit.real(n), slot[:, 0, :], ALU.add).then_inc(hsum, 1)
                    dve.wait_ge(hsum, n + 1)
                    dve.nop().then_inc(free, 1)
                fn.on_dve(dve, own)
                dve.wait_ge(side, 32)
                svf = sv[:, :, :, :].rearrange("p h a k -> p (h a) k")
                for j in range(ST):
                    dve.wait_ge(s_copied, 4 * (j + 1))
                    for i in range(NS):
                        own.step(dve.max(svf[:, i, 0:8], sc[:, i, :]))
                    own.wait()
                    for i in range(NS):
                        own.step(dve.max_index(si[:, i, 0:8], svf[:, i, 0:8], sc[:, i, :]))
                        own.step(dve.match_replace(rest[:, i, :], svf[:, i, 0:8], sc[:, i, :], -3e38))
                    own.wait()
                    dve.nop().then_inc(s_used, 1)
                    for i in range(NS):
                        own.step(dve.max(svf[:, i, 8:16], rest[:, i, :]))
                    own.wait()
                    for i in range(NS):
                        own.step(dve.max_index(si[:, i, 8:16], svf[:, i, 8:16], rest[:, i, :]))
                    own.wait()
                    own.step(dve.tensor_copy(sif[:, :, :, :].rearrange("p h a k -> p (h a) k"), si[:, :, :]))
                    for h in range(PH):
                        own.step(dve.tensor_tensor(
                            cand[:, h, :].rearrange("p (a b) -> p a b", a=TOPK),
                            sv[:, h, 0, :].unsqueeze(2).to_broadcast([P, TOPK, TOPK]),
                            sv[:, h, 1, :].unsqueeze(1).to_broadcast([P, TOPK, TOPK]), ALU.add))
                    own.wait()
                    for h in range(PH):
                        own.step(dve.max(tops[:, h, 0:8], cand[:, h, :]))
                    own.wait()
                    for h in range(PH):
                        own.step(dve.max_index(sel[:, h, 0:8], tops[:, h, 0:8], cand[:, h, :]))
                        own.step(dve.match_replace(left[:, h, :], tops[:, h, 0:8], cand[:, h, :], -3e38))
                    own.wait()
                    for h in range(PH):
                        own.step(dve.max(tops[:, h, 8:16], left[:, h, :]))
                    own.wait()
                    for h in range(PH):
                        own.step(dve.max_index(sel[:, h, 8:16], tops[:, h, 8:16], left[:, h, :]))
                    own.step(dve.tensor_copy(tot[:, :], tops[:, :, 0]))
                    own.wait()
                    dve.tensor_tensor(tops[:, :, :], tops[:, :, :], tot[:, :].unsqueeze(2).to_broadcast([P, PH, TOPK]),
                                      ALU.subtract).then_inc(shifted, 1)
                    self_ = sel[:, :, :].rearrange("p h k -> p (h k)")
                    own.step(dve.tensor_scalar(ab[:, 0, :], self_, 4, None, ALU.logical_shift_right))
                    own.step(dve.tensor_scalar(ab[:, 1, :], self_, 15, None, ALU.bitwise_and))
                    own.wait()
                    own.link(dve.tensor_copy(abf[:, :, :], ab[:, :, :]))
                    if j:
                        dve.wait_ge(turned, j)
                    for i in range(2):
                        own.link(dve.tensor_tensor(
                            eq[:, :, :, :].rearrange("p h k a -> p (h k) a"),
                            abf[:, i, :].unsqueeze(2).to_broadcast([P, PH * TOPK, TOPK]),
                            i16[:, :].unsqueeze(1).to_broadcast([P, PH * TOPK, TOPK]), ALU.is_equal))
                        for h in range(PH):
                            own.step(dve.tensor_tensor(
                                eq[:, h, :, :], eq[:, h, :, :],
                                sif[:, h, i, :].unsqueeze(1).to_broadcast([P, TOPK, TOPK]), ALU.mult))
                        own.wait()
                        own.link(dve.tensor_reduce(three[:, i, :], eq[:, :, :, :].rearrange("p h k a -> p (h k) a"),
                                                   AX, ALU.add))
                    dve.wait_ge(exped, j + 1)
                    own.link(dve.tensor_reduce(tot[:, :], tops[:, :, :], AX, ALU.add))
                    own.link(dve.reciprocal(tot[:, :], tot[:, :]))
                    dve.scalar_tensor_tensor(
                        out=three[:, 2, :].rearrange("p (h k) -> p h k", h=PH), in0=tops[:, :, :], scalar=GSCALE,
                        in1=tot[:, :].unsqueeze(2).to_broadcast([P, PH, TOPK]), op0=ALU.mult, op1=ALU.mult)\
                        .then_inc(ready, 1)
                    dve.wait_ge(ready, j + 1)
                dve.wait_ge(turned, ST)
                for i in range(2):
                    own.step(dve.tensor_copy(io["idx"][:, i, :], ps[:, 5 + i, :]))
                own.link(dve.tensor_copy(io["gate"][:, 0, :], ps[:, 7, :]))
                own.link(dve.tensor_tensor(io["gate"][:, 1, :], ps[:, 7, :], io["gate"][:, 0, :], ALU.subtract))


CHUNKS = NK
PARTS = 4
PCH = CHUNKS // PARTS
TB = SEQ // PCH
GRP = 2


def experts(kit, io):
    nc, t = kit.nc, kit.t
    with Stage(kit, "experts") as st:
        ps = st.banks()
        xn, idx, gate = io["xn"], io["idx"], io["gate"]
        G = st.sb("gates", [P, PCH * SEQ])
        U = st.sb("u", [P, D])
        Us = Split(st.sb("u_hi", [P, 2, D], F32R), st.sb("u_lo", [P, 2, D], F32R))
        V = st.sb("v", [P, D])
        VS = 3
        Vs = Split(st.sb("v_hi", [P, VS, D], F32R), st.sb("v_lo", [P, VS, D], F32R))
        W = st.sb("w", [P, 2, SEQ])
        WS = 2 * GRP
        Ws = Split(st.sb("w_hi", [P, WS, SEQ], F32R), st.sb("w_lo", [P, WS, SEQ], F32R))
        O2 = st.sb("second_hot", [P, 2, NK, TB], F16)
        O1 = st.sb("first_hot", [P, 2, 2, PCH, TB], F16)
        E1 = st.sb("first_eq", [P, PCH, TB], F16)
        iota = st.sb("iota", [P, NK, TB], F16)
        side = st.sem("side_loaded")
        u_in, v_in = st.sem("u_in"), st.sem("v_in")
        u_hi, u_lo = st.sem("u_rounded"), st.sem("u_split")
        v_hi, v_lo = st.sem("v_rounded"), st.sem("v_split")
        acted = st.sem("first_done")
        gelued = st.sem("gelued")
        weighed = st.sem("weighed")
        w_hi, w_lo = st.sem("w_rounded"), st.sem("w_split")
        hot = st.sem("hot_made")
        gated = st.sem("gates_summed")
        gcopied = st.sem("gates_copied")
        odone = st.sem("second_done")
        oadded = st.sem("second_added")
        own_sem = st.sem("vector_steps")
        groups = CHUNKS // GRP

        def region(par, n):
            if par == 0:
                return G[:, n * SEQ:(n + 1) * SEQ].rearrange("p (s t) -> p s t", s=PCH)
            return G[:, :].rearrange("p (s n t) -> p s n t", s=PCH, n=PCH)[:, :, n, :]

        with nc.Block() as block:

            @block.sync
            def _(sp):
                sp.dma_start(iota[:, :, :], t["c_iota16"].rearrange("p (k t) -> p k t", t=TB)).then_inc(side, 16)
                for n in range(CHUNKS):
                    if n:
                        sp.wait_ge(u_lo, n)
                    sp.dma_start(U[:, :], t["peer_uT"][n * P:(n + 1) * P, :]).then_inc(u_in, 16)

            def gate_block(pe, b):
                pe.wait_ge(hot, b + 1)
                if b >= 2:
                    pe.wait_ge(gcopied, b - 1)
                for i in range(TB):
                    for piece in range(2):
                        mm = pe.matmul(ps[:, 6 + b % 2, i * PCH:(i + 1) * PCH], O2[:, b % 2, :, i],
                                       O1[:, b % 2, piece, :, i], start=(piece == 0), stop=(piece == 1))
                mm.then_inc(gated, 1)

            @block.tensor
            def _(pe):
                for b in range(PCH):
                    gate_block(pe, b)
                for g in range(groups + 1):
                    if g < groups:
                        for c in range(GRP):
                            n = g * GRP + c
                            pe.wait_ge(u_lo, n + 1)
                            if n >= 3:
                                pe.wait_ge(gelued, n - 2)
                            for k in range(DT):
                                mm = product(pe, ps[:, n % 3, :], Us.pair(slice(None), n % 2, slice(k * P, (k + 1) * P)),
                                             xn.pair(slice(None), k), k == 0, k == DT - 1)
                            mm.then_inc(acted, 1)
                            if n < CHUNKS - PCH:
                                gate_block(pe, PCH + n)
                    if g >= 1:
                        q = g - 1
                        pe.wait_ge(v_lo, GRP * g)
                        pe.wait_ge(w_lo, GRP * g)
                        for d in range(DT):
                            m = q * DT + d
                            if m >= 3:
                                pe.wait_ge(oadded, m - 2)
                            for c in range(GRP):
                                n = q * GRP + c
                                mm = product(pe, ps[:, 3 + m % 3, :],
                                             Vs.pair(slice(None), n % VS, slice(d * P, (d + 1) * P)),
                                             Ws.pair(slice(None), n % WS), c == 0, c == GRP - 1)
                            mm.then_inc(odone, 1)

            @block.gpsimd
            def _(pool):
                for n in range(-1, CHUNKS + 1):
                    if n + 1 < CHUNKS:
                        pool.wait_ge(u_hi, n + 2)
                        at = (slice(None), (n + 1) % 2)
                        pool.tensor_tensor(Us.lo[at], U[:, :], Us.hi[at].bitcast(F32), ALU.subtract).then_inc(u_lo, 1)
                    if n >= 1:
                        pool.wait_ge(v_hi, n)
                        at = (slice(None), (n - 1) % VS)
                        pool.tensor_tensor(Vs.lo[at], V[:, :], Vs.hi[at].bitcast(F32), ALU.subtract).then_inc(v_lo, 1)

            @block.scalar
            def _(act):
                def round_u(n):
                    act.wait_ge(u_in, 16 * (n + 1))
                    if n >= 2:
                        act.wait_ge(acted, n - 1)
                    act.activation(Us.hi[:, n % 2, :], U[:, :], ACT.Copy).then_inc(u_hi, 1)

                def load_v(n):
                    if n:
                        act.wait_ge(v_lo, n)
                    act.dma_start(V[:, :], t["peer_v"][n * P:(n + 1) * P, :]).then_inc(v_in, 16)

                def round_v(n):
                    act.wait_ge(v_in, 16 * (n + 1))
                    if n >= VS:
                        act.wait_ge(odone, DT * ((n - VS) // GRP + 1))
                    act.activation(Vs.hi[:, n % VS, :], V[:, :], ACT.Copy).then_inc(v_hi, 1)

                def keep(b, par):
                    act.wait_ge(gated, b + 1)
                    act.activation(region(par, b % PCH), ps[:, 6 + b % 2, :].rearrange("p (t i) -> p i t", i=PCH),
                                   ACT.Copy).then_inc(gcopied, 1)

                round_u(0)
                for b in range(PCH):
                    keep(b, 1)
                for n in range(CHUNKS + 1):
                    if n >= 1:
                        load_v(n - 1)
                    if n + 1 < CHUNKS:
                        round_u(n + 1)
                    if n < CHUNKS:
                        act.wait_ge(acted, n + 1)
                        if n >= 2:
                            act.wait_ge(w_lo, n - 1)
                        act.activation(W[:, n % 2, :], ps[:, n % 3, :], ACT.Gelu).then_inc(gelued, 1)
                    if n >= 1:
                        round_v(n - 1)
                    if n < CHUNKS - PCH:
                        act.wait_ge(weighed, n + 1)
                        keep(PCH + n, (n // PCH) % 2)

            @block.vector
            def _(dve):
                own = Count(dve, own_sem)
                dve.wait_ge(side, 16)

                def hots(b):
                    part, tb = b // PCH, b % PCH
                    tok = slice(tb * TB, (tb + 1) * TB)
                    if b >= 2:
                        dve.wait_ge(gated, b - 1)
                    own.step(dve.tensor_tensor(E1[:, :, :], iota[:, part * PCH:(part + 1) * PCH, :],
                                               idx[:, 0, tok].unsqueeze(1).to_broadcast([P, PCH, TB]), ALU.is_equal))
                    own.step(dve.tensor_tensor(O2[:, b % 2, :, :], iota[:, :, :],
                                               idx[:, 1, tok].unsqueeze(1).to_broadcast([P, NK, TB]), ALU.is_equal))
                    own.wait()
                    for piece in range(2):
                        own.step(dve.tensor_tensor(O1[:, b % 2, piece, :, :], E1[:, :, :],
                                                   gate[:, piece, tok].unsqueeze(1).to_broadcast([P, PCH, TB]),
                                                   ALU.mult))
                    own.wait()
                    dve.nop().then_inc(hot, 1)

                def weigh(n):
                    dve.wait_ge(gelued, n + 1)
                    dve.wait_ge(gcopied, PCH * (n // PCH + 1))
                    if n >= WS:
                        dve.wait_ge(odone, DT * ((n - WS) // GRP + 1))
                    x = W[:, n % 2, :]
                    w = x.rearrange("p (s t) -> p s t", s=PCH)
                    dve.scalar_tensor_tensor(out=w, in0=region((n // PCH) % 2, n % PCH), scalar=1.0 / GSCALE, in1=w,
                                             op0=ALU.mult, op1=ALU.mult).then_inc(weighed, 1)
                    dve.wait_ge(weighed, n + 1)
                    Ws.write_hi(dve, (slice(None), n % WS), x).then_inc(w_hi, 1)
                    dve.wait_ge(w_hi, n + 1)
                    Ws.write_lo(dve, (slice(None), n % WS), x).then_inc(w_lo, 1)

                def add_group(q):
                    for d in range(DT):
                        m = q * DT + d
                        dve.wait_ge(odone, m + 1)
                        if q:
                            dve.wait_ge(oadded, m - DT + 1)
                        dve.tensor_tensor(kit.real(d), kit.real(d), ps[:, 3 + m % 3, :], ALU.add).then_inc(oadded, 1)

                for b in range(PCH + 1):
                    hots(b)
                for g in range(groups + 1):
                    for c in range(GRP):
                        n = g * GRP + c
                        if g < groups:
                            weigh(n)
                        if g >= 1 and c == GRP - 1:
                            add_group(g - 1)
                        if n + 1 < CHUNKS - PCH:
                            hots(PCH + n + 1)
                dve.wait_ge(oadded, groups * DT)


def short(kit):
    nc, t = kit.nc, kit.t
    with Stage(kit, "short") as st:
        ps = st.banks()
        hn = Split(st.sb("hn_hi", [P, DT, SEQ], F32R), st.sb("hn_lo", [P, DT, SEQ], F32R))
        cbuf = st.sb("c", [P, 2, SEQ])
        cv = st.sb("cv", [P, 2, 2 + SEQ])
        u = Split(st.sb("u_hi", [P, DT, SEQ], F32R), st.sb("u_lo", [P, DT, SEQ], F32R))
        um = st.sb("u", [P, 2, SEQ])
        gf = Norm(st, "gf", kit.real, kit.real, DT, SEQ, EPS1, lambda j: kit.gain("g_final", j), ps[:, 7:8, :], 1)
        an = Norm(st, "an", kit.real, None, DT, SEQ, EPS2, lambda j: kit.gain("a_norm_2", j),
                  ps[:, 7:8, :], 1, need=(gf.out, lambda j: j + 1), bufs=gf.bufs,
                  split=(hn, lambda j: (slice(None), j)))
        padded, copied, mixed, added = st.sem("padded"), st.sem("c_copied"), st.sem("mixed"), st.sem("added")
        own_sem = st.sem("vector_steps")
        tiles = []
        for i in range(DT):
            for part in "cvb":
                tiles.append(tile((part, i), lambda k: [hn.pair(slice(None), k)], need=(an.out, lambda k: k + 1)))
        for n in range(DT):
            tiles.append(tile(("o", n), lambda k: [u.pair(slice(None), k)], need=(mixed, lambda k: k + 1)))
        lin = split_linear(st, one_bank_slots(ps, 0, 7), tiles, 4, D,
                           pieces(t["a_w_in"], 3 * DT, D) + pieces(t["a_w_out"], DT, D))
        with nc.Block() as block:

            @block.sync
            def _(sp):
                lin.ring.load_all(sp)

            @block.gpsimd
            def _(pool):
                pool.memset(cv[:, :, 0:2], 0.0).then_inc(padded, 1)
                lin.ring.split_all(pool)

            @block.tensor
            def _(pe):
                gf.on_pe(pe)
                pe.wait_ge(gf.var, 1)
                an.on_pe(pe)
                lin.run(pe)

            @block.scalar
            def _(act):
                gf.on_act(act)
                an.on_act(act, lambda: lin.ring.round_to(act, 2))
                for i in range(DT):
                    slot, free = rounding(lin, act, ("c", i))
                    if i >= 2:
                        act.wait_ge(mixed, i - 1)
                    act.activation(cbuf[:, i % 2, :], slot[:, 0, :], ACT.Copy).then_inc(copied, 1)
                    act.wait_ge(copied, i + 1)
                    act.nop().then_inc(free, 1)
                lin.ring.round_to(act, len(tiles))

            @block.vector
            def _(dve):
                own = Count(dve, own_sem)
                gf.on_dve(dve, own)
                an.on_dve(dve, own)
                dve.wait_ge(padded, 1)
                for i in range(DT):
                    slot, free = lin.arrived(dve, ("v", i))
                    dve.wait_ge(copied, i + 1)
                    own.link(dve.tensor_tensor(cv[:, i % 2, 2:], slot[:, 0, :], cbuf[:, i % 2, :], ALU.mult))
                    dve.nop().then_inc(free, 1)
                    w = [kit.gain("a_conv_2", k * DT + i) for k in range(3)]
                    own.link(dve.tensor_scalar(um[:, i % 2, :], cv[:, i % 2, 0:SEQ], w[0], None, ALU.mult))
                    for k in (1, 2):
                        own.link(dve.scalar_tensor_tensor(out=um[:, i % 2, :], in0=cv[:, i % 2, k:k + SEQ], scalar=w[k],
                                                          in1=um[:, i % 2, :], op0=ALU.mult, op1=ALU.add))
                    slot, free = lin.arrived(dve, ("b", i))
                    own.link(dve.tensor_tensor(um[:, i % 2, :], um[:, i % 2, :], slot[:, 0, :], ALU.mult))
                    dve.nop().then_inc(free, 1)
                    own.link(u.write_hi(dve, (slice(None), i), um[:, i % 2, :]))
                    u.write_lo(dve, (slice(None), i), um[:, i % 2, :]).then_inc(mixed, 1)
                for n in range(DT):
                    slot, free = lin.arrived(dve, ("o", n))
                    dve.tensor_tensor(kit.real(n), kit.real(n), slot[:, 0, :], ALU.add).then_inc(added, 1)
                    dve.wait_ge(added, n + 1)
                    dve.nop().then_inc(free, 1)


def ffn(kit, layer, final=None):
    nc, t = kit.nc, kit.t
    with Stage(kit, f"ffn{layer}") as st:
        ps = st.banks()
        hn = Split(st.sb("hn_hi", [P, DT, SEQ], F32R), st.sb("hn_lo", [P, DT, SEQ], F32R))
        silu = st.sb("silu", [P, 2, SEQ])
        prod = st.sb("prod", [P, 2, SEQ])
        mid = Split(st.sb("mid_hi", [P, FT, SEQ], F32R), st.sb("mid_lo", [P, FT, SEQ], F32R))
        gu = t["f_w_gu"][layer * 2 * FT * P:(layer + 1) * 2 * FT * P, :]
        down = t["f_w_down"][layer * DT * P:(layer + 1) * DT * P, :]
        half = FT // 2 * P
        halves = [w[:, i * half:(i + 1) * half] for w in pieces(down, DT, F) for i in range(2)]
        fn = Norm(st, "fn", kit.real, None, DT, SEQ, EPS2, lambda j: kit.gain("f_norm_2", layer * DT + j),
                  ps[:, 7:8, :], 1, split=(hn, lambda j: (slice(None), j)))
        silued, multiplied, mixed, added = st.sem("silued"), st.sem("multiplied"), st.sem("mixed"), st.sem("added")
        own_sem, stored = st.sem("vector_steps"), kit.stored
        last = None
        if final is not None:
            last = Norm(st, "last", kit.real, kit.real, DT, SEQ, EPS2,
                        lambda j: kit.gain("final_norm_2", j), ps[:, 7:8, :], 1, need=(added, lambda j: j + 1),
                        bufs=fn.bufs)
        tiles = []
        for i in range(FT):
            for part in "gu":
                tiles.append(tile((part, i), lambda k: [hn.pair(slice(None), k)], need=(fn.out, lambda k: k + 1)))
        for n in range(DT):
            for i in range(2):
                tiles.append(tile(("d", n), lambda k: [mid.pair(slice(None), k)],
                                  ks=range(i * FT // 2, (i + 1) * FT // 2), need=(mixed, lambda k: k + 1),
                                  start=(i == 0), stop=(i == 1)))
        lin = split_linear(st, one_bank_slots(ps, 0, 7), tiles, 3, half, pieces(gu, 2 * FT, D) + halves)
        with nc.Block() as block:

            @block.sync
            def _(sp):
                lin.ring.load_all(sp)
                if last is not None:
                    for j in range(DT):
                        sp.wait_ge(last.out, j + 1)
                        sp.dma_start(final[j * P:(j + 1) * P, :], kit.real(j)).then_inc(stored, 16)
                    sp.wait_ge(stored, 16 * DT)

            @block.gpsimd
            def _(pool):
                lin.ring.split_all(pool)

            @block.tensor
            def _(pe):
                fn.on_pe(pe)
                lin.run(pe)
                if last is not None:
                    last.on_pe(pe)

            @block.scalar
            def _(act):
                fn.on_act(act, lambda: lin.ring.round_to(act, 2))
                for i in range(FT):
                    slot, free = rounding(lin, act, ("g", i))
                    if i >= 2:
                        act.wait_ge(multiplied, i - 1)
                    act.activation(silu[:, i % 2, :], slot[:, 0, :], ACT.Silu).then_inc(silued, 1)
                    act.wait_ge(silued, i + 1)
                    act.nop().then_inc(free, 1)
                lin.ring.round_to(act, len(tiles))
                if last is not None:
                    last.on_act(act)

            @block.vector
            def _(dve):
                own = Count(dve, own_sem)
                fn.on_dve(dve, own)
                for i in range(FT):
                    slot, free = lin.arrived(dve, ("u", i))
                    dve.wait_ge(silued, i + 1)
                    if i >= 2:
                        dve.wait_ge(mixed, i - 1)
                    dve.tensor_tensor(prod[:, i % 2, :], slot[:, 0, :], silu[:, i % 2, :], ALU.mult)\
                       .then_inc(multiplied, 1)
                    dve.wait_ge(multiplied, i + 1)
                    dve.nop().then_inc(free, 1)
                    own.link(mid.write_hi(dve, (slice(None), i), prod[:, i % 2, :]))
                    mid.write_lo(dve, (slice(None), i), prod[:, i % 2, :]).then_inc(mixed, 1)
                for n in range(DT):
                    slot, free = lin.arrived(dve, ("d", n))
                    dve.tensor_tensor(kit.real(n), kit.real(n), slot[:, 0, :], ALU.add).then_inc(added, 1)
                    dve.wait_ge(added, n + 1)
                    dve.nop().then_inc(free, 1)
                if last is not None:
                    last.on_dve(dve, own)


def nsa_in(kit, io):
    nc, t = kit.nc, kit.t
    with Stage(kit, "nsain") as st:
        ps = st.banks()
        hn = Split(st.sb("hn_hi", [P, DT, SEQ], F32R), st.sb("hn_lo", [P, DT, SEQ], F32R))
        kn = Norm(st, "kn", kit.real, None, DT, SEQ, EPS2, lambda j: kit.gain("kv_norm_2", j),
                  ps[:, 7:8, :], 1, split=(hn, lambda j: (slice(None), j)))
        raw = st.sb("raw", [P, 2, NG, SEQ])
        X = st.sb("X", [P, 2, 2, NG, SEQ // DC, DC // 2])
        w1 = st.sb("w1", [P, LC // 2, CH])
        w2 = st.sb("w2", [P, 2, 2, HD])
        pe2 = st.sb("pe2", [P, 2, LC])
        hid = st.sb("hid", [P, 2, NG * NC])
        side = st.sem("side_loaded")
        w1_in = [st.sem("w1k_loaded"), st.sem("w1v_loaded")]
        b_out = st.sem("b_normed")
        x_made, hid_done, hid_silu, c_done, c_copied = (st.sem(n) for n in
                                                        ("x_made", "hid_done", "hid_silu", "c_done", "c_copied"))
        vcopied, gcopied = st.sem("v_copied"), st.sem("g_copied")

        def values(i):
            def by(pe, whi, wlo):
                if i == 0:
                    pe.wait_ge(kn.var, 1)
                for half in range(2):
                    k, c = 2 * i + half, slice(half * SEQ, (half + 1) * SEQ)
                    for j in range(ST):
                        x = hn.pair(slice(None), k, slice(j * P, (j + 1) * P))
                        mm = product(pe, ps[:, 4 + j, :], x, (whi[:, c], wlo[:, c]), k == 0, k == DT - 1)
                return mm
            return by

        def gates(pe, whi, wlo):
            pe.wait_ge(vcopied, 1)
            for j in range(ST):
                for k in range(DT):
                    c = slice(k * 3 * NH, (k + 1) * 3 * NH)
                    mm = product(pe, ps[:, 4, j * 3 * NH:(j + 1) * 3 * NH],
                                 hn.pair(slice(None), k, slice(j * P, (j + 1) * P)), (whi[:, c], wlo[:, c]),
                                 k == 0, k == DT - 1)
            return mm

        x = lambda k: [hn.pair(slice(None), k)]
        tiles = [tile(("k", n), x, need=(kn.out, lambda k: k + 1)) for n in range(8)]
        tiles += [tile(("v", i), by=values(i)) for i in range(DT // 2)]
        n_keys = len(tiles)
        tiles += [tile(("q", n), x, need=(b_out, lambda k: k + 1)) for n in range(DT)] + [tile("gates", by=gates)]
        lin = split_linear(st, one_bank_slots(ps, 0, 4), tiles, 3, D,
                           pieces(t["w_kraw"], 8, D) + [t["w_v2"][:, i * D:(i + 1) * D] for i in range(DT // 2)]
                           + pieces(t["w_q2"], DT, D) + [t["w_gate2"][:, :]])
        own_sem = st.sem("vector_steps")
        act_sem = st.sem("scalar_steps")
        with nc.Block() as block:

            @block.sync
            def _(sp):
                sp.dma_start(w2[:, :, :, :], t["cmp_w2"].rearrange("p (a c n) -> p a c n", a=2, c=2)).then_inc(side, 16)
                sp.dma_start(pe2[:, :, :], t["cmp_pe"].rearrange("p (a l) -> p a l", a=2)).then_inc(side, 16)
                for h in range(NH):
                    sp.dma_start(io["qT"][HD:HD + 2, h, :], t["c_qrows"][2 * h:2 * h + 2, :]).then_inc(side, 16)
                for g in range(NG):
                    for b in range(2):
                        sp.dma_start(io["kT"][HD:HD + 2, b, g, :], t["c_krows"]).then_inc(side, 16)
                sp.dma_start(io["kc"][HD:HD + 2, :, :], t["c_crows"].rearrange("r (g n) -> r g n", g=NG)).then_inc(side, 16)
                sp.dma_start(io["vis"][:, :, :, :], t["c_vis"].rearrange("p (a j n) -> p a j n", a=2, j=ST)).then_inc(side, 16)
                sp.dma_start(w1[:, :, :], t["cmp_w1"][0:P, :].rearrange("p (m c) -> p m c", c=CH)).then_inc(w1_in[0], 16)
                lin.ring.load_all(sp)

            n_side = 16 * (2 + NH + 2 * NG + 2)

            @block.tensor
            def _(pe):
                kn.on_pe(pe)
                lin.run(pe, lambda n: n < n_keys)
                pe.wait_ge(side, n_side)
                pe.wait_ge(vcopied, ST)
                for kind in range(2):
                    pe.wait_ge(w1_in[kind], 16)
                    pe.wait_ge(x_made, kind + 1)
                    for c in range(2):
                        for m in range(LC // 2):
                            win, r = m // (DC // 2), m % (DC // 2)
                            mm = pe.matmul(ps[:, 5 + c, 0:NG * NC], w1[:, m, c * P:(c + 1) * P],
                                           X[:, kind, win, :, win:win + NC, r], start=(m == 0), stop=(m == LC // 2 - 1))
                    mm.then_inc(hid_done, 1)
                    pe.wait_ge(hid_silu, 2 * (kind + 1))
                    if kind == 0:
                        for c in range(2):
                            mm = pe.matmul(ps[0:HD, 7, 0:NG * NC], w2[:, 0, c, :], hid[:, c, :],
                                           start=(c == 0), stop=(c == 1))
                        mm.then_inc(c_done, 1)
                        pe.wait_ge(c_copied, 1)
                    else:
                        for g in range(NG):
                            for c in range(2):
                                mm = pe.matmul(ps[0:NC, 7, g * HD:(g + 1) * HD], hid[:, c, g * NC:(g + 1) * NC],
                                               w2[:, 1, c, :], start=(c == 0), stop=(c == 1))
                        mm.then_inc(c_done, 1)
                lin.run(pe, lambda n: n >= n_keys)

            @block.gpsimd
            def _(pool):
                lin.ring.split_all(pool)

            @block.scalar
            def _(act):
                own = Count(act, act_sem)
                kn.on_act(act, lambda: lin.ring.round_to(act, 2))
                for n in (4, 5, 6, 7):
                    slot, free = rounding(lin, act, ("k", n))
                    for e in range(2):
                        own.step(act.activation(io["kT"][0:HD, (n - 4) // 2, 2 * (n % 2) + e, :],
                                                slot[e * HD:(e + 1) * HD, 0, :], ACT.Copy))
                    own.wait()
                    act.nop().then_inc(free, 1)
                rounding(lin, act, ("v", DT // 2 - 1))
                for j in range(ST):
                    act.activation(io["v"][:, j, :], ps[:, 4 + j, :], ACT.Copy).then_inc(vcopied, 1)
                for kind in range(2):
                    act.wait_ge(hid_done, kind + 1)
                    if kind == 0:
                        act.dma_start(w1[:, :, :], t["cmp_w1"][P:2 * P, :].rearrange("p (m c) -> p m c", c=CH))\
                           .then_inc(w1_in[1], 16)
                    else:
                        act.wait_ge(c_done, 1)
                    for c in range(2):
                        act.activation(hid[:, c, :], ps[:, 5 + c, 0:NG * NC], ACT.Silu).then_inc(hid_silu, 1)
                    act.wait_ge(c_done, kind + 1)
                    if kind == 0:
                        act.activation(io["kc"][0:HD, :, :].rearrange("p g n -> p (g n)"), ps[0:HD, 7, 0:NG * NC],
                                       ACT.Copy).then_inc(c_copied, 1)
                own.link(act.activation(io["vc"][:, :], ps[0:NC, 7, 0:NG * HD], ACT.Copy))
                for n in range(DT):
                    slot, free = rounding(lin, act, ("q", n))
                    for e in range(2):
                        own.step(act.activation(io["qT"][0:HD, 2 * n + e, :], slot[e * HD:(e + 1) * HD, 0, :],
                                                ACT.Copy, scale=HD ** -0.5))
                    own.wait()
                    act.nop().then_inc(free, 1)
                rounding(lin, act, "gates")
                own.link(act.activation(io["gate"][:, :, :].rearrange("p j n -> p (j n)"), ps[:, 4, 0:ST * 3 * NH],
                                        ACT.Sigmoid))

            @block.vector
            def _(dve):
                own = Count(dve, own_sem)
                kn.on_dve(dve, own)
                dve.wait_ge(side, n_side)
                for kind in range(2):
                    for n in range(2):
                        slot, free = lin.arrived(dve, ("k", 2 * kind + n))
                        for e in range(2):
                            g = 2 * n + e
                            own.step(dve.tensor_copy(raw[0:HD, kind, g, :], slot[e * HD:(e + 1) * HD, 0, :]))
                            own.step(dve.tensor_copy(raw[HD:P, kind, g, 0:SEQ - 1], slot[e * HD:(e + 1) * HD, 0, 1:SEQ]))
                        own.wait()
                        dve.nop().then_inc(free, 1)
                    for win in range(2):
                        for g in range(NG):
                            own.step(dve.tensor_tensor(
                                X[:, kind, win, g, :, :], raw[:, kind, g, :].rearrange("p (n r) -> p n r", r=DC)[:, :, 0:DC:2],
                                pe2[:, kind, win * DC:(win + 1) * DC:2].unsqueeze(1)
                                .to_broadcast([P, SEQ // DC, DC // 2]), ALU.add))
                    own.wait()
                    dve.nop().then_inc(x_made, 1)
                lin.arrived(dve, ("v", DT // 2 - 1))
                kn.scale(dve, own, kit.real, lambda j: kit.gain("b_norm_2", j), kn.split, b_out)


def nsa(kit, io):
    nc = kit.nc
    with Stage(kit, "nsa") as st:
        ps = st.banks()
        items = []
        for hp in range(NH // 2):
            for j in range(ST):
                for h in (2 * hp, 2 * hp + 1):
                    g = h // HPG
                    q = io["qT"][:, h, j * P:(j + 1) * P]
                    out = lambda o, e=h % 2, j=j: o[e * HD:(e + 1) * HD, j * P:(j + 1) * P]
                    gate = lambda b: io["gate"][:, j, 3 * h + b:3 * h + b + 1]
                    items.append(dict(q=q, ks=[(io["kc"][:, g, :], 0)], lo=0, hi=NC,
                                      masks=[(0, io["vis"][:, 0, j, :])],
                                      pts=[(0, NC, io["vc"][:, g * HD:(g + 1) * HD])], out=out, bank=hp,
                                      start=True, stop=False, scale=1.0, gate=gate(0), vis=io["vis"][:, 1, j, :]))
                    for b in range(2):
                        n = (j + 1) * P
                        items.append(dict(
                            q=q, ks=[(io["kT"][:, b, g, 0:n], 0)], lo=0, hi=n, masks=[(j * P, kit.tri[:, :])],
                            pts=[(i * P, P, io["v"][:, i, (b * NG + g) * HD:(b * NG + g + 1) * HD])
                                 for i in range(j + 1)],
                            out=out, bank=hp, start=False, stop=(b == 1), scale=1.0, gate=gate(1 + b), vis=None))
        at = Attention(st, items, [ps[:, i, :] for i in range(3)], [ps[:, 3 + i, :] for i in range(2)],
                       [ps[:, 6, :], ps[:, 7, :]], SEQ,
                       lambda dve, b, o: dve.tensor_copy(io["attnT"][:, b, :], o))
        with nc.Block() as block:

            @block.tensor
            def _(pe):
                at.on_pe(pe)

            @block.scalar
            def _(act):
                at.on_act(act)

            @block.vector
            def _(dve):
                at.on_dve(dve)


def nsa_out(kit, io):
    nc, t = kit.nc, kit.t
    with Stage(kit, "nsaout") as st:
        ps = st.banks()
        attn = Split(st.sb("attn_hi", [P, DT, SEQ], F32R), st.sb("attn_lo", [P, DT, SEQ], F32R))
        split = st.sem("attn_split")
        lin = split_linear(st, one_bank_slots(ps, 0, 6),
                           [tile(("o", n), lambda k: [attn.pair(slice(None), k)], need=(split, lambda k: k + 1))
                            for n in range(DT)], 4, D, pieces(t["b_w_o"], DT, D))
        added, own_sem = st.sem("added"), st.sem("vector_steps")
        with nc.Block() as block:

            @block.sync
            def _(sp):
                lin.ring.load_all(sp)

            @block.gpsimd
            def _(pool):
                lin.ring.split_all(pool)

            @block.scalar
            def _(act):
                lin.ring.round_to(act, DT)

            @block.tensor
            def _(pe):
                lin.run(pe)

            @block.vector
            def _(dve):
                own = Count(dve, own_sem)
                attn.write_all(dve, own, io["attnT"], DT, split)
                for n in range(DT):
                    slot, free = lin.arrived(dve, ("o", n))
                    dve.tensor_tensor(kit.real(n), kit.real(n), slot[:, 0, :], ALU.add).then_inc(added, 1)
                    dve.wait_ge(added, n + 1)
                    dve.nop().then_inc(free, 1)


def build_program(nc, t, out, dump=None, upto=99):
    with ExitStack() as ctx:
        kit = Kit(nc, t, ctx)

        def done(n):
            if dump is not None and upto == n:
                dump(kit)
                return True
            return False

        with ExitStack() as late:
            sb = lambda n, s, d=F32: late.enter_context(nc.sbuf_tensor(n, s, d))
            io = {"hn": Split(sb("xn_hi", [P, DT, T1], F32R), sb("xn_lo", [P, DT, T1], F32R)),
                  "idx": sb("idx", [P, 2, SEQ], F16), "gate": sb("gate", [P, 2, SEQ], F16)}
            io["xn"] = Split(io["hn"].hi[:, :, 0:SEQ], io["hn"].lo[:, :, 0:SEQ])
            with ExitStack() as first:
                sb1 = lambda n, s, d=F32: first.enter_context(nc.sbuf_tensor(n, s, d))
                io["mixT"] = sb1("mixT", [P, 2 * CT, SEQ])
                with ExitStack() as qkv:
                    sb2 = lambda n, s, d=F32: qkv.enter_context(nc.sbuf_tensor(n, s, d))
                    io.update(qT=sb2("qT", [DQ, HEADS, SEQ]), kT=sb2("kT", [DQ, HEADS, T1]), v=sb2("v", [P, ST + 1, CC]))
                    front(kit, io)
                    kit.io = io
                    if done(1):
                        return
                    mla(kit, io)
                    if done(2):
                        return
                route(kit, io)
            if done(3):
                return
            experts(kit, io)
        if done(4):
            return
        short(kit)
        if done(5):
            return
        ffn(kit, 0)
        if done(6):
            return
        with ExitStack() as qkv:
            sb = lambda n, s, d=F32: qkv.enter_context(nc.sbuf_tensor(n, s, d))
            io = {"qT": sb("q2T", [HD + 2, NH, SEQ]), "kT": sb("k2T", [HD + 2, 2, NG, SEQ]),
                  "v": sb("v2", [P, ST, 2 * NG * HD]), "gate": sb("gate2", [P, ST, 3 * NH]),
                  "kc": sb("kc", [HD + 2, NG, NC]), "vc": sb("vc", [NC, NG * HD]), "vis": sb("vis", [P, 2, ST, NC])}
            nsa_in(kit, io)
            kit.io = io
            if done(7):
                return
            io["attnT"] = sb("attn2T", [P, DT, SEQ])
            nsa(kit, io)
            if done(8):
                return
            nsa_out(kit, io)
        if done(9):
            return
        ffn(kit, 1, final=out)


def constants():
    f = np.float32
    pos = np.arange(T1, dtype=f)
    freq = (f(10000.0) ** (-np.arange(ROPE // 2, dtype=f) / f(ROPE // 2))).astype(f)
    ang = (freq[:, None] * pos[None, :]).astype(f)
    cos, sin = np.cos(ang).astype(f), np.sin(ang).astype(f)
    slopes = np.exp2(-8.0 * np.arange(1, NH + 1) / NH).astype(f)
    tok = np.arange(SEQ, dtype=f)
    qrows = np.stack([np.stack([np.full(SEQ, s, f), -s * tok]) for s in slopes]).reshape(2 * NH, SEQ)
    centre = np.arange(NC, dtype=f) * DC + (LC - 1) / 2.0
    end = np.arange(NC) * DC + LC - 1
    see = (end[None, :] <= np.arange(SEQ)[:, None])
    vis = np.stack([np.where(see, 0.0, NEG), see.astype(f)]).astype(f).reshape(2, ST, P, NC).transpose(2, 0, 1, 3)
    return {
        "c_cos": np.tile(np.concatenate([cos, cos]), (4, 1)),
        "c_sin": np.tile(np.concatenate([-sin, sin]), (4, 1)),
        "c_ident": np.eye(P, dtype=f),
        "c_tri": np.where(np.arange(P)[None, :] <= np.arange(P)[:, None], 0.0, NEG).astype(f),
        "c_iota": np.tile(np.arange(TOPK, dtype=f), (P, 1)),
        "c_iota16": np.tile(np.repeat(np.arange(NK), TB).astype(np.float16), (P, 1)),
        "c_qrows": qrows.astype(f),
        "c_krows": np.stack([tok, np.ones(SEQ, f)]),
        "c_crows": np.tile(np.stack([centre, np.ones(NC)]).astype(f), (1, NG)),
        "c_vis": vis.reshape(P, 2 * ST * NC),
    }


def tiles_of(w, m=P):
    k, n = w.shape
    return w.reshape(k // P, P, n // m, m).transpose(2, 1, 0, 3).reshape(n // m * P, k // P * m)


def lay_out(i):
    ht = np.concatenate([i["meta"], i["x"][0]], axis=0).T
    a = {"hT0": ht.reshape(DT, P, T1).transpose(1, 0, 2).reshape(P, DT * T1)}
    a["gains"] = np.concatenate([i[n].reshape(-1, P) for n, _ in GAINS], axis=0).T
    w = i["w_in"][0]
    ab = np.concatenate([np.concatenate([w[:, CC + c * P:CC + (c + 1) * P], w[:, c * P:(c + 1) * P]], axis=1)
                         for c in range(CT)], axis=1)
    c0 = 2 * CC
    a["w_ab"] = tiles_of(ab)
    a["w_cq"] = tiles_of(w[:, c0:c0 + QL])
    a["w_ckv"] = tiles_of(w[:, c0 + QL:c0 + QL + KVL])
    kr = w[:, c0 + QL + KVL:]
    a["w_krope"] = tiles_of(np.concatenate([kr, kr[:, ROPE // 2:], kr[:, :ROPE // 2]] * 2, axis=1))
    uq = i["w_uq"][0].reshape(QL, HEADS, DQ)
    nope, rope = uq[:, :, :NOPE], uq[:, :, NOPE:]
    swap = np.concatenate([rope[:, :, ROPE // 2:], rope[:, :, :ROPE // 2]], axis=2)
    rope, swap = rope.reshape(QL, 2, P), swap.reshape(QL, 2, P)
    both = np.stack([rope, swap], axis=2).reshape(QL, 4 * P)
    a["w_uq"] = tiles_of(np.concatenate([nope.reshape(QL, HEADS * NOPE), both], axis=1))
    ukv = i["w_ukv"][0].reshape(KVL, HEADS, NOPE + VH)
    a["w_ukv"] = np.concatenate([ukv[:, :, :NOPE].reshape(KVL, -1), ukv[:, :, NOPE:].reshape(KVL, -1)], axis=1)
    a["w_out"] = tiles_of(i["w_out"][0])
    a["peer_wq"] = tiles_of(i["peer_wq"][0])
    a["peer_keys"] = i["peer_keys"][0].transpose(1, 3, 0, 2).reshape(P, PH * NK)
    a["peer_uT"] = i["peer_u"][0].reshape(CHUNKS, P, DT, P).transpose(0, 3, 2, 1).reshape(CHUNKS * P, D)
    a["peer_v"] = i["peer_v"][0]
    wi = i["a_w_in_2"][0]
    order = [wi[:, p * D + n * P:p * D + (n + 1) * P] for n in range(DT) for p in (1, 2, 0)]
    a["a_w_in"] = tiles_of(np.concatenate(order, axis=1))
    a["a_w_out"] = tiles_of(i["a_w_out_2"][0])
    gu = i["f_w_gu_2"]
    order = [gu[:, :, p * F + n * P:p * F + (n + 1) * P] for n in range(FT) for p in range(2)]
    gu = np.concatenate(order, axis=2)
    a["f_w_gu"] = np.concatenate([tiles_of(gu[0]), tiles_of(gu[1])], axis=0)
    a["f_w_down"] = np.concatenate([tiles_of(i["f_w_down_2"][0]), tiles_of(i["f_w_down_2"][1])], axis=0)
    kv = i["w_kv_2"].reshape(D, 6, NG * HD)
    a["w_kraw"] = tiles_of(np.concatenate([kv[:, s] for s in (0, 1, 2, 4)], axis=1))
    a["w_v2"] = np.concatenate([kv[:, 3], kv[:, 5]], axis=1).reshape(DT, P, -1).transpose(1, 0, 2).reshape(P, -1)
    qg = i["b_w_qg_2"][0]
    a["w_q2"] = tiles_of(qg[:, :NH * HD])
    a["w_gate2"] = qg[:, NH * HD:].reshape(DT, P, -1).transpose(1, 0, 2).reshape(P, -1)
    a["b_w_o"] = tiles_of(i["b_w_o_2"][0])
    w1 = np.stack([i["cmp_w1_k_2"], i["cmp_w1_v_2"]]).reshape(2, LC // 2, P, CH)
    a["cmp_w1"] = w1.transpose(0, 2, 1, 3).reshape(2 * P, LC // 2 * CH)
    w2 = np.stack([i["cmp_w2_k_2"], i["cmp_w2_v_2"]]).reshape(2, 2, P, HD)
    a["cmp_w2"] = w2.transpose(2, 0, 1, 3).reshape(P, 4 * HD)
    pe = np.stack([i["cmp_pe_k_2"], i["cmp_pe_v_2"]]).transpose(2, 0, 1)
    a["cmp_pe"] = np.concatenate([pe, np.roll(pe, -1, axis=2)], axis=0).reshape(P, 2 * LC)
    return a


def kernel(**inputs):
    import concourse.bacc as bacc
    from concourse.bass_utils import run_bass_kernel_spmd

    nc = bacc.Bacc("TRN2", target_bir_lowering=False, num_devices=1)
    laid = lay_out({k: np.asarray(v) for k, v in inputs.items()})
    laid.update(constants())
    arrays, aps = {}, {}
    for name, a in laid.items():
        a = np.ascontiguousarray(a)
        arrays[f"in_{name}"] = a
        aps[name] = nc.dram_tensor(f"in_{name}", a.shape, mybir.dt.from_np(a.dtype), kind="ExternalInput").ap()
    out = nc.dram_tensor("out_T", (D, SEQ), F32, kind="ExternalOutput").ap()
    build_program(nc, aps, out)
    r = run_bass_kernel_spmd(nc, [arrays], core_ids=[0])
    return np.ascontiguousarray(r.results[0]["out_T"].T)[None]
```

```python
from contextlib import ExitStack

import numpy as np

import concourse.bass as bass
from concourse import mybir

F32 = mybir.dt.float32
F32R = mybir.dt.float32r
F16 = mybir.dt.float16
U32 = mybir.dt.uint32
ALU = mybir.AluOpType
ACT = mybir.ActivationFunctionType
AX = mybir.AxisListType.X

P = 128
D = 1024
DT = D // P
SEQ = 512
NMETA = 16
T1 = SEQ + NMETA
HT = T1 // 2
ST = SEQ // P

HEADS = 8
NOPE = 64
ROPE = 32
VH = 64
DQ = NOPE + ROPE
QL = 256
KVL = 128
CC = 512
CT = CC // P
CK = 31
NK = 128
PH = 8
TOPK = 16
TOP4 = 4
NCAND = TOP4 * TOPK + (TOPK - TOP4) * TOP4
EPS1 = 1e-6

F = 2816
FT = F // P
NH = 16
NG = 4
HPG = NH // NG
HD = 64
LC = 32
DC = 16
NC = (SEQ - LC) // DC + 1
CH = 256
EPS2 = 1e-5
NEG = -1e30
GSCALE = 16384.0

GAINS = [("g_mix_norm", 8), ("g_q", 2), ("g_kv", 1), ("conv_b", 4), ("g_conv_ln", 4), ("b_conv_ln", 4),
         ("g_out_attn", 4), ("g_out_conv", 4), ("g_ffn_norm", 8), ("g_final", 8), ("conv_w", CK * CT),
         ("a_norm_2", 8), ("kv_norm_2", 8), ("b_norm_2", 8), ("f_norm_2", 16), ("final_norm_2", 8),
         ("a_conv_2", 24)]
GCOL = {}
_at = 0
for _name, _n in GAINS:
    GCOL[_name] = _at
    _at += _n
NGAIN = _at


class Count:

    def __init__(self, eng, sem):
        self.eng, self.sem, self.n = eng, sem, 0

    def step(self, ins):
        self.n += 1
        return ins.then_inc(self.sem, 1)

    def wait(self):
        self.eng.wait_ge(self.sem, self.n)

    def link(self, ins):
        self.step(ins)
        self.wait()


class Kit:

    def __init__(self, nc, t, ctx):
        self.nc, self.t, self.ctx = nc, t, ctx
        sb = lambda n, s, d=F32: ctx.enter_context(nc.sbuf_tensor(n, s, d))
        self.hT = sb("hT", [P, DT, T1])
        self.gains = sb("gains", [P, NGAIN])
        self.ones = sb("ones", [P, P])
        self.ident = sb("ident", [P, P])
        self.tri = sb("tri", [P, P])
        self.loaded = [ctx.enter_context(nc.semaphore(f"h_loaded{i}")) for i in range(DT // 2)]
        self.stored = ctx.enter_context(nc.semaphore("output_stored"))
        self.made = ctx.enter_context(nc.semaphore("ones_made"))

    def gain(self, name, j):
        c = GCOL[name] + j
        return self.gains[:, c:c + 1]

    def real(self, j):
        return self.hT[:, j, NMETA:T1]


class Stage:

    def __init__(self, kit, name):
        self.kit, self.nc, self.name = kit, kit.nc, name
        self.ctx = ExitStack()
        self.sems = []

    def __enter__(self):
        self.ctx.__enter__()
        return self

    def __exit__(self, kind, *a):
        if kind is None:
            self.nc.clear_and_free_semaphores(self.sems)
            self.nc.all_engine_barrier()
        return self.ctx.__exit__(kind, *a)

    def sb(self, name, shape, dt=F32):
        return self.ctx.enter_context(self.nc.sbuf_tensor(f"{self.name}_{name}", shape, dt))

    def banks(self, n=8):
        return self.ctx.enter_context(self.nc.psum_tensor(f"{self.name}_psum", [P, n, 512], F32))

    def sem(self, name):
        self.sems.append(self.nc.alloc_semaphore(f"{self.name}_{name}"))
        return self.sems[-1]


class SplitRing:

    def __init__(self, st, name, slots, cols, tiles, done):
        self.buf = st.sb(name, [P, slots, cols])
        self.hi = st.sb(f"{name}_hi", [P, 2, cols], F32R)
        self.lo = st.sb(f"{name}_lo", [P, 2, cols], F32R)
        self.n, self.tiles, self.done, self.n_rounded = slots, tiles, done, 0
        self.into = [st.sem(f"{name}_in{i}") for i in range(slots)]
        self.rounded = st.sem(f"{name}_rounded")
        self.split = st.sem(f"{name}_split")

    def load_first(self, sp):
        for n, w in enumerate(self.tiles[:self.n]):
            sp.dma_start(self.buf[:, n, 0:w.shape[1]], w).then_inc(self.into[n], 16)
        self.n_loaded = self.n

    n_loaded = 0

    def load_all(self, sp):
        for n, w in enumerate(self.tiles):
            if n < self.n_loaded:
                continue
            if n >= self.n:
                sp.wait_ge(self.split, n - self.n + 1)
            sp.dma_start(self.buf[:, n % self.n, 0:w.shape[1]], w).then_inc(self.into[n % self.n], 16)

    def round_to(self, act, m):
        for n in range(self.n_rounded, min(m, len(self.tiles))):
            c = self.tiles[n].shape[1]
            act.wait_ge(self.into[n % self.n], 16 * (n // self.n + 1))
            if n >= 2:
                act.wait_ge(self.done, n - 1)
            act.activation(self.hi[:, n % 2, 0:c], self.buf[:, n % self.n, 0:c], ACT.Copy).then_inc(self.rounded, 1)
        self.n_rounded = max(self.n_rounded, min(m, len(self.tiles)))

    def split_all(self, pool):
        for n, w in enumerate(self.tiles):
            c = w.shape[1]
            pool.wait_ge(self.rounded, n + 1)
            pool.tensor_tensor(self.lo[:, n % 2, 0:c], self.buf[:, n % self.n, 0:c],
                               self.hi[:, n % 2, 0:c].bitcast(F32), ALU.subtract).then_inc(self.split, 1)

    def take(self, pe, n):
        pe.wait_ge(self.split, n + 1)
        return self.hi[:, n % 2, :], self.lo[:, n % 2, :]


def product(pe, out, w, x, start, stop):
    pe.matmul(out, w[0], x[0], start=start, stop=False)
    pe.matmul(out, w[0], x[1], start=False, stop=False)
    return pe.matmul(out, w[1], x[0], start=False, stop=stop)


def tile(key, rhs=None, ks=DT, need=None, start=True, stop=True, by=None):
    start = start and by is None
    return dict(by=by, key=key, rhs=rhs, ks=range(ks) if isinstance(ks, int) else ks, need=need, start=start, stop=stop)


class SplitLinear:

    def __init__(self, st, slots, tiles, name="lin"):
        self.slots, self.tiles = slots, tiles
        self.index, self.place = {}, []
        s = -1
        for n, x in enumerate(tiles):
            s += x["start"]
            self.place.append(s)
            if x["stop"]:
                self.index[x["key"]] = n
        self.done = st.sem(f"{name}_done")
        self.free = [st.sem(f"{name}_free{i}") for i in range(len(slots))]
        self.uses = s + 1

    def run(self, pe, only=None):
        for n, x in enumerate(self.tiles):
            if only is not None and not only(n):
                continue
            whi, wlo = self.ring.take(pe, n)
            if x["by"] is not None:
                x["by"](pe, whi, wlo).then_inc(self.done, 1)
                continue
            use = self.place[n]
            s = use % len(self.slots)
            if x["start"] and use >= len(self.slots):
                pe.wait_ge(self.free[s], use // len(self.slots))
            for i, k in enumerate(x["ks"]):
                if x["need"] is not None:
                    pe.wait_ge(x["need"][0], x["need"][1](k))
                c = slice(i * P, (i + 1) * P)
                for half, pair in enumerate(x["rhs"](k)):
                    mm = product(pe, self.slots[s][:, half, 0:pair[0].shape[-1]], (whi[:, c], wlo[:, c]), pair,
                                 x["start"] and i == 0, x["stop"] and i == len(x["ks"]) - 1)
            mm.then_inc(self.done, 1)

    def all_free(self, pe):
        for s in range(len(self.slots)):
            pe.wait_ge(self.free[s], len([u for u in range(self.uses) if u % len(self.slots) == s]))

    def arrived(self, eng, key):
        n = self.index[key]
        eng.wait_ge(self.done, n + 1)
        s = self.place[n] % len(self.slots)
        return self.slots[s], self.free[s]


def rounding(lin, act, key):
    n = lin.index[key]
    lin.ring.round_to(act, n + 2)
    there = lin.arrived(act, key)
    lin.ring.round_to(act, n + 3)
    return there


def split_linear(st, slots, tiles, ring_slots, cols, weights):
    lin = SplitLinear(st, slots, tiles)
    lin.ring = SplitRing(st, "w", ring_slots, cols, weights, lin.done)
    return lin


class Split:

    def __init__(self, hi, lo):
        self.hi, self.lo = hi, lo

    def pair(self, *at):
        return self.hi[at], self.lo[at]

    def write_hi(self, dve, at, src):
        return dve.tensor_copy(self.hi[at], src)

    def write_lo(self, dve, at, src):
        return dve.tensor_tensor(self.lo[at], src, self.hi[at].bitcast(F32), ALU.subtract)

    def write_all(self, dve, own, src, n, there):
        for k in range(n + 1):
            if k:
                own.wait()
            if k < n:
                own.step(self.write_hi(dve, (slice(None), k), src[:, k, :]))
            if k:
                self.write_lo(dve, (slice(None), k - 1), src[:, k - 1, :]).then_inc(there, 1)


class Norm:

    def __init__(self, st, name, src, dst, n, width, eps, gain, ps, parts, need=None, bufs=None, split=None):
        self.kit = st.kit
        self.src, self.dst, self.n, self.eps, self.gain = src, dst, n, eps, gain
        self.ps, self.parts, self.need, self.dim, self.split = ps, parts, need, n * P, split
        self.width = width
        sq, rs, tmp = bufs or (st.sb(f"{name}_sq", [P, 2, width]), st.sb(f"{name}_rs", [P, width]), None)
        if split is not None and tmp is None:
            tmp = st.sb(f"{name}_tmp", [P, 3, width])
        self.bufs = (sq, rs, tmp)
        self.sq, self.rs = sq[:, :, 0:width], rs[:, 0:width]
        self.tmp = None if tmp is None else tmp[:, :, 0:width]
        self.squared = st.sem(f"{name}_squared")
        self.summed = st.sem(f"{name}_summed")
        self.var = st.sem(f"{name}_var")
        self.root = st.sem(f"{name}_root")
        self.out = st.sem(f"{name}_out")

    def cols(self, x):
        w = self.width // self.parts
        return [x[:, i * w:(i + 1) * w] for i in range(self.parts)]

    def halves(self, x):
        return x.rearrange("p (a b) -> p a b", a=self.parts)

    def on_act(self, act, meanwhile=None):
        self.squares(act)
        if meanwhile is not None:
            meanwhile()
        self.take_root(act)

    def squares(self, act):
        for j in range(self.n):
            if self.need is not None:
                sem = self.need[0][j] if isinstance(self.need[0], list) else self.need[0]
                act.wait_ge(sem, self.need[1](j))
            if j >= 2:
                act.wait_ge(self.summed, j - 1)
            act.activation(self.sq[:, j % 2, :], self.src(j), ACT.Square).then_inc(self.squared, 1)

    def take_root(self, act):
        act.wait_ge(self.var, 1)
        act.activation(self.rs, self.rs, ACT.Sqrt).then_inc(self.root, 1)

    def on_pe(self, pe):
        for j in range(self.n):
            pe.wait_ge(self.squared, j + 1)
            for i, x in enumerate(self.cols(self.sq[:, j % 2, :])):
                mm = pe.matmul(self.ps[:, i, 0:x.shape[-1]], self.kit.ones[:, :], x,
                               start=(j == 0), stop=(j == self.n - 1))
            mm.then_inc(self.summed, 1)

    def on_dve(self, dve, own):
        self.variance(dve)
        self.finish(dve, own)

    def variance(self, dve):
        w = self.width // self.parts
        dve.wait_ge(self.summed, self.n)
        dve.tensor_scalar(self.halves(self.rs), self.ps[:, 0:self.parts, 0:w], 1.0 / self.dim, self.eps,
                          ALU.mult, ALU.add).then_inc(self.var, 1)

    def finish(self, dve, own):
        dve.wait_ge(self.root, 1)
        own.link(dve.reciprocal(self.rs, self.rs))
        self.scale(dve, own, self.src, self.gain, self.split, self.out)

    def scale(self, dve, own, src, gain, split, out):
        if split is None:
            for j in range(self.n):
                dve.scalar_tensor_tensor(out=self.dst(j), in0=src(j), scalar=gain(j), in1=self.rs,
                                         op0=ALU.mult, op1=ALU.mult).then_inc(out, 1)
            dve.wait_ge(out, self.n)
            return
        to, at = split
        for j in range(self.n + 2):
            if j < self.n:
                own.step(dve.scalar_tensor_tensor(out=self.tmp[:, j % 3, :], in0=src(j), scalar=gain(j),
                                                  in1=self.rs, op0=ALU.mult, op1=ALU.mult))
            if 0 <= j - 1 < self.n:
                own.step(to.write_hi(dve, at(j - 1), self.tmp[:, (j - 1) % 3, :]))
            if j >= 2:
                own.step(to.write_lo(dve, at(j - 2), self.tmp[:, (j - 2) % 3, :]))
            own.wait()
            if j >= 2:
                dve.nop().then_inc(out, 1)


def one_bank_slots(ps, first, n):
    return [ps[:, first + i:first + i + 1, :] for i in range(n)]


def two_bank_slots(ps, first, n):
    return [ps[:, first + 2 * i:first + 2 * i + 2, :] for i in range(n)]


def pieces(w, tiles, cols):
    return [w[n * P:(n + 1) * P, 0:cols] for n in range(tiles)]


class Conv:

    def __init__(self, kit, src, acc):
        self.kit, self.src, self.acc = kit, src, acc
        self.taps = [0] * CT
        self.last = [0] * CT

    def new_stage(self):
        self.last = [0] * CT

    def run(self, dve, own, m, there=CT):
        for _ in range(m):
            left = [c for c in range(there) if self.taps[c] < CK]
            if not left:
                return
            c = left[sum(self.taps) % len(left)]
            k = self.taps[c]
            src, acc = self.src[:, c, NMETA + k:NMETA + k + SEQ], self.acc[:, c, :]
            w = self.kit.gain("conv_w", k * CT + c)
            if self.last[c]:
                dve.wait_ge(own.sem, self.last[c])
            if k:
                ins = dve.scalar_tensor_tensor(out=acc, in0=src, scalar=w, in1=acc, op0=ALU.mult, op1=ALU.add)
            else:
                ins = dve.tensor_scalar(acc, src, w, self.kit.gain("conv_b", c), ALU.mult, ALU.add)
            own.step(ins)
            self.taps[c], self.last[c] = k + 1, own.n


def front(kit, out):
    nc, t = kit.nc, kit.t
    with Stage(kit, "front") as st:
        ps = st.banks()
        hn = out["hn"]
        conv_in, conv = out["conv_in"], out["conv"]
        sig = st.sb("sig", [P, 2, T1])
        cq = st.sb("cq", [P, 2, SEQ])
        cqn = Split(st.sb("cq_hi", [P, 2, SEQ], F32R), st.sb("cq_lo", [P, 2, SEQ], F32R))
        ckv = st.sb("ckv", [P, T1])
        cos = st.sb("cos", [P, T1])
        sin = st.sb("sin", [P, T1])
        wkv = st.sb("wkv", [P, HEADS * (NOPE + VH)])
        rot = st.sb("rot", [P, 2, T1])
        kr = st.sb("kr", [ROPE, T1])
        side = st.sem("side_loaded")

        def halves(k):
            return [hn.pair(slice(None), k, slice(0, HT)), hn.pair(slice(None), k, slice(HT, T1))]

        mix = Norm(st, "mix", lambda j: kit.hT[:, j, :], None, DT, T1, EPS1,
                   lambda j: kit.gain("g_mix_norm", j), ps[:, 6:8, :], 2, need=([kit.loaded[j // 2] for j in range(DT)], lambda j: 16),
                   split=(hn, lambda j: (slice(None), j)))
        qn = Norm(st, "qn", lambda j: cq[:, j, :], None, 2, SEQ, EPS1,
                  lambda j: kit.gain("g_q", j), ps[:, 6:7, :], 1, need=(st.sem("cq_copied"), lambda j: j + 1),
                  bufs=mix.bufs, split=(cqn, lambda j: (slice(None), j)))
        kn = Norm(st, "kn", lambda j: ckv[:, :], lambda j: ckv[:, :], 1, T1, EPS1,
                  lambda j: kit.gain("g_kv", 0), ps[:, 6:8, :], 2, need=(st.sem("ckv_copied"), lambda j: 1),
                  bufs=mix.bufs)
        cq_copied, ckv_copied = qn.need[0], kn.need[0]

        tiles = []
        for c in range(CT):
            tiles.append(tile(("b", c), halves, need=(mix.out, lambda k: k + 1)))
            tiles.append(tile(("a", c), halves))
        tiles.append(tile(("ckv", 0), halves))
        tiles.append(tile(("krope", 0), halves))
        for c in range(2):
            tiles.append(tile(("cq", c), lambda k: [hn.pair(slice(None), k, slice(NMETA, T1))]))
        for c in range(8):
            tiles.append(tile(("q", c), lambda k: [cqn.pair(slice(None), k)], ks=2, need=(qn.out, lambda k: k + 1)))
        lin = split_linear(st, two_bank_slots(ps, 0, 3), tiles, 3, D,
                           pieces(t["w_ab"], 2 * CT, D) + pieces(t["w_ckv"], 1, D) + [t["w_krope"][:, :]]
                           + pieces(t["w_cq"], 2, D) + pieces(t["w_uq"], 8, 2 * P))
        n_before_q = lin.index[("q", 0)]

        gated = st.sem("gated")
        sig_done = st.sem("sig_done")
        padded = st.sem("padded")
        kv_done = st.sem("kv_done")
        kv_free = st.sem("kv_free")
        kr_done = st.sem("kr_done")
        kr_spread = st.sem("kr_spread")
        act_steps = st.sem("act_steps")

        with nc.Block() as block:

            @block.sync
            def _(sp):
                for i in range(DT // 2):
                    sp.dma_start(kit.hT[:, 2 * i:2 * i + 2, :], t["hT0"][:, 2 * i * T1:2 * (i + 1) * T1]
                                 .rearrange("p (j n) -> p j n", j=2)).then_inc(kit.loaded[i], 16)
                sp.dma_start(kit.gains[:, :], t["gains"]).then_inc(side, 16)
                lin.ring.load_first(sp)
                sp.dma_start(kit.ident[:, :], t["c_ident"]).then_inc(side, 16)
                sp.dma_start(kit.tri[:, :], t["c_tri"]).then_inc(side, 16)
                sp.dma_start(cos[:, :], t["c_cos"]).then_inc(side, 16)
                sp.dma_start(sin[:, :], t["c_sin"]).then_inc(side, 16)
                sp.dma_start(wkv[:, :], t["w_ukv"]).then_inc(side, 16)
                lin.ring.load_all(sp)

            @block.tensor
            def _(pe):
                pe.wait_ge(kit.made, 1)
                mix.on_pe(pe)
                lin.run(pe, lambda n: n < n_before_q)
                pe.wait_ge(mix.var, 1)
                kn.on_pe(pe)
                pe.wait_ge(kn.var, 1)
                qn.on_pe(pe)
                lin.run(pe, lambda n: n >= n_before_q)
                pe.wait_ge(kn.out, 1)
                pe.wait_ge(side, 96)
                for s in range(3):
                    pe.wait_ge(lin.free[s], len([n for n in range(len(tiles)) if n % 3 == s]))
                for c in range(HEADS // 2):
                    if c >= 2:
                        pe.wait_ge(kv_free, c - 1)
                    for half in range(2):
                        mm = pe.matmul(ps[:, 2 * (c % 2) + half, 0:HT], wkv[:, c * P:(c + 1) * P],
                                       ckv[:, half * HT:(half + 1) * HT], start=True, stop=True)
                    mm.then_inc(kv_done, 1)
                pe.wait_ge(kv_free, HEADS // 2)
                for j in range(ST + 1):
                    if j >= 2:
                        pe.wait_ge(kv_free, HEADS // 2 + j - 1)
                    lo, m = (NMETA + j * P, P) if j < ST else (0, NMETA)
                    pe.matmul(ps[0:m, j % 2, 0:CC], ckv[:, lo:lo + m], wkv[:, HEADS * NOPE:],
                              start=True, stop=True).then_inc(kv_done, 1)

            @block.scalar
            def _(act):
                mix.on_act(act, lambda: lin.ring.round_to(act, 2))
                for c in range(CT):
                    slot, free = rounding(lin, act, ("b", c))
                    if c >= 2:
                        act.wait_ge(gated, c - 1)
                    act.activation(sig[:, c % 2, :].rearrange("p (a b) -> p a b", a=2), slot[:, :, 0:HT],
                                   ACT.Sigmoid).then_inc(sig_done, 1)
                    act.wait_ge(sig_done, c + 1)
                    act.nop().then_inc(free, 1)
                slot, free = rounding(lin, act, ("ckv", 0))
                act.activation(ckv[:, :].rearrange("p (a b) -> p a b", a=2), slot[:, :, 0:HT],
                               ACT.Copy).then_inc(ckv_copied, 1)
                act.wait_ge(ckv_copied, 1)
                act.nop().then_inc(free, 1)
                for c in range(2):
                    slot, free = rounding(lin, act, ("cq", c))
                    act.activation(cq[:, c, :], slot[:, 0, :], ACT.Copy).then_inc(cq_copied, 1)
                    act.wait_ge(cq_copied, c + 1)
                    act.nop().then_inc(free, 1)
                kn.on_act(act)
                qn.on_act(act)
                for c in range(4):
                    slot, free = rounding(lin, act, ("q", c))
                    for e in range(2):
                        act.activation(out["qT"][0:NOPE, 2 * c + e, :], slot[e * NOPE:(e + 1) * NOPE, 0, :],
                                       ACT.Copy).then_inc(act_steps, 1)
                    act.wait_ge(act_steps, 2 * (c + 1))
                    act.nop().then_inc(free, 1)
                lin.ring.round_to(act, len(tiles))
                for c in range(HEADS // 2):
                    act.wait_ge(kv_done, c + 1)
                    for e in range(2):
                        act.activation(out["kT"][0:NOPE, 2 * c + e, :].rearrange("p (a b) -> p a b", a=2),
                                       ps[e * NOPE:(e + 1) * NOPE, 2 * (c % 2):2 * (c % 2) + 2, 0:HT],
                                       ACT.Copy).then_inc(act_steps, 1)
                    act.wait_ge(act_steps, 8 + 2 * (c + 1))
                    act.nop().then_inc(kv_free, 1)
                for j in range(ST + 1):
                    act.wait_ge(kv_done, HEADS // 2 + j + 1)
                    m = P if j < ST else NMETA
                    act.activation(out["v"][0:m, j, :], ps[0:m, j % 2, :], ACT.Copy).then_inc(kv_free, 1)
                act.wait_ge(kr_done, 1)
                for h in range(HEADS):
                    act.activation(out["kT"][NOPE:DQ, h, :], kr[:, :], ACT.Copy).then_inc(kr_spread, 1)

            @block.gpsimd
            def _(pool):
                pool.memset(kit.ones[:, :], 1.0).then_inc(kit.made, 1)
                pool.memset(conv_in[:, :, 0:CK - 1], 0.0).then_inc(padded, 1)
                lin.ring.split_all(pool)

            own_sem = st.sem("vector_steps")

            @block.vector
            def _(dve):
                own = Count(dve, own_sem)
                mix.variance(dve)
                dve.wait_ge(side, 96)
                mix.finish(dve, own)
                dve.wait_ge(padded, 1)
                for c in range(CT):
                    slot, free = lin.arrived(dve, ("a", c))
                    dve.wait_ge(sig_done, c + 1)
                    dve.tensor_tensor(conv_in[:, c, CK - 1:].rearrange("p (a b) -> p a b", a=2), slot[:, :, 0:HT],
                                      sig[:, c % 2, :].rearrange("p (a b) -> p a b", a=2), ALU.mult).then_inc(gated, 1)
                    dve.wait_ge(gated, c + 1)
                    dve.nop().then_inc(free, 1)
                    conv.run(dve, own, 14, c + 1)
                slot, free = lin.arrived(dve, ("krope", 0))
                for e, tab in enumerate((cos, sin)):
                    own.step(dve.tensor_tensor(
                        rot[0:ROPE, e, :].rearrange("p (a b) -> p a b", a=2), slot[e * ROPE:(e + 1) * ROPE, :, 0:HT],
                        tab[0:ROPE, :].rearrange("p (a b) -> p a b", a=2), ALU.mult))
                own.wait()
                dve.nop().then_inc(free, 1)
                own.step(dve.tensor_tensor(kr[:, :], rot[0:ROPE, 0, :], rot[0:ROPE, 1, :], ALU.add))
                own.wait()
                dve.nop().then_inc(kr_done, 1)
                conv.run(dve, own, 12)
                kn.on_dve(dve, own)
                qn.on_dve(dve, own)
                for c in range(2):
                    for e, tab in enumerate((cos, sin)):
                        slot, free = lin.arrived(dve, ("q", 4 + 2 * c + e))
                        own.link(dve.tensor_tensor(rot[:, e, 0:SEQ], slot[:, 0, :], tab[:, NMETA:T1], ALU.mult))
                        dve.nop().then_inc(free, 1)
                    for a in range(4):
                        own.step(dve.tensor_tensor(out["qT"][NOPE:DQ, 4 * c + a, :], rot[a * ROPE:(a + 1) * ROPE, 0, 0:SEQ],
                                                   rot[a * ROPE:(a + 1) * ROPE, 1, 0:SEQ], ALU.add))
                    own.wait()
                conv.run(dve, own, 16)
                own.wait()


class Attention:

    def __init__(self, st, items, s_slots, pt_slots, o_slots, pcols, flush, lag=2, negated=False):
        self.items, self.st = items, st
        self.ident = st.kit.ident
        self.S, self.PT, self.O, self.flush = s_slots, pt_slots, o_slots, flush
        self.lag, self.negated = lag, negated
        self.R = lag + 2
        self.pr = st.sb("probs", [P, self.R, pcols])
        self.pts = st.sb("probsT", [P, 3, pt_slots[0].shape[-1]])
        n = len(items)
        self.mx = st.sb("mx", [P, 4])
        self.nm = st.sb("nm", [P, 4])
        self.ls = st.sb("ls", [P, 4])
        self.rl = st.sb("rl", [P, 4])
        names = ("scored", "maxed", "exped", "scaled", "turned", "copied", "summed", "flushed", "steps", "extra")
        self.s = {k: st.sem(k) for k in names}
        self.last = {}
        for i, it in enumerate(items):
            self.last[it["bank"]] = i

    def on_pe(self, pe, between=None):
        it, s, n_items = self.items, self.s, len(self.items)
        for n in range(n_items + self.lag + 1):
            if n < n_items:
                x = it[n]
                if n >= len(self.S):
                    pe.wait_ge(s["exped"], n - len(self.S) + 1)
                for keys, col in x["ks"]:
                    mm = pe.matmul(self.S[n % len(self.S)][:, col:col + keys.shape[-1]], x["q"], keys,
                                   start=True, stop=True)
                mm.then_inc(s["scored"], 1)
            if self.lag <= n < n_items + self.lag:
                m = n - self.lag
                x = it[m]
                pe.wait_ge(s["scaled"], m + 1)
                if m >= len(self.PT):
                    pe.wait_ge(s["copied"], m - len(self.PT) + 1)
                pr = self.pr[:, m % self.R, :]
                for j, (col, w, _) in enumerate(x["pts"]):
                    mm = pe.transpose(self.PT[m % len(self.PT)][0:w, j * P:(j + 1) * P], pr[:, col:col + w],
                                      self.ident[:, :])
                mm.then_inc(s["turned"], 1)
            if n >= self.lag + 1:
                m = n - self.lag - 1
                x = it[m]
                pe.wait_ge(s["copied"], m + 1)
                b = x["bank"]
                if b >= len(self.O) and (m == 0 or it[m - 1]["bank"] != b):
                    pe.wait_ge(s["flushed"], b - len(self.O) + 1)
                pt = self.pts[:, m % 3, :]
                for j, (_, w, v) in enumerate(x["pts"]):
                    mm = pe.matmul(x["out"](self.O[b % len(self.O)]), v, pt[0:w, j * P:(j + 1) * P],
                                   start=(x["start"] and j == 0), stop=(x["stop"] and j == len(x["pts"]) - 1))
                mm.then_inc(s["summed"], 1)
            if between is not None:
                between(n)

    def on_act(self, act, between=None):
        it, s, n_items = self.items, self.s, len(self.items)
        for n in range(n_items + self.lag):
            if n < n_items:
                x = it[n]
                act.wait_ge(s["maxed"], n + 1)
                if n >= self.R:
                    act.wait_ge(s["turned"], n - self.R + 1)
                act.activation(self.pr[:, n % self.R, 0:x["hi"] - x["lo"]], self.S[n % len(self.S)][:, x["lo"]:x["hi"]],
                               ACT.Exp, bias=self.nm[:, n % 4:n % 4 + 1], scale=x["scale"],
                               accum_out=self.ls[:, n % 4:n % 4 + 1]).then_inc(s["exped"], 1)
            if n >= self.lag:
                m = n - self.lag
                x = it[m]
                act.wait_ge(s["turned"], m + 1)
                if m >= 3:
                    act.wait_ge(s["summed"], m - 2)
                runs = []
                for j, (_, w, _) in enumerate(x["pts"]):
                    if runs and runs[-1][2] == w:
                        runs[-1][1] = j + 1
                    else:
                        runs.append([j, j + 1, w])
                for i, (a, b, w) in enumerate(runs):
                    c = act.activation(self.pts[0:w, m % 3, a * P:b * P],
                                       self.PT[m % len(self.PT)][0:w, a * P:b * P], ACT.Copy)
                    if i < len(runs) - 1:
                        c.then_inc(s["extra"], 1)
                        self.extra = self.extra + 1
                        act.wait_ge(s["extra"], self.extra)
                c.then_inc(s["copied"], 1)
            if between is not None:
                between(n)

    extra = 0

    def on_dve(self, dve, between=None):
        it, s, n_items = self.items, self.s, len(self.items)
        own = Count(dve, s["steps"])
        back = self.lag - 1
        for n in range(n_items + self.lag + 3):
            m = n - back
            if n < n_items:
                x = it[n]
                S = self.S[n % len(self.S)]
                dve.wait_ge(s["scored"], n + 1)
                col, mask = x["mask"]
                own.step(dve.tensor_tensor(S[:, col:col + mask.shape[-1]], S[:, col:col + mask.shape[-1]], mask,
                                           ALU.add))
                masked = own.n
            if 0 <= m < n_items:
                c = slice(m % 4, m % 4 + 1)
                dve.wait_ge(s["exped"], m + 1)
                own.step(dve.reciprocal(self.rl[:, c], self.ls[:, c]))
                turned_over = own.n
            if n < n_items:
                cn = slice(n % 4, n % 4 + 1)
                dve.wait_ge(own.sem, masked)
                if self.negated:
                    dve.tensor_reduce(self.nm[:, cn], S[:, x["lo"]:x["hi"]], AX, ALU.min).then_inc(s["maxed"], 1)
                else:
                    own.link(dve.tensor_reduce(self.mx[:, cn], S[:, x["lo"]:x["hi"]], AX, ALU.max))
                    dve.tensor_scalar(self.nm[:, cn], self.mx[:, cn], -x["scale"], None, ALU.mult)\
                       .then_inc(s["maxed"], 1)
            if 0 <= m < n_items:
                y = it[m]
                dve.wait_ge(own.sem, turned_over)
                pr = self.pr[:, m % self.R, 0:y["hi"] - y["lo"]]
                if y["gate"] is None:
                    dve.tensor_scalar(pr, pr, self.rl[:, c], None, ALU.mult).then_inc(s["scaled"], 1)
                else:
                    dve.tensor_scalar(pr, pr, self.rl[:, c], y["gate"], ALU.mult, ALU.mult).then_inc(s["scaled"], 1)
            for b, i in self.last.items():
                if i + self.lag + 2 == n:
                    dve.wait_ge(s["summed"], i + 1)
                    self.flush(dve, b, self.O[b % len(self.O)]).then_inc(s["flushed"], 1)
            if between is not None:
                between(n)


def mla(kit, io):
    nc = kit.nc
    with Stage(kit, "mla") as st:
        ps = st.banks()
        flat = ps[:, :, :].rearrange("p b n -> p (b n)")
        attn = st.sb("attnT", [P, CT, SEQ])
        items = []
        off = 512 - NMETA
        for hp in range(HEADS // 2):
            for j in range(ST):
                for h in (2 * hp, 2 * hp + 1):
                    keys = (j + 1) * P
                    items.append(dict(
                        q=io["qT"][:, h, j * P:(j + 1) * P],
                        ks=[(io["kT"][:, h, 0:NMETA], off), (io["kT"][:, h, NMETA:NMETA + keys], 512)],
                        lo=off, hi=512 + keys, mask=(512 + j * P, kit.tri[:, :]),
                        pts=[(NMETA + i * P, P, io["v"][:, i, h * VH:(h + 1) * VH]) for i in range(j + 1)]
                        + [(0, NMETA, io["v"][0:NMETA, ST, h * VH:(h + 1) * VH])],
                        out=lambda o, e=h % 2, j=j: o[e * VH:(e + 1) * VH, j * P:(j + 1) * P],
                        bank=hp, start=True, stop=True, scale=DQ ** -0.5, gate=None))
        at = Attention(st, items, [flat[:, 0:1024], flat[:, 1024:2048]], [flat[:, 2048:2048 + 640]],
                       [ps[:, 7, :]], T1,
                       lambda dve, b, o: dve.tensor_copy(attn[:, b, :], o))
        an = Norm(st, "an", lambda j: attn[:, j, :], lambda j: io["mixT"][:, j, :], CT, SEQ, EPS1,
                  lambda j: kit.gain("g_out_attn", j), ps[:, 0:1, :], 1, need=(at.s["flushed"], lambda j: j + 1))
        conv, acc = io["conv"], io["mixT"][:, CT:2 * CT, :]
        mu = st.sb("mu", [P, SEQ])
        conv_done, ln_sum, centred, silu_done = (st.sem(n) for n in ("conv_done", "ln_sum", "centred", "silu_done"))
        ln = Norm(st, "ln", lambda j: acc[:, j, :], lambda j: acc[:, j, :], CT, SEQ, EPS1,
                  lambda j: 1.0, ps[:, 6:7, :], 1, need=(centred, lambda j: j + 1))
        cn = Norm(st, "cn", lambda j: acc[:, j, :], lambda j: acc[:, j, :], CT, SEQ, EPS1,
                  lambda j: kit.gain("g_out_conv", j), ps[:, 6:7, :], 1, need=(silu_done, lambda j: j + 1))
        own_sem, conv_sem = st.sem("vector_steps"), st.sem("conv_steps")
        conv_steps = 21
        per_step = -(-(CK * CT - sum(conv.taps)) // conv_steps)
        first = conv_steps + 1
        with nc.Block() as block:

            @block.tensor
            def _(pe):
                def mean():
                    pe.wait_ge(conv_done, 1)
                    for c in range(CT):
                        mm = pe.matmul(ps[:, 6, :], kit.ones[:, :], acc[:, c, :], start=(c == 0), stop=(c == CT - 1))
                    mm.then_inc(ln_sum, 1)

                def sum_cn():
                    pe.wait_ge(ln.var, 1)
                    cn.on_pe(pe)

                def sum_ln():
                    pe.wait_ge(centred, 1)
                    ln.on_pe(pe)

                steps = {first: mean, first + 3: sum_ln, first + 9: sum_cn}
                at.on_pe(pe, lambda n: steps[n]() if n in steps else None)
                an.on_pe(pe)

            @block.scalar
            def _(act):
                def silu():
                    for c in range(CT):
                        act.wait_ge(ln.out, c + 1)
                        act.activation(acc[:, c, :], acc[:, c, :], ACT.Silu, bias=kit.gain("b_conv_ln", c),
                                       scale=kit.gain("g_conv_ln", c)).then_inc(silu_done, 1)
                    cn.squares(act)

                steps = {first + 2: lambda: ln.squares(act), first + 5: lambda: ln.take_root(act), first + 8: silu,
                         first + 11: lambda: cn.take_root(act)}
                at.on_act(act, lambda n: steps[n]() if n in steps else None)
                an.on_act(act)

            @block.vector
            def _(dve):
                own, taps = Count(dve, own_sem), Count(dve, conv_sem)
                conv.new_stage()

                def centre():
                    dve.wait_ge(ln_sum, 1)
                    own.link(dve.tensor_scalar(mu[:, :], ps[:, 6, :], 1.0 / CC, None, ALU.mult))
                    for c in range(CT):
                        dve.tensor_tensor(acc[:, c, :], acc[:, c, :], mu[:, :], ALU.subtract).then_inc(centred, 1)
                    dve.wait_ge(centred, CT)

                steps = {first + 1: centre, first + 4: lambda: ln.variance(dve), first + 6: lambda: ln.finish(dve, own),
                         first + 10: lambda: cn.variance(dve), first + 12: lambda: cn.finish(dve, own)}

                def between(n):
                    if n < conv_steps:
                        conv.run(dve, taps, per_step)
                    if n == conv_steps:
                        taps.wait()
                        dve.nop().then_inc(conv_done, 1)
                    if n in steps:
                        steps[n]()

                at.on_dve(dve, between)
                an.on_dve(dve, own)


def route(kit, io):
    nc, t = kit.nc, kit.t
    NS = 2 * PH
    with Stage(kit, "route") as st:
        ps = st.banks()
        keys = st.sb("keys", [P, PH, NK])
        qT = st.sb("qT", [P, PH, SEQ])
        sc = st.sb("scores", [P, NS, NK])
        rest = st.sb("rest", [P, NS, NK])
        sv = st.sb("sv", [P, PH, 2, TOPK])
        si = st.sb("si", [P, NS, TOPK], U32)
        sif = st.sb("sif", [P, 2, TOPK, PH], F16)
        cand = st.sb("cand", [P, PH, NCAND])
        left = rest[:, :, :].rearrange("p (h a) n -> p h (a n)", a=2)[:, :, 0:NCAND]
        tops = st.sb("tops", [P, PH, TOPK])
        sel = st.sb("sel", [P, PH, TOPK], U32)
        ab = st.sb("ab", [P, 4, PH * TOPK], U32)
        abf = st.sb("abf", [P, 4, PH * TOPK])
        second = st.sb("second", [P, PH * TOPK])
        ab16 = st.sb("ab16", [P, 2, TOPK, PH], F16)
        eq = st.sb("eq", [P, 2, TOPK, TOPK * PH], F16)
        three = st.sb("three", [P, 3, PH * TOPK])
        tot = st.sb("tot", [P, PH])
        places = st.sb("places", [P, TOPK, TOPK * PH], F16)
        mix = Split(st.sb("mix_hi", [P, 2 * CT, SEQ], F32R), st.sb("mix_lo", [P, 2 * CT, SEQ], F32R))
        mix_split = st.sem("mix_split")
        side = st.sem("side_loaded")
        hsum = st.sem("residual_added")
        q_copied = st.sem("q_copied")
        scored = st.sem("scored")
        s_copied = st.sem("s_copied")
        s_used = st.sem("s_used")
        shifted = st.sem("shifted")
        exped = st.sem("exped")
        ready = st.sem("gates_ready")
        turned = st.sem("turned")
        own_sem = st.sem("vector_steps")
        fin_sem = st.sem("turned_copied")

        fn = Norm(st, "fn", lambda j: kit.real(j), None, DT, SEQ, EPS1,
                  lambda j: kit.gain("g_ffn_norm", j), ps[:, 4:5, :], 1, need=(hsum, lambda j: j + 1),
                  split=(io["xn"], lambda j: (slice(None), j)))
        tiles = [tile(("o", n), lambda k: [mix.pair(slice(None), k)], need=(mix_split, lambda k: k + 1)) for n in range(DT)]
        tiles += [tile(("q", n), lambda k: [io["xn"].pair(slice(None), k)], need=(fn.out, lambda k: k + 1))
                  for n in range(DT)]
        lin = split_linear(st, one_bank_slots(ps, 0, 4), tiles, 3, D,
                           pieces(t["w_out"], DT, D) + pieces(t["peer_wq"], DT, D))
        with nc.Block() as block:

            @block.sync
            def _(sp):
                lin.ring.load_first(sp)
                sp.dma_start(keys[:, :, :], t["peer_keys"].rearrange("p (h n) -> p h n", h=PH)).then_inc(side, 16)
                sp.dma_start(places[:, :, :], t["c_places"].rearrange("p (a n) -> p a n", a=TOPK)).then_inc(side, 16)
                lin.ring.load_all(sp)

            @block.gpsimd
            def _(pool):
                lin.ring.split_all(pool)

            @block.tensor
            def _(pe):
                lin.run(pe, lambda n: n < DT)
                fn.on_pe(pe)
                lin.run(pe, lambda n: n >= DT)
                pe.wait_ge(side, 32)
                pe.wait_ge(q_copied, DT)
                for j in range(ST + 1):
                    if 0 < j < ST:
                        pe.wait_ge(s_copied, 4 * j)
                    for h in range(PH if j < ST else 0):
                        for half in range(2):
                            lo = half * (P // 2)
                            bank = 2 * half + h // 4
                            mm = pe.matmul(ps[:, bank, (h % 4) * NK:(h % 4 + 1) * NK],
                                           qT[lo:lo + P // 2, h, j * P:(j + 1) * P], keys[lo:lo + P // 2, h, :],
                                           start=True, stop=True)
                    if j < ST:
                        mm.then_inc(scored, 1)
                    if j:
                        pe.wait_ge(ready, j)
                        for i in range(3):
                            mm = pe.transpose(ps[:, 5 + i, (j - 1) * P:j * P], three[:, i, :], kit.ident[:, :])
                        mm.then_inc(turned, 1)

            @block.scalar
            def _(act):
                lin.ring.round_to(act, DT)
                fn.on_act(act, lambda: lin.ring.round_to(act, DT + 2))
                for n in range(DT):
                    slot, free = rounding(lin, act, ("q", n))
                    act.activation(qT[:, n, :], slot[:, 0, :], ACT.Copy).then_inc(q_copied, 1)
                    act.wait_ge(q_copied, n + 1)
                    act.nop().then_inc(free, 1)
                for j in range(ST + 1):
                    if j < ST:
                        act.wait_ge(scored, j + 1)
                        if j:
                            act.wait_ge(s_used, j)
                    for bank in range(4 if j < ST else 0):
                        half, h0 = bank // 2, 4 * (bank % 2)
                        act.activation(sc[:, :, :].rearrange("p (h a) n -> p h a n", a=2)[:, h0:h0 + 4, half, :],
                                       ps[:, bank, :].rearrange("p (h n) -> p h n", h=4), ACT.Copy)\
                            .then_inc(s_copied, 1)
                    if j:
                        act.wait_ge(shifted, j)
                        act.activation(tops[:, :, :], tops[:, :, :], ACT.Exp).then_inc(exped, 1)

            @block.vector
            def _(dve):
                own = Count(dve, own_sem)
                mix.write_all(dve, own, io["mixT"], DT, mix_split)
                for n in range(DT):
                    slot, free = lin.arrived(dve, ("o", n))
                    dve.tensor_tensor(kit.real(n), kit.real(n), slot[:, 0, :], ALU.add).then_inc(hsum, 1)
                    dve.wait_ge(hsum, n + 1)
                    dve.nop().then_inc(free, 1)
                fn.on_dve(dve, own)
                dve.wait_ge(side, 32)
                svf = sv[:, :, :, :].rearrange("p h a k -> p (h a) k")
                for j in range(ST):
                    dve.wait_ge(s_copied, 4 * (j + 1))
                    for i in range(NS):
                        own.step(dve.max(svf[:, i, 0:8], sc[:, i, :]))
                    own.wait()
                    for i in range(NS):
                        own.step(dve.max_index(si[:, i, 0:8], svf[:, i, 0:8], sc[:, i, :]))
                        own.step(dve.match_replace(rest[:, i, :], svf[:, i, 0:8], sc[:, i, :], -3e38))
                    own.wait()
                    dve.nop().then_inc(s_used, 1)
                    for i in range(NS):
                        own.step(dve.max(svf[:, i, 8:16], rest[:, i, :]))
                    own.wait()
                    for i in range(NS):
                        own.step(dve.max_index(si[:, i, 8:16], svf[:, i, 8:16], rest[:, i, :]))
                    own.wait()
                    own.step(dve.tensor_copy(sif[:, :, :, :].rearrange("p i a h -> p h i a"),
                                             si[:, :, :].rearrange("p (h i) a -> p h i a", i=2)))
                    for c0, c1, a0, a1, b in ((0, TOP4 * TOPK, 0, TOP4, TOPK), (TOP4 * TOPK, NCAND, TOP4, TOPK, TOP4)):
                        own.step(dve.tensor_tensor(
                            cand[:, :, c0:c1].rearrange("p h (a b) -> p h a b", b=b),
                            sv[:, :, 0, a0:a1].unsqueeze(3).to_broadcast([P, PH, a1 - a0, b]),
                            sv[:, :, 1, 0:b].unsqueeze(2).to_broadcast([P, PH, a1 - a0, b]), ALU.add))
                    own.wait()
                    for h in range(PH):
                        own.step(dve.max(tops[:, h, 0:8], cand[:, h, :]))
                    own.wait()
                    for h in range(PH):
                        own.step(dve.max_index(sel[:, h, 0:8], tops[:, h, 0:8], cand[:, h, :]))
                        own.step(dve.match_replace(left[:, h, :], tops[:, h, 0:8], cand[:, h, :], -3e38))
                    own.wait()
                    for h in range(PH):
                        own.step(dve.max(tops[:, h, 8:16], left[:, h, :]))
                    own.wait()
                    for h in range(PH):
                        own.step(dve.max_index(sel[:, h, 8:16], tops[:, h, 8:16], left[:, h, :]))
                    own.step(dve.tensor_copy(tot[:, :], tops[:, :, 0]))
                    own.wait()
                    dve.tensor_tensor(tops[:, :, :], tops[:, :, :], tot[:, :].unsqueeze(2).to_broadcast([P, PH, TOPK]),
                                      ALU.subtract).then_inc(shifted, 1)
                    picked = sel[:, :, :].rearrange("p h k -> p (h k)")
                    for i, (amount, op) in enumerate(((4, ALU.logical_shift_right), (15, ALU.bitwise_and),
                                                      (2, ALU.logical_shift_right), (3, ALU.bitwise_and))):
                        own.step(dve.tensor_scalar(ab[:, i, :], picked, amount, None, op))
                    own.wait()
                    own.link(dve.tensor_copy(abf[:, :, :], ab[:, :, :]))
                    own.step(dve.tensor_scalar(second[:, :], abf[:, 0, :], float(TOP4), None, ALU.is_ge))
                    own.step(dve.tensor_scalar(abf[:, 2, :], abf[:, 2, :], float(TOP4 - TOPK), None, ALU.add))
                    own.wait()
                    own.link(dve.tensor_tensor(abf[:, 2:4, :], abf[:, 2:4, :], abf[:, 0:2, :], ALU.subtract))
                    own.link(dve.tensor_tensor(abf[:, 2:4, :], abf[:, 2:4, :],
                                               second[:, :].unsqueeze(1).to_broadcast([P, 2, PH * TOPK]), ALU.mult))
                    own.link(dve.tensor_tensor(ab16[:, :, :, :].rearrange("p i k h -> p i h k"),
                                               abf[:, 0:2, :].rearrange("p i (h k) -> p i h k", h=PH),
                                               abf[:, 2:4, :].rearrange("p i (h k) -> p i h k", h=PH), ALU.add))
                    if j:
                        dve.wait_ge(turned, j)
                    for i in range(2):
                        own.step(dve.tensor_tensor(
                            eq[:, i, :, :], ab16[:, i, :, :].rearrange("p k h -> p (k h)").unsqueeze(1)
                            .to_broadcast([P, TOPK, TOPK * PH]), places[:, :, :], ALU.is_equal))
                    own.wait()
                    for i in range(2):
                        e = eq[:, i, :, :].rearrange("p a (k h) -> p a k h", h=PH)
                        own.step(dve.tensor_tensor(
                            e, e, sif[:, i, :, :].unsqueeze(2).to_broadcast([P, TOPK, TOPK, PH]), ALU.mult))
                    own.wait()
                    for a in (8, 4, 2):
                        own.link(dve.tensor_tensor(eq[:, :, 0:a, :], eq[:, :, 0:a, :], eq[:, :, a:2 * a, :], ALU.add))
                    own.link(dve.tensor_tensor(three[:, 0:2, :], eq[:, :, 0, :], eq[:, :, 1, :], ALU.add))
                    dve.wait_ge(exped, j + 1)
                    own.link(dve.tensor_reduce(tot[:, :], tops[:, :, :], AX, ALU.add))
                    own.link(dve.reciprocal(tot[:, :], tot[:, :]))
                    dve.scalar_tensor_tensor(
                        out=three[:, 2, :].rearrange("p (k h) -> p h k", h=PH), in0=tops[:, :, :], scalar=GSCALE,
                        in1=tot[:, :].unsqueeze(2).to_broadcast([P, PH, TOPK]), op0=ALU.mult, op1=ALU.mult)\
                        .then_inc(ready, 1)
                    dve.wait_ge(ready, j + 1)
                dve.wait_ge(turned, ST)
                for i in range(2):
                    own.step(dve.tensor_copy(io["idx"][:, i, :], ps[:, 5 + i, :]))
                own.link(dve.tensor_copy(io["gate"][:, 0, :], ps[:, 7, :]))
                own.link(dve.tensor_tensor(io["gate"][:, 1, :], ps[:, 7, :], io["gate"][:, 0, :], ALU.subtract))


CHUNKS = NK
PARTS = 4
PCH = CHUNKS // PARTS
TB = SEQ // PCH
GRP = 2


def experts(kit, io):
    nc, t = kit.nc, kit.t
    with Stage(kit, "experts") as st:
        ps = st.banks()
        xn, idx, gate = io["xn"], io["idx"], io["gate"]
        G = st.sb("gates", [P, PCH * SEQ])
        U = st.sb("u", [P, D])
        Us = Split(st.sb("u_hi", [P, 2, D], F32R), st.sb("u_lo", [P, 2, D], F32R))
        V = st.sb("v", [P, D])
        VS = 3
        Vs = Split(st.sb("v_hi", [P, VS, D], F32R), st.sb("v_lo", [P, VS, D], F32R))
        W = st.sb("w", [P, 2, SEQ])
        WS = 2 * GRP
        Ws = Split(st.sb("w_hi", [P, WS, SEQ], F32R), st.sb("w_lo", [P, WS, SEQ], F32R))
        O2 = st.sb("second_hot", [P, 2, NK, TB], F16)
        O1 = st.sb("first_hot", [P, 2, 2, PCH, TB], F16)
        E1 = st.sb("first_eq", [P, 2, PCH, TB], F16)
        iota = st.sb("iota", [P, NK, TB], F16)
        side = st.sem("side_loaded")
        u_in, v_in = st.sem("u_in"), st.sem("v_in")
        u_hi, u_lo = st.sem("u_rounded"), st.sem("u_split")
        v_hi, v_lo = st.sem("v_rounded"), st.sem("v_split")
        acted = st.sem("first_done")
        gelued = st.sem("gelued")
        weighed = st.sem("weighed")
        w_hi, w_lo = st.sem("w_rounded"), st.sem("w_split")
        hot = st.sem("hot_made")
        gated = st.sem("gates_summed")
        gcopied = st.sem("gates_copied")
        odone = st.sem("second_done")
        oadded = st.sem("second_added")
        own_sem = st.sem("vector_steps")
        groups = CHUNKS // GRP
        EARLY = 2

        def region(par, n):
            if par == 0:
                return G[:, n * SEQ:(n + 1) * SEQ].rearrange("p (s t) -> p s t", s=PCH)
            return G[:, :].rearrange("p (s n t) -> p s n t", s=PCH, n=PCH)[:, :, n, :]

        with nc.Block() as block:

            @block.sync
            def _(sp):
                sp.dma_start(iota[:, :, :], t["c_iota16"].rearrange("p (k t) -> p k t", t=TB)).then_inc(side, 16)
                for n in range(CHUNKS):
                    if n:
                        sp.wait_ge(u_lo, n)
                    sp.dma_start(U[:, :], t["peer_uT"][n * P:(n + 1) * P, :]).then_inc(u_in, 16)

            def gate_block(pe, b):
                pe.wait_ge(hot, 2 * (b + 1))
                if b >= 2:
                    pe.wait_ge(gcopied, b - 1)
                for i in range(TB):
                    for piece in range(2):
                        mm = pe.matmul(ps[:, 6 + b % 2, i * PCH:(i + 1) * PCH], O2[:, b % 2, :, i],
                                       O1[:, b % 2, piece, :, i], start=(piece == 0), stop=(piece == 1))
                mm.then_inc(gated, 1)

            @block.tensor
            def _(pe):
                def first_product(n, k):
                    if k == 0:
                        pe.wait_ge(u_lo, n + 1)
                        if n >= 3:
                            pe.wait_ge(gelued, n - 2)
                    mm = product(pe, ps[:, n % 3, :], Us.pair(slice(None), n % 2, slice(k * P, (k + 1) * P)),
                                 xn.pair(slice(None), k), k == 0, k == DT - 1)
                    if k == DT - 1:
                        mm.then_inc(acted, 1)

                for b in range(PCH):
                    gate_block(pe, b)
                    if b >= PCH - EARLY * DT:
                        first_product((b - (PCH - EARLY * DT)) // DT, b % DT)
                for g in range(groups + 1):
                    if g < groups:
                        for c in range(GRP):
                            n = g * GRP + c
                            for k in range(DT if n >= EARLY else 0):
                                first_product(n, k)
                            if n < CHUNKS - PCH:
                                gate_block(pe, PCH + n)
                    if g >= 1:
                        q = g - 1
                        pe.wait_ge(v_lo, GRP * g)
                        pe.wait_ge(w_lo, GRP * g)
                        for d in range(DT):
                            m = q * DT + d
                            if m >= 3:
                                pe.wait_ge(oadded, m - 2)
                            for c in range(GRP):
                                n = q * GRP + c
                                mm = product(pe, ps[:, 3 + m % 3, :],
                                             Vs.pair(slice(None), n % VS, slice(d * P, (d + 1) * P)),
                                             Ws.pair(slice(None), n % WS), c == 0, c == GRP - 1)
                            mm.then_inc(odone, 1)

            @block.gpsimd
            def _(pool):
                for n in range(-1, CHUNKS + 1):
                    if n + 1 < CHUNKS:
                        pool.wait_ge(u_hi, n + 2)
                        at = (slice(None), (n + 1) % 2)
                        pool.tensor_tensor(Us.lo[at], U[:, :], Us.hi[at].bitcast(F32), ALU.subtract).then_inc(u_lo, 1)
                    if n >= 1:
                        pool.wait_ge(v_hi, n)
                        at = (slice(None), (n - 1) % VS)
                        pool.tensor_tensor(Vs.lo[at], V[:, :], Vs.hi[at].bitcast(F32), ALU.subtract).then_inc(v_lo, 1)

            @block.scalar
            def _(act):
                def round_u(n):
                    act.wait_ge(u_in, 16 * (n + 1))
                    if n >= 2:
                        act.wait_ge(acted, n - 1)
                    act.activation(Us.hi[:, n % 2, :], U[:, :], ACT.Copy).then_inc(u_hi, 1)

                def load_v(n):
                    if n:
                        act.wait_ge(v_lo, n)
                    act.dma_start(V[:, :], t["peer_v"][n * P:(n + 1) * P, :]).then_inc(v_in, 16)

                def round_v(n):
                    act.wait_ge(v_in, 16 * (n + 1))
                    if n >= VS:
                        act.wait_ge(odone, DT * ((n - VS) // GRP + 1))
                    act.activation(Vs.hi[:, n % VS, :], V[:, :], ACT.Copy).then_inc(v_hi, 1)

                def keep(b, par):
                    act.wait_ge(gated, b + 1)
                    act.activation(region(par, b % PCH), ps[:, 6 + b % 2, :].rearrange("p (t i) -> p i t", i=PCH),
                                   ACT.Copy).then_inc(gcopied, 1)

                for n in range(EARLY):
                    round_u(n)
                for b in range(PCH):
                    keep(b, 1)
                for n in range(CHUNKS + 1):
                    if n >= 1:
                        load_v(n - 1)
                    if EARLY <= n + 1 < CHUNKS:
                        round_u(n + 1)
                    if n < CHUNKS:
                        act.wait_ge(acted, n + 1)
                        if n >= 2:
                            act.wait_ge(w_lo, n - 1)
                        act.activation(W[:, n % 2, :], ps[:, n % 3, :], ACT.Gelu).then_inc(gelued, 1)
                    if n >= 1:
                        round_v(n - 1)
                    if n < CHUNKS - PCH:
                        act.wait_ge(weighed, n + 1)
                        keep(PCH + n, (n // PCH) % 2)

            @block.vector
            def _(dve):
                own = Count(dve, own_sem)
                dve.wait_ge(side, 16)

                def hots(b):
                    part, tb = b // PCH, b % PCH
                    tok = slice(tb * TB, (tb + 1) * TB)
                    if b >= 2:
                        dve.wait_ge(gated, b - 1)
                        dve.wait_ge(hot, 2 * (b - 1))
                    own.step(dve.tensor_tensor(E1[:, b % 2, :, :], iota[:, part * PCH:(part + 1) * PCH, :],
                                               idx[:, 0, tok].unsqueeze(1).to_broadcast([P, PCH, TB]), ALU.is_equal))
                    dve.tensor_tensor(O2[:, b % 2, :, :], iota[:, :, :],
                                      idx[:, 1, tok].unsqueeze(1).to_broadcast([P, NK, TB]),
                                      ALU.is_equal).then_inc(hot, 1)
                    own.wait()
                    dve.tensor_tensor(O1[:, b % 2, :, :, :], E1[:, b % 2, :, :].unsqueeze(1).to_broadcast([P, 2, PCH, TB]),
                                      gate[:, :, tok].unsqueeze(2).to_broadcast([P, 2, PCH, TB]),
                                      ALU.mult).then_inc(hot, 1)

                def weigh(n):
                    dve.wait_ge(gelued, n + 1)
                    dve.wait_ge(gcopied, PCH * (n // PCH + 1))
                    if n >= WS:
                        dve.wait_ge(odone, DT * ((n - WS) // GRP + 1))
                    x = W[:, n % 2, :]
                    w = x.rearrange("p (s t) -> p s t", s=PCH)
                    dve.scalar_tensor_tensor(out=w, in0=region((n // PCH) % 2, n % PCH), scalar=1.0 / GSCALE, in1=w,
                                             op0=ALU.mult, op1=ALU.mult).then_inc(weighed, 1)
                    dve.wait_ge(weighed, n + 1)
                    Ws.write_hi(dve, (slice(None), n % WS), x).then_inc(w_hi, 1)
                    dve.wait_ge(w_hi, n + 1)
                    Ws.write_lo(dve, (slice(None), n % WS), x).then_inc(w_lo, 1)

                def add_group(q):
                    for d in range(DT):
                        m = q * DT + d
                        dve.wait_ge(odone, m + 1)
                        if q:
                            dve.wait_ge(oadded, m - DT + 1)
                        dve.tensor_tensor(kit.real(d), kit.real(d), ps[:, 3 + m % 3, :], ALU.add).then_inc(oadded, 1)

                for b in range(PCH + 1):
                    hots(b)
                for g in range(groups + 1):
                    for c in range(GRP):
                        n = g * GRP + c
                        if g < groups:
                            weigh(n)
                        if g >= 1 and c == GRP - 1:
                            add_group(g - 1)
                        if n + 1 < CHUNKS - PCH:
                            hots(PCH + n + 1)
                dve.wait_ge(oadded, groups * DT)


def short(kit):
    nc, t = kit.nc, kit.t
    with Stage(kit, "short") as st:
        ps = st.banks()
        hn = Split(st.sb("hn_hi", [P, DT, SEQ], F32R), st.sb("hn_lo", [P, DT, SEQ], F32R))
        cbuf = st.sb("c", [P, 2, SEQ])
        cv = st.sb("cv", [P, 2, 2 + SEQ])
        u = Split(st.sb("u_hi", [P, DT, SEQ], F32R), st.sb("u_lo", [P, DT, SEQ], F32R))
        um = st.sb("u", [P, 2, SEQ])
        gf = Norm(st, "gf", kit.real, kit.real, DT, SEQ, EPS1, lambda j: kit.gain("g_final", j), ps[:, 7:8, :], 1)
        an = Norm(st, "an", kit.real, None, DT, SEQ, EPS2, lambda j: kit.gain("a_norm_2", j),
                  ps[:, 7:8, :], 1, need=(gf.out, lambda j: j + 1), bufs=gf.bufs,
                  split=(hn, lambda j: (slice(None), j)))
        padded, copied, mixed, added = st.sem("padded"), st.sem("c_copied"), st.sem("mixed"), st.sem("added")
        own_sem = st.sem("vector_steps")
        tiles = []
        for i in range(DT):
            for part in "cvb":
                tiles.append(tile((part, i), lambda k: [hn.pair(slice(None), k)], need=(an.out, lambda k: k + 1)))
        for n in range(DT):
            tiles.append(tile(("o", n), lambda k: [u.pair(slice(None), k)], need=(mixed, lambda k: k + 1)))
        lin = split_linear(st, one_bank_slots(ps, 0, 7), tiles, 4, D,
                           pieces(t["a_w_in"], 3 * DT, D) + pieces(t["a_w_out"], DT, D))
        with nc.Block() as block:

            @block.sync
            def _(sp):
                lin.ring.load_all(sp)

            @block.gpsimd
            def _(pool):
                pool.memset(cv[:, :, 0:2], 0.0).then_inc(padded, 1)
                lin.ring.split_all(pool)

            @block.tensor
            def _(pe):
                gf.on_pe(pe)
                pe.wait_ge(gf.var, 1)
                an.on_pe(pe)
                lin.run(pe)

            @block.scalar
            def _(act):
                gf.on_act(act)
                an.on_act(act, lambda: lin.ring.round_to(act, 2))
                for i in range(DT):
                    slot, free = rounding(lin, act, ("c", i))
                    if i >= 2:
                        act.wait_ge(mixed, i - 1)
                    act.activation(cbuf[:, i % 2, :], slot[:, 0, :], ACT.Copy).then_inc(copied, 1)
                    act.wait_ge(copied, i + 1)
                    act.nop().then_inc(free, 1)
                lin.ring.round_to(act, len(tiles))

            @block.vector
            def _(dve):
                own = Count(dve, own_sem)
                gf.on_dve(dve, own)
                an.on_dve(dve, own)
                dve.wait_ge(padded, 1)
                for i in range(DT):
                    slot, free = lin.arrived(dve, ("v", i))
                    dve.wait_ge(copied, i + 1)
                    own.link(dve.tensor_tensor(cv[:, i % 2, 2:], slot[:, 0, :], cbuf[:, i % 2, :], ALU.mult))
                    dve.nop().then_inc(free, 1)
                    w = [kit.gain("a_conv_2", k * DT + i) for k in range(3)]
                    own.link(dve.tensor_scalar(um[:, i % 2, :], cv[:, i % 2, 0:SEQ], w[0], None, ALU.mult))
                    for k in (1, 2):
                        own.link(dve.scalar_tensor_tensor(out=um[:, i % 2, :], in0=cv[:, i % 2, k:k + SEQ], scalar=w[k],
                                                          in1=um[:, i % 2, :], op0=ALU.mult, op1=ALU.add))
                    slot, free = lin.arrived(dve, ("b", i))
                    own.link(dve.tensor_tensor(um[:, i % 2, :], um[:, i % 2, :], slot[:, 0, :], ALU.mult))
                    dve.nop().then_inc(free, 1)
                    own.link(u.write_hi(dve, (slice(None), i), um[:, i % 2, :]))
                    u.write_lo(dve, (slice(None), i), um[:, i % 2, :]).then_inc(mixed, 1)
                for n in range(DT):
                    slot, free = lin.arrived(dve, ("o", n))
                    dve.tensor_tensor(kit.real(n), kit.real(n), slot[:, 0, :], ALU.add).then_inc(added, 1)
                    dve.wait_ge(added, n + 1)
                    dve.nop().then_inc(free, 1)


def ffn(kit, layer, final=None):
    nc, t = kit.nc, kit.t
    with Stage(kit, f"ffn{layer}") as st:
        ps = st.banks()
        hn = Split(st.sb("hn_hi", [P, DT, SEQ], F32R), st.sb("hn_lo", [P, DT, SEQ], F32R))
        silu = st.sb("silu", [P, 2, SEQ])
        prod = st.sb("prod", [P, 2, SEQ])
        mid = Split(st.sb("mid_hi", [P, FT, SEQ], F32R), st.sb("mid_lo", [P, FT, SEQ], F32R))
        gu = t["f_w_gu"][layer * 2 * FT * P:(layer + 1) * 2 * FT * P, :]
        down = t["f_w_down"][layer * DT * P:(layer + 1) * DT * P, :]
        half = FT // 2 * P
        halves = [w[:, i * half:(i + 1) * half] for w in pieces(down, DT, F) for i in range(2)]
        fn = Norm(st, "fn", kit.real, None, DT, SEQ, EPS2, lambda j: kit.gain("f_norm_2", layer * DT + j),
                  ps[:, 7:8, :], 1, split=(hn, lambda j: (slice(None), j)))
        silued, multiplied, mixed, added = st.sem("silued"), st.sem("multiplied"), st.sem("mixed"), st.sem("added")
        own_sem, stored = st.sem("vector_steps"), kit.stored
        last = None
        if final is not None:
            last = Norm(st, "last", kit.real, kit.real, DT, SEQ, EPS2,
                        lambda j: kit.gain("final_norm_2", j), ps[:, 7:8, :], 1, need=(added, lambda j: j + 1),
                        bufs=fn.bufs)
        tiles = []
        for i in range(FT):
            for part in "gu":
                tiles.append(tile((part, i), lambda k: [hn.pair(slice(None), k)], need=(fn.out, lambda k: k + 1)))
        for n in range(DT):
            for i in range(2):
                tiles.append(tile(("d", n), lambda k: [mid.pair(slice(None), k)],
                                  ks=range(i * FT // 2, (i + 1) * FT // 2), need=(mixed, lambda k: k + 1),
                                  start=(i == 0), stop=(i == 1)))
        lin = split_linear(st, one_bank_slots(ps, 0, 7), tiles, 3, half, pieces(gu, 2 * FT, D) + halves)
        with nc.Block() as block:

            @block.sync
            def _(sp):
                lin.ring.load_all(sp)
                if last is not None:
                    for j in range(DT):
                        sp.wait_ge(last.out, j + 1)
                        sp.dma_start(final[j * P:(j + 1) * P, :], kit.real(j)).then_inc(stored, 16)
                    sp.wait_ge(stored, 16 * DT)

            @block.gpsimd
            def _(pool):
                lin.ring.split_all(pool)

            @block.tensor
            def _(pe):
                fn.on_pe(pe)
                lin.run(pe)
                if last is not None:
                    last.on_pe(pe)

            @block.scalar
            def _(act):
                fn.on_act(act, lambda: lin.ring.round_to(act, 2))
                for i in range(FT):
                    slot, free = rounding(lin, act, ("g", i))
                    if i >= 2:
                        act.wait_ge(multiplied, i - 1)
                    act.activation(silu[:, i % 2, :], slot[:, 0, :], ACT.Silu).then_inc(silued, 1)
                    act.wait_ge(silued, i + 1)
                    act.nop().then_inc(free, 1)
                lin.ring.round_to(act, len(tiles))
                if last is not None:
                    last.on_act(act)

            @block.vector
            def _(dve):
                own = Count(dve, own_sem)
                fn.on_dve(dve, own)
                for i in range(FT):
                    slot, free = lin.arrived(dve, ("u", i))
                    dve.wait_ge(silued, i + 1)
                    if i >= 2:
                        dve.wait_ge(mixed, i - 1)
                    dve.tensor_tensor(prod[:, i % 2, :], slot[:, 0, :], silu[:, i % 2, :], ALU.mult)\
                       .then_inc(multiplied, 1)
                    dve.wait_ge(multiplied, i + 1)
                    dve.nop().then_inc(free, 1)
                    own.link(mid.write_hi(dve, (slice(None), i), prod[:, i % 2, :]))
                    mid.write_lo(dve, (slice(None), i), prod[:, i % 2, :]).then_inc(mixed, 1)
                for n in range(DT):
                    slot, free = lin.arrived(dve, ("d", n))
                    dve.tensor_tensor(kit.real(n), kit.real(n), slot[:, 0, :], ALU.add).then_inc(added, 1)
                    dve.wait_ge(added, n + 1)
                    dve.nop().then_inc(free, 1)
                if last is not None:
                    last.on_dve(dve, own)


def nsa_in(kit, io):
    nc, t = kit.nc, kit.t
    with Stage(kit, "nsain") as st:
        ps = st.banks()
        hn = Split(st.sb("hn_hi", [P, DT, SEQ], F32R), st.sb("hn_lo", [P, DT, SEQ], F32R))
        kn = Norm(st, "kn", kit.real, None, DT, SEQ, EPS2, lambda j: kit.gain("kv_norm_2", j),
                  ps[:, 7:8, :], 1, split=(hn, lambda j: (slice(None), j)))
        raw = st.sb("raw", [P, 2, NG, SEQ])
        X = st.sb("X", [P, 2, 2, NG, SEQ // DC, DC // 2])
        w1 = st.sb("w1", [P, LC // 2, CH])
        w2 = st.sb("w2", [P, 2, 2, HD])
        pe2 = st.sb("pe2", [P, 2, LC])
        hid = st.sb("hid", [P, 2, NG * NC])
        side = st.sem("side_loaded")
        w1_in = [st.sem("w1k_loaded"), st.sem("w1v_loaded")]
        b_out = st.sem("b_normed")
        x_made, hid_done, hid_silu, c_done, c_copied = (st.sem(n) for n in
                                                        ("x_made", "hid_done", "hid_silu", "c_done", "c_copied"))
        vcopied, gcopied = st.sem("v_copied"), st.sem("g_copied")

        def values(i):
            def by(pe, whi, wlo):
                if i == 0:
                    pe.wait_ge(kn.var, 1)
                for half in range(2):
                    k, c = 2 * i + half, slice(half * SEQ, (half + 1) * SEQ)
                    for j in range(ST):
                        x = hn.pair(slice(None), k, slice(j * P, (j + 1) * P))
                        mm = product(pe, ps[:, 4 + j, :], x, (whi[:, c], wlo[:, c]), k == 0, k == DT - 1)
                return mm
            return by

        def gates(pe, whi, wlo):
            pe.wait_ge(vcopied, 1)
            for j in range(ST):
                for k in range(DT):
                    c = slice(k * 3 * NH, (k + 1) * 3 * NH)
                    mm = product(pe, ps[:, 4, j * 3 * NH:(j + 1) * 3 * NH],
                                 hn.pair(slice(None), k, slice(j * P, (j + 1) * P)), (whi[:, c], wlo[:, c]),
                                 k == 0, k == DT - 1)
            return mm

        x = lambda k: [hn.pair(slice(None), k)]
        tiles = [tile(("k", n), x, need=(kn.out, lambda k: k + 1)) for n in range(8)]
        tiles += [tile(("v", i), by=values(i)) for i in range(DT // 2)]
        n_keys = len(tiles)
        tiles += [tile(("q", n), x, need=(b_out, lambda k: k + 1)) for n in range(DT)] + [tile("gates", by=gates)]
        lin = split_linear(st, one_bank_slots(ps, 0, 4), tiles, 3, D,
                           pieces(t["w_kraw"], 8, D) + [t["w_v2"][:, i * D:(i + 1) * D] for i in range(DT // 2)]
                           + pieces(t["w_q2"], DT, D) + [t["w_gate2"][:, :]])
        own_sem = st.sem("vector_steps")
        act_sem = st.sem("scalar_steps")
        with nc.Block() as block:

            @block.sync
            def _(sp):
                lin.ring.load_first(sp)
                sp.dma_start(w2[:, :, :, :], t["cmp_w2"].rearrange("p (a c n) -> p a c n", a=2, c=2)).then_inc(side, 16)
                sp.dma_start(pe2[:, :, :], t["cmp_pe"].rearrange("p (a l) -> p a l", a=2)).then_inc(side, 16)
                for h in range(NH):
                    sp.dma_start(io["qT"][HD:HD + 2, h, :], t["c_qrows"][2 * h:2 * h + 2, :]).then_inc(side, 16)
                for g in range(NG):
                    for b in range(2):
                        sp.dma_start(io["kT"][HD:HD + 2, b, g, :], t["c_krows"]).then_inc(side, 16)
                sp.dma_start(io["kc"][HD:HD + 2, :, :], t["c_crows"].rearrange("r (g n) -> r g n", g=NG)).then_inc(side, 16)
                sp.dma_start(io["tri"][:, :], t["c_tri2"]).then_inc(side, 16)
                sp.dma_start(io["vis"][:, :, :, :], t["c_vis"].rearrange("p (a j n) -> p a j n", a=2, j=ST)).then_inc(side, 16)
                sp.dma_start(w1[:, :, :], t["cmp_w1"][0:P, :].rearrange("p (m c) -> p m c", c=CH)).then_inc(w1_in[0], 16)
                lin.ring.load_all(sp)

            n_side = 16 * (3 + NH + 2 * NG + 2)

            @block.tensor
            def _(pe):
                kn.on_pe(pe)
                lin.run(pe, lambda n: n < n_keys)
                pe.wait_ge(side, n_side)
                pe.wait_ge(vcopied, ST)
                for kind in range(2):
                    pe.wait_ge(w1_in[kind], 16)
                    pe.wait_ge(x_made, kind + 1)
                    for c in range(2):
                        for m in range(LC // 2):
                            win, r = m // (DC // 2), m % (DC // 2)
                            mm = pe.matmul(ps[:, 5 + c, 0:NG * NC], w1[:, m, c * P:(c + 1) * P],
                                           X[:, kind, win, :, win:win + NC, r], start=(m == 0), stop=(m == LC // 2 - 1))
                    mm.then_inc(hid_done, 1)
                    pe.wait_ge(hid_silu, 2 * (kind + 1))
                    if kind == 0:
                        for c in range(2):
                            mm = pe.matmul(ps[0:HD, 7, 0:NG * NC], w2[:, 0, c, :], hid[:, c, :],
                                           start=(c == 0), stop=(c == 1))
                        mm.then_inc(c_done, 1)
                        pe.wait_ge(c_copied, 1)
                    else:
                        for g in range(NG):
                            for c in range(2):
                                mm = pe.matmul(ps[0:NC, 7, g * HD:(g + 1) * HD], hid[:, c, g * NC:(g + 1) * NC],
                                               w2[:, 1, c, :], start=(c == 0), stop=(c == 1))
                        mm.then_inc(c_done, 1)
                lin.run(pe, lambda n: n >= n_keys)

            @block.gpsimd
            def _(pool):
                lin.ring.split_all(pool)

            @block.scalar
            def _(act):
                own = Count(act, act_sem)
                kn.on_act(act, lambda: lin.ring.round_to(act, 2))
                for n in (4, 5, 6, 7):
                    slot, free = rounding(lin, act, ("k", n))
                    for e in range(2):
                        own.step(act.activation(io["kT"][0:HD, (n - 4) // 2, 2 * (n % 2) + e, :],
                                                slot[e * HD:(e + 1) * HD, 0, :], ACT.Copy))
                    own.wait()
                    act.nop().then_inc(free, 1)
                rounding(lin, act, ("v", DT // 2 - 1))
                for j in range(ST):
                    act.activation(io["v"][:, j, :], ps[:, 4 + j, :], ACT.Copy).then_inc(vcopied, 1)
                for kind in range(2):
                    act.wait_ge(hid_done, kind + 1)
                    if kind == 0:
                        act.dma_start(w1[:, :, :], t["cmp_w1"][P:2 * P, :].rearrange("p (m c) -> p m c", c=CH))\
                           .then_inc(w1_in[1], 16)
                    else:
                        act.wait_ge(c_done, 1)
                    for c in range(2):
                        act.activation(hid[:, c, :], ps[:, 5 + c, 0:NG * NC], ACT.Silu).then_inc(hid_silu, 1)
                    act.wait_ge(c_done, kind + 1)
                    if kind == 0:
                        act.activation(io["kc"][0:HD, :, :].rearrange("p g n -> p (g n)"), ps[0:HD, 7, 0:NG * NC],
                                       ACT.Copy).then_inc(c_copied, 1)
                own.link(act.activation(io["vc"][:, :], ps[0:NC, 7, 0:NG * HD], ACT.Copy))
                for n in range(DT):
                    slot, free = rounding(lin, act, ("q", n))
                    for e in range(2):
                        own.step(act.activation(io["qT"][0:HD, 2 * n + e, :], slot[e * HD:(e + 1) * HD, 0, :],
                                                ACT.Copy, scale=-HD ** -0.5))
                    own.wait()
                    act.nop().then_inc(free, 1)
                rounding(lin, act, "gates")
                own.link(act.activation(io["gate"][:, :, :].rearrange("p j n -> p (j n)"), ps[:, 4, 0:ST * 3 * NH],
                                        ACT.Sigmoid))

            @block.vector
            def _(dve):
                own = Count(dve, own_sem)
                kn.on_dve(dve, own)
                dve.wait_ge(side, n_side)
                for kind in range(2):
                    for n in range(2):
                        slot, free = lin.arrived(dve, ("k", 2 * kind + n))
                        for e in range(2):
                            g = 2 * n + e
                            own.step(dve.tensor_copy(raw[0:HD, kind, g, :], slot[e * HD:(e + 1) * HD, 0, :]))
                            own.step(dve.tensor_copy(raw[HD:P, kind, g, 0:SEQ - 1], slot[e * HD:(e + 1) * HD, 0, 1:SEQ]))
                        own.wait()
                        dve.nop().then_inc(free, 1)
                    for win in range(2):
                        for g in range(NG):
                            own.step(dve.tensor_tensor(
                                X[:, kind, win, g, :, :], raw[:, kind, g, :].rearrange("p (n r) -> p n r", r=DC)[:, :, 0:DC:2],
                                pe2[:, kind, win * DC:(win + 1) * DC:2].unsqueeze(1)
                                .to_broadcast([P, SEQ // DC, DC // 2]), ALU.add))
                    own.wait()
                    dve.nop().then_inc(x_made, 1)
                lin.arrived(dve, ("v", DT // 2 - 1))
                kn.scale(dve, own, kit.real, lambda j: kit.gain("b_norm_2", j), kn.split, b_out)


LAG = 2


def nsa(kit, io):
    nc = kit.nc
    with Stage(kit, "nsa") as st:
        ps = st.banks()
        def item(h, j, kind, start, stop):
            g = h // HPG
            x = dict(q=io["qT"][:, h, j * P:(j + 1) * P], lo=0, bank=h // 2, start=start, stop=stop, scale=-1.0,
                     out=lambda o: o[(h % 2) * HD:(h % 2 + 1) * HD, j * P:(j + 1) * P],
                     gate=io["gate"][:, j, 3 * h + kind:3 * h + kind + 1])
            if kind == 0:
                x.update(ks=[(io["kc"][:, g, :], 0)], hi=NC, mask=(0, io["vis"][:, 0, j, :]),
                         pts=[(0, NC, io["vc"][:, g * HD:(g + 1) * HD])])
            else:
                b, n = kind - 1, (j + 1) * P
                x.update(ks=[(io["kT"][:, b, g, 0:n], 0)], hi=n, mask=(j * P, io["tri"][:, :]),
                         pts=[(i * P, P, io["v"][:, i, (b * NG + g) * HD:(b * NG + g + 1) * HD])
                              for i in range(j + 1)])
            return x

        items = []
        for hp in range(NH // 2):
            for j in range(ST) if hp % 2 == 0 else reversed(range(ST)):
                kinds = (0, 1, 2) if j % 2 == 0 else (2, 1, 0)
                for kind in kinds:
                    for h in (2 * hp, 2 * hp + 1):
                        items.append(item(h, j, kind, kind == kinds[0], kind == kinds[-1]))
        at = Attention(st, items, [ps[:, i, :] for i in range(4)], [ps[:, 4 + i, :] for i in range(2)],
                       [ps[:, 6, :], ps[:, 7, :]], SEQ,
                       lambda dve, b, o: dve.tensor_copy(io["attnT"][:, b, :], o), lag=LAG,
                       negated=True)
        gates_cut = st.sem("gates_cut")
        with nc.Block() as block:

            @block.tensor
            def _(pe):
                at.on_pe(pe)

            @block.scalar
            def _(act):
                at.on_act(act)

            @block.vector
            def _(dve):
                for j in range(ST):
                    gates = io["gate"][:, j, 0:3 * NH:3]
                    dve.tensor_scalar(gates, gates, io["vis"][:, 1, j, 0:1], None, ALU.mult).then_inc(gates_cut, 1)
                dve.wait_ge(gates_cut, ST)
                at.on_dve(dve)


def nsa_out(kit, io):
    nc, t = kit.nc, kit.t
    with Stage(kit, "nsaout") as st:
        ps = st.banks()
        attn = Split(st.sb("attn_hi", [P, DT, SEQ], F32R), st.sb("attn_lo", [P, DT, SEQ], F32R))
        split = st.sem("attn_split")
        lin = split_linear(st, one_bank_slots(ps, 0, 6),
                           [tile(("o", n), lambda k: [attn.pair(slice(None), k)], need=(split, lambda k: k + 1))
                            for n in range(DT)], 4, D, pieces(t["b_w_o"], DT, D))
        added, own_sem = st.sem("added"), st.sem("vector_steps")
        with nc.Block() as block:

            @block.sync
            def _(sp):
                lin.ring.load_all(sp)

            @block.gpsimd
            def _(pool):
                lin.ring.split_all(pool)

            @block.scalar
            def _(act):
                lin.ring.round_to(act, DT)

            @block.tensor
            def _(pe):
                lin.run(pe)

            @block.vector
            def _(dve):
                own = Count(dve, own_sem)
                attn.write_all(dve, own, io["attnT"], DT, split)
                for n in range(DT):
                    slot, free = lin.arrived(dve, ("o", n))
                    dve.tensor_tensor(kit.real(n), kit.real(n), slot[:, 0, :], ALU.add).then_inc(added, 1)
                    dve.wait_ge(added, n + 1)
                    dve.nop().then_inc(free, 1)


def build_program(nc, t, out, dump=None, upto=99):
    with ExitStack() as ctx:
        kit = Kit(nc, t, ctx)

        def done(n):
            if dump is not None and upto == n:
                dump(kit)
                return True
            return False

        with ExitStack() as late:
            sb = lambda n, s, d=F32: late.enter_context(nc.sbuf_tensor(n, s, d))
            io = {"hn": Split(sb("xn_hi", [P, DT, T1], F32R), sb("xn_lo", [P, DT, T1], F32R)),
                  "idx": sb("idx", [P, 2, SEQ], F16), "gate": sb("gate", [P, 2, SEQ], F16)}
            io["xn"] = Split(io["hn"].hi[:, :, 0:SEQ], io["hn"].lo[:, :, 0:SEQ])
            with ExitStack() as first:
                sb1 = lambda n, s, d=F32: first.enter_context(nc.sbuf_tensor(n, s, d))
                io["mixT"] = sb1("mixT", [P, 2 * CT, SEQ])
                with ExitStack() as qkv:
                    sb2 = lambda n, s, d=F32: qkv.enter_context(nc.sbuf_tensor(n, s, d))
                    io["conv_in"] = sb2("conv_in", [P, CT, CK - 1 + T1])
                    io["conv"] = Conv(kit, io["conv_in"], io["mixT"][:, CT:2 * CT, :])
                    io.update(qT=sb2("qT", [DQ, HEADS, SEQ]), kT=sb2("kT", [DQ, HEADS, T1]), v=sb2("v", [P, ST + 1, CC]))
                    front(kit, io)
                    kit.io = io
                    if done(1):
                        return
                    mla(kit, io)
                    if done(2):
                        return
                route(kit, io)
            if done(3):
                return
            experts(kit, io)
        if done(4):
            return
        short(kit)
        if done(5):
            return
        ffn(kit, 0)
        if done(6):
            return
        with ExitStack() as qkv:
            sb = lambda n, s, d=F32: qkv.enter_context(nc.sbuf_tensor(n, s, d))
            io = {"qT": sb("q2T", [HD + 2, NH, SEQ]), "kT": sb("k2T", [HD + 2, 2, NG, SEQ]),
                  "v": sb("v2", [P, ST, 2 * NG * HD]), "gate": sb("gate2", [P, ST, 3 * NH]),
                  "kc": sb("kc", [HD + 2, NG, NC]), "vc": sb("vc", [NC, NG * HD]), "vis": sb("vis", [P, 2, ST, NC]), "tri": sb("tri2", [P, P])}
            nsa_in(kit, io)
            kit.io = io
            if done(7):
                return
            io["attnT"] = sb("attn2T", [P, DT, SEQ])
            nsa(kit, io)
            if done(8):
                return
            nsa_out(kit, io)
        if done(9):
            return
        ffn(kit, 1, final=out)


def constants():
    f = np.float32
    pos = np.arange(T1, dtype=f)
    freq = (f(10000.0) ** (-np.arange(ROPE // 2, dtype=f) / f(ROPE // 2))).astype(f)
    ang = (freq[:, None] * pos[None, :]).astype(f)
    cos, sin = np.cos(ang).astype(f), np.sin(ang).astype(f)
    slopes = np.exp2(-8.0 * np.arange(1, NH + 1) / NH).astype(f)
    tok = np.arange(SEQ, dtype=f)
    qrows = -np.stack([np.stack([np.full(SEQ, s, f), -s * tok]) for s in slopes]).reshape(2 * NH, SEQ)
    centre = np.arange(NC, dtype=f) * DC + (LC - 1) / 2.0
    end = np.arange(NC) * DC + LC - 1
    see = (end[None, :] <= np.arange(SEQ)[:, None])
    vis = np.stack([np.where(see, 0.0, -NEG), see.astype(f)]).astype(f).reshape(2, ST, P, NC).transpose(2, 0, 1, 3)
    return {
        "c_cos": np.tile(np.concatenate([cos, cos]), (4, 1)),
        "c_sin": np.tile(np.concatenate([-sin, sin]), (4, 1)),
        "c_ident": np.eye(P, dtype=f),
        "c_tri": np.where(np.arange(P)[None, :] <= np.arange(P)[:, None], 0.0, NEG).astype(f),
        "c_tri2": np.where(np.arange(P)[None, :] <= np.arange(P)[:, None], 0.0, -NEG).astype(f),
        "c_places": np.tile(np.repeat(np.arange(TOPK), TOPK * PH).astype(np.float16), (P, 1)),
        "c_iota16": np.tile(np.repeat(np.arange(NK), TB).astype(np.float16), (P, 1)),
        "c_qrows": qrows.astype(f),
        "c_krows": np.stack([tok, np.ones(SEQ, f)]),
        "c_crows": np.tile(np.stack([centre, np.ones(NC)]).astype(f), (1, NG)),
        "c_vis": vis.reshape(P, 2 * ST * NC),
    }


def tiles_of(w, m=P):
    k, n = w.shape
    return w.reshape(k // P, P, n // m, m).transpose(2, 1, 0, 3).reshape(n // m * P, k // P * m)


def lay_out(i):
    ht = np.concatenate([i["meta"], i["x"][0]], axis=0).T
    a = {"hT0": ht.reshape(DT, P, T1).transpose(1, 0, 2).reshape(P, DT * T1)}
    a["gains"] = np.concatenate([i[n].reshape(-1, P) for n, _ in GAINS], axis=0).T
    w = i["w_in"][0]
    ab = np.concatenate([np.concatenate([w[:, CC + c * P:CC + (c + 1) * P], w[:, c * P:(c + 1) * P]], axis=1)
                         for c in range(CT)], axis=1)
    c0 = 2 * CC
    a["w_ab"] = tiles_of(ab)
    a["w_cq"] = tiles_of(w[:, c0:c0 + QL])
    a["w_ckv"] = tiles_of(w[:, c0 + QL:c0 + QL + KVL])
    kr = w[:, c0 + QL + KVL:]
    a["w_krope"] = tiles_of(np.concatenate([kr, kr[:, ROPE // 2:], kr[:, :ROPE // 2]] * 2, axis=1))
    uq = i["w_uq"][0].reshape(QL, HEADS, DQ)
    nope, rope = uq[:, :, :NOPE], uq[:, :, NOPE:]
    swap = np.concatenate([rope[:, :, ROPE // 2:], rope[:, :, :ROPE // 2]], axis=2)
    rope, swap = rope.reshape(QL, 2, P), swap.reshape(QL, 2, P)
    both = np.stack([rope, swap], axis=2).reshape(QL, 4 * P)
    a["w_uq"] = tiles_of(np.concatenate([nope.reshape(QL, HEADS * NOPE), both], axis=1))
    ukv = i["w_ukv"][0].reshape(KVL, HEADS, NOPE + VH)
    a["w_ukv"] = np.concatenate([ukv[:, :, :NOPE].reshape(KVL, -1), ukv[:, :, NOPE:].reshape(KVL, -1)], axis=1)
    a["w_out"] = tiles_of(i["w_out"][0])
    a["peer_wq"] = tiles_of(i["peer_wq"][0])
    a["peer_keys"] = i["peer_keys"][0].transpose(1, 3, 0, 2).reshape(P, PH * NK)
    a["peer_uT"] = i["peer_u"][0].reshape(CHUNKS, P, DT, P).transpose(0, 3, 2, 1).reshape(CHUNKS * P, D)
    a["peer_v"] = i["peer_v"][0]
    wi = i["a_w_in_2"][0]
    order = [wi[:, p * D + n * P:p * D + (n + 1) * P] for n in range(DT) for p in (1, 2, 0)]
    a["a_w_in"] = tiles_of(np.concatenate(order, axis=1))
    a["a_w_out"] = tiles_of(i["a_w_out_2"][0])
    gu = i["f_w_gu_2"]
    order = [gu[:, :, p * F + n * P:p * F + (n + 1) * P] for n in range(FT) for p in range(2)]
    gu = np.concatenate(order, axis=2)
    a["f_w_gu"] = np.concatenate([tiles_of(gu[0]), tiles_of(gu[1])], axis=0)
    a["f_w_down"] = np.concatenate([tiles_of(i["f_w_down_2"][0]), tiles_of(i["f_w_down_2"][1])], axis=0)
    kv = i["w_kv_2"].reshape(D, 6, NG * HD)
    a["w_kraw"] = tiles_of(np.concatenate([kv[:, s] for s in (0, 1, 2, 4)], axis=1))
    a["w_v2"] = np.concatenate([kv[:, 3], kv[:, 5]], axis=1).reshape(DT, P, -1).transpose(1, 0, 2).reshape(P, -1)
    qg = i["b_w_qg_2"][0]
    a["w_q2"] = tiles_of(qg[:, :NH * HD])
    a["w_gate2"] = qg[:, NH * HD:].reshape(DT, P, -1).transpose(1, 0, 2).reshape(P, -1)
    a["b_w_o"] = tiles_of(i["b_w_o_2"][0])
    w1 = np.stack([i["cmp_w1_k_2"], i["cmp_w1_v_2"]]).reshape(2, LC // 2, P, CH)
    a["cmp_w1"] = w1.transpose(0, 2, 1, 3).reshape(2 * P, LC // 2 * CH)
    w2 = np.stack([i["cmp_w2_k_2"], i["cmp_w2_v_2"]]).reshape(2, 2, P, HD)
    a["cmp_w2"] = w2.transpose(2, 0, 1, 3).reshape(P, 4 * HD)
    pe = np.stack([i["cmp_pe_k_2"], i["cmp_pe_v_2"]]).transpose(2, 0, 1)
    a["cmp_pe"] = np.concatenate([pe, np.roll(pe, -1, axis=2)], axis=0).reshape(P, 2 * LC)
    return a


def kernel(**inputs):
    import concourse.bacc as bacc
    from concourse.bass_utils import run_bass_kernel_spmd

    nc = bacc.Bacc("TRN2", target_bir_lowering=False, num_devices=1)
    laid = lay_out({k: np.asarray(v) for k, v in inputs.items()})
    laid.update(constants())
    arrays, aps = {}, {}
    for name, a in laid.items():
        a = np.ascontiguousarray(a)
        arrays[f"in_{name}"] = a
        aps[name] = nc.dram_tensor(f"in_{name}", a.shape, mybir.dt.from_np(a.dtype), kind="ExternalInput").ap()
    out = nc.dram_tensor("out_T", (D, SEQ), F32, kind="ExternalOutput").ap()
    build_program(nc, aps, out)
    r = run_bass_kernel_spmd(nc, [arrays], core_ids=[0])
    return np.ascontiguousarray(r.results[0]["out_T"].T)[None]
```
